# Optimizing a Trainium2 kernel written in Bass

```python
import jax, jax.numpy as jnp
from jax import lax
import numpy as np

D_MODEL = 1024
BATCH = 1
SEQ = 512
DEPTH = 1
DEC_BATCH = 8
DEC_SEQ = 4
PAST_LEN = 4096
PAGE_SIZE = 128

D_MIX = D_MODEL
D_POOL = D_MIX // 2
D_CONV = D_MIX - D_POOL
POOL_WINDOWS = (2, 4, 8, 16)
N_POOL_GROUPS = len(POOL_WINDOWS)
POOL_GROUP = D_POOL // N_POOL_GROUPS
POOL_STATE = max(POOL_WINDOWS) - 1
N_CONV_HEADS = 8
CONV_W = 3
CONV_STATE = CONV_W - 1
D_IN = D_POOL + 3 * D_CONV
N_EXPERTS = 32
TOP_K = 4
D_FF = D_MODEL
SWIGLU_LIMIT = 7.0
SWIGLU_ALPHA = 1.702
MOE_BLOCK = 128
EPS = 1e-5

kernel_name = "hybrid_pool_shortconv_moe_adaln_step"

def rmsnorm(x, g):
    xf = x.astype(jnp.float32)
    y = xf * lax.rsqrt(jnp.mean(xf * xf, axis=-1, keepdims=True) + EPS)
    return (y * g.astype(jnp.float32)).astype(x.dtype)

def pool_mixer(u, prefix, pos0, w_pool, pool_scale):
    b, t, _ = u.shape
    ext_raw = jnp.concatenate([prefix, u], axis=1)
    ext = ext_raw.astype(jnp.float32)
    cs = jnp.concatenate([jnp.zeros((b, 1, D_POOL), jnp.float32),
                          jnp.cumsum(ext, axis=1)], axis=1)
    pos = pos0 + jnp.arange(t)
    end = cs[:, POOL_STATE + 1:]
    means = []
    for g, w in enumerate(POOL_WINDOWS):
        sl = slice(g * POOL_GROUP, (g + 1) * POOL_GROUP)
        start = cs[:, POOL_STATE + 1 - w: POOL_STATE + 1 - w + t, sl]
        cnt = jnp.minimum(pos + 1, w).astype(jnp.float32)[None, :, None]
        means.append((end[..., sl] - start) / cnt)
    pooled = jnp.concatenate(means, axis=-1) - ext[:, POOL_STATE:]
    pooled = pooled.astype(u.dtype).reshape(b, t, N_POOL_GROUPS, POOL_GROUP)
    mixed = jnp.einsum("btgc,gcd->btgd", pooled, w_pool).reshape(b, t, D_POOL)
    return mixed * pool_scale, ext_raw[:, -POOL_STATE:]

def conv_mixer(gate_b, gate_c, val, prefix, w_conv):
    t = val.shape[1]
    v = gate_c * val
    ext = jnp.concatenate([prefix, v], axis=1)
    y = w_conv[0] * ext[:, 0:t] + w_conv[1] * ext[:, 1:t + 1] + w_conv[2] * ext[:, 2:t + 2]
    return gate_b * y, ext[:, -CONV_STATE:]

def moe(h, w_router, b_router, w_gate, b_gate, w_up, b_up, w_down, b_down):
    n = h.shape[0]
    logits = h.astype(jnp.float32) @ w_router.astype(jnp.float32) + b_router.astype(jnp.float32)
    top_v, top_i = lax.top_k(logits, TOP_K)
    gates = jax.nn.softmax(top_v, axis=-1).astype(h.dtype)
    nk = n * TOP_K
    e_flat = top_i.reshape(-1)
    tok_flat = jnp.repeat(jnp.arange(n), TOP_K)
    g_flat = gates.reshape(-1)
    order = jnp.argsort(e_flat, stable=True)
    e_s, tok_s, g_s = e_flat[order], tok_flat[order], g_flat[order]
    counts = jnp.zeros((N_EXPERTS,), jnp.int32).at[e_flat].add(1)
    padded = (counts + MOE_BLOCK - 1) // MOE_BLOCK * MOE_BLOCK
    start = jnp.cumsum(counts) - counts
    pad_end = jnp.cumsum(padded)
    pad_start = pad_end - padded
    dest = pad_start[e_s] + (jnp.arange(nk) - start[e_s])
    n_blocks = -(-nk // MOE_BLOCK) + N_EXPERTS
    rows = jnp.zeros((n_blocks * MOE_BLOCK, h.shape[1]), h.dtype).at[dest].set(h[tok_s])
    block_start = jnp.arange(n_blocks) * MOE_BLOCK
    block_expert = jnp.minimum(jnp.sum(block_start[:, None] >= pad_end[None, :], axis=1),
                               N_EXPERTS - 1).astype(jnp.int32)

    def expert_block(args):
        xb, e = args
        g = xb @ w_gate[e] + b_gate[e]
        u = xb @ w_up[e] + b_up[e]
        g = jnp.minimum(g, SWIGLU_LIMIT)
        u = jnp.clip(u, -SWIGLU_LIMIT, SWIGLU_LIMIT)
        glu = g * jax.nn.sigmoid(SWIGLU_ALPHA * g)
        return ((u + 1.0) * glu) @ w_down[e] + b_down[e]

    y_rows = lax.map(expert_block, (rows.reshape(n_blocks, MOE_BLOCK, -1), block_expert))
    y_rows = y_rows.reshape(n_blocks * MOE_BLOCK, -1)
    contrib = y_rows[dest] * g_s[:, None]
    return jnp.zeros_like(h).at[tok_s].add(contrib)

def layer(x, c, pool_prefix, conv_prefix, pos0, norm1, norm2, w_ada, b_ada, w_in, w_pool,
          pool_scale, w_conv, w_out, w_router, b_router, w_gate, b_gate, w_up, b_up,
          w_down, b_down):
    b, t, d = x.shape
    mod = jax.nn.silu(c) @ w_ada + b_ada
    sh1, sc1, g1, sh2, sc2, g2 = jnp.split(mod[:, None, :], 6, axis=-1)
    h = rmsnorm(x, norm1) * (1.0 + sc1) + sh1
    z = h @ w_in
    u, gate_b, gate_c, val = jnp.split(z, [D_POOL, D_POOL + D_CONV, D_POOL + 2 * D_CONV], axis=-1)
    pool_out, pool_state = pool_mixer(u, pool_prefix, pos0, w_pool, pool_scale)
    conv_out, conv_state = conv_mixer(gate_b, gate_c, val, conv_prefix, w_conv)
    mix = jnp.concatenate([pool_out, conv_out], axis=-1) @ w_out
    x = x + g1 * mix
    h2 = rmsnorm(x, norm2) * (1.0 + sc2) + sh2
    ffn = moe(h2.reshape(b * t, d), w_router, b_router, w_gate, b_gate, w_up, b_up,
              w_down, b_down).reshape(b, t, d)
    x = x + g2 * ffn
    return x, pool_state, conv_state

def setup_inputs(seed: int = 0) -> dict:
    key = jax.random.key(seed)
    ks = jax.random.split(key, 26)
    f32 = jnp.float32
    nrm = lambda k, shape, s: (jax.random.normal(k, shape, f32) * s)
    L = DEPTH
    return {
        "x_prompt": nrm(ks[0], (BATCH, SEQ, D_MODEL), 1.0),
        "x_sample": nrm(ks[1], (DEC_BATCH, DEC_SEQ, D_MODEL), 1.0),
        "state_pool": nrm(ks[2], (L, DEC_BATCH, POOL_STATE, D_POOL), 1.0),
        "state_conv": nrm(ks[3], (L, DEC_BATCH, CONV_STATE, D_CONV), 1.0),
        "c_prompt": nrm(ks[4], (BATCH, D_MODEL), 1.0),
        "c_sample": nrm(ks[5], (DEC_BATCH, D_MODEL), 1.0),
        "norm1": 1.0 + nrm(ks[6], (L, D_MODEL), 0.02),
        "norm2": 1.0 + nrm(ks[7], (L, D_MODEL), 0.02),
        "w_ada": nrm(ks[8], (L, D_MODEL, 6 * D_MODEL), 0.5 * D_MODEL ** -0.5),
        "b_ada": nrm(ks[9], (L, 6 * D_MODEL), 0.02),
        "w_in": nrm(ks[10], (L, D_MODEL, D_IN), D_MODEL ** -0.5),
        "w_pool": nrm(ks[11], (L, N_POOL_GROUPS, POOL_GROUP, POOL_GROUP), POOL_GROUP ** -0.5),
        "pool_scale": 1.0 + nrm(ks[12], (L, D_POOL), 0.1),
        "w_conv": nrm(ks[13], (L, CONV_W, D_CONV), CONV_W ** -0.5),
        "w_out": nrm(ks[14], (L, D_MIX, D_MODEL), D_MIX ** -0.5),
        "w_router": nrm(ks[15], (L, D_MODEL, N_EXPERTS), D_MODEL ** -0.5),
        "b_router": nrm(ks[16], (L, N_EXPERTS), 0.01),
        "w_gate": nrm(ks[17], (L, N_EXPERTS, D_MODEL, D_FF), D_MODEL ** -0.5),
        "b_gate": nrm(ks[18], (L, N_EXPERTS, D_FF), 0.02),
        "w_up": nrm(ks[19], (L, N_EXPERTS, D_MODEL, D_FF), D_MODEL ** -0.5),
        "b_up": nrm(ks[20], (L, N_EXPERTS, D_FF), 0.02),
        "w_down": nrm(ks[21], (L, N_EXPERTS, D_FF, D_MODEL), D_FF ** -0.5),
        "b_down": nrm(ks[22], (L, N_EXPERTS, D_MODEL), 0.02),
        "final_norm": 1.0 + nrm(ks[23], (D_MODEL,), 0.02),
    }

def reference(x_prompt, x_sample, state_pool, state_conv, c_prompt, c_sample, norm1, norm2,
              w_ada, b_ada, w_in, w_pool, pool_scale, w_conv, w_out, w_router, b_router,
              w_gate, b_gate, w_up, b_up, w_down, b_down, final_norm):
    yp, ys = x_prompt, x_sample
    pool_p, conv_p, pool_s, conv_s = [], [], [], []
    zero_pool = jnp.zeros((x_prompt.shape[0], POOL_STATE, D_POOL), x_prompt.dtype)
    zero_conv = jnp.zeros((x_prompt.shape[0], CONV_STATE, D_CONV), x_prompt.dtype)
    for l in range(DEPTH):
        params = (norm1[l], norm2[l], w_ada[l], b_ada[l], w_in[l], w_pool[l], pool_scale[l],
                  w_conv[l], w_out[l], w_router[l], b_router[l], w_gate[l], b_gate[l],
                  w_up[l], b_up[l], w_down[l], b_down[l])
        yp, sp, scp = layer(yp, c_prompt, zero_pool, zero_conv, 0, *params)
        ys, ss, scs = layer(ys, c_sample, state_pool[l], state_conv[l], PAST_LEN, *params)
        pool_p.append(sp)
        conv_p.append(scp)
        pool_s.append(ss)
        conv_s.append(scs)
    y_prompt = rmsnorm(yp, final_norm)
    y_sample = rmsnorm(ys, final_norm)
    return (y_prompt, y_sample, jnp.stack(pool_p), jnp.stack(conv_p), jnp.stack(pool_s), jnp.stack(conv_s))


_drawn_inputs = setup_inputs


def setup_inputs(seed=0):
    import zlib

    import numpy as np

    out = dict(_drawn_inputs(seed))
    spreads = {}
    factors = {'norm2': 3.49,
     'b_router': 5.018,
     'b_gate': 8.0,
     'b_up': 8.0,
     'b_down': 28.159,
     'final_norm': 8.446}
    for name, (base, spread) in spreads.items():
        noise = np.random.default_rng([zlib.crc32(name.encode()), seed]).standard_normal(out[name].shape)
        drawn = base * np.exp(spread * noise) if base else spread * noise
        out[name] = __import__('jax').numpy.asarray(drawn.astype(out[name].dtype))
    for name, factor in factors.items():
        out[name] = (out[name] * factor).astype(out[name].dtype)
    return out
```

```python
from contextlib import ExitStack

import concourse.bass as bass
from concourse import mybir

ALU = mybir.AluOpType
ACT = mybir.ActivationFunctionType
AX = mybir.AxisListType
F32 = mybir.dt.float32
F32R = mybir.dt.float32r
BF16 = mybir.dt.bfloat16
I32 = mybir.dt.int32
U32 = mybir.dt.uint32

P = 128
D = 1024
KT = D // P
SEQ = 512
DEC_B, DEC_T = 8, 4
NS = DEC_B * DEC_T
PT = SEQ // P
TT = PT + 1
NTOK = SEQ + NS
NC = 1 + DEC_B
DP = 512
GR = DP // P
WINDOWS = (2, 4, 8, 16)
PAST = 15
CPAST = 2
E = 32
TOPK = 4
LIMIT = 7.0
ALPHA = 1.702
EPS = 1e-5
HALF = 512
CW = 256
ADA_CH = 6 * D // CW
IN_CH = 4 * DP // CW
OUT_CH = D // CW
DENSE_CH = ADA_CH + IN_CH + OUT_CH
SLOTS = 6
KC = 2
MCH = KT // KC
SPLIT = 3
SLOT_F = KC * D
MAX_OV = TOPK * NTOK // P - 1
MAIN_ROWS = E * P
EXTRA = -(-NTOK // P) - 1
ZW = 256
NSLOT_ROWS = MAIN_ROWS + MAX_OV * P


def hybrid_step(nc, x_prompt, x_sample, state_pool, state_conv, c_prompt, c_sample, norm1, norm2,
                w_ada, b_ada, w_in, w_pool, pool_scale, w_conv, w_out, w_router, b_router,
                w_gate, b_gate, w_up, b_up, w_down, b_down, final_norm,
                y_prompt, y_sample, new_pool_prompt, new_conv_prompt, new_pool_sample, new_conv_sample):
    h2_dram = nc.dram_tensor("h2_rows", (NTOK, D), F32).ap()
    y_dram = nc.dram_tensor("expert_rows", (NSLOT_ROWS, D), F32).ap()

    top = ExitStack()
    with top:
        def sem(name):
            return top.enter_context(nc.semaphore(name))

        def keep(name, shape, dt=F32):
            return top.enter_context(nc.sbuf_tensor(name, shape, dt))

        psum = [top.enter_context(nc.psum_tensor(f"acc{i}", [P, 2, HALF], F32)) for i in range(4)]
        acc_g, acc_u, acc_y, tp = psum

        raw = [keep(f"raw{s}", [P, SLOT_F]) for s in range(SLOTS)]
        x_sb = keep("x_sb", [P, TT, D])
        g2_rows = keep("g2_rows", [NC, D])
        bias_t = [keep(f"bias_{m}", [2 * E, D], F32R) for m in ("gate", "up", "down")]
        ident = keep("ident", [P, P])
        iota_m = keep("iota_m", [P, P])
        rank_m = keep("rank_m", [P, TT, E + 1])
        slot_f = keep("slot_f", [P, TT, TOPK])
        slot_rel = keep("slot_rel", [P, TT, TOPK])
        slot_i = keep("slot_i", [P, TT, TOPK], U32)
        gates = keep("gates", [P, TT, TOPK])
        tok_bf = keep("tok_bf", [P, TT, 2], BF16)
        expert_id2 = keep("expert_id2", [2 * E, E + 1])
        pmod = keep("pmod", [2 * E, 1])
        n_ov_i = keep("n_ov_i", [P, 1], I32)
        ov_expert = keep("ov_expert", [P, MAX_OV])
        ov_expert_i = keep("ov_expert_i", [P, MAX_OV], I32)
        sel_p = keep("sel_p", [NC, P])
        sel_s = keep("sel_s", [NC, NS])
        ss = keep("ss", [P, TT])
        rstd = keep("rstd", [P, TT])
        eps_c = keep("eps_c", [P, 1])

        raw_loaded = [sem(f"raw_loaded{s}") for s in range(SLOTS)]

        part = ExitStack()

        def sb(name, shape, dt=F32):
            return part.enter_context(nc.sbuf_tensor(name, shape, dt))

        c_sg = sb("c_sg", [P, KT, NC])
        c_act = sb("c_act", [P, KT, NC])
        mod = sb("mod", [NC, 6 * D])
        n2_rows = sb("n2_rows", [NC, D])
        junk = sb("junk", [P, D])
        h_row = [sb(f"h_row{i}", [P, D]) for i in range(2)]
        h_t = sb("h_t", [P, KT, NTOK])
        uext = sb("uext", [P, GR, PAST + SEQ])
        uext_s = sb("uext_s", [P, GR, DEC_B, PAST + DEC_T])
        vext = sb("vext", [P, GR, CPAST + SEQ])
        vext_s = sb("vext_s", [P, GR, DEC_B, CPAST + DEC_T])
        gate_b = sb("gate_b", [P, GR, NTOK])
        gate_c = sb("gate_c", [P, GR, NTOK])
        mix_t = h_t
        pooled = gate_c
        wsum = [sb(f"wsum{i}", [P, PAST + SEQ]) for i in range(2)]
        g1_bc = sb("g1_bc", [P, D])
        c_rows = g1_bc[0:NC, :]
        g1_bc_s = sb("g1_bc_s", [NS, D])
        n1_rows = g1_bc_s[0:NC, :]
        par = sb("par", [P, 5 * GR])
        par_rows = sb("par_rows", [5 * GR, P])
        wpool_sb = sb("wpool_sb", [P, GR, P])
        wr_sb = sb("wr_sb", [P, KT, E])
        br_bc = sb("br_bc", [P, E])
        inv_n = sb("inv_n", [P, 16])
        sp_rows = sb("sp_rows", [DEC_B * PAST, DP])
        sc_rows = sb("sc_rows", [DEC_B * CPAST, DP])
        u_new = gate_b[:, :, SEQ:NTOK]
        v_new = gate_c[:, :, SEQ:SEQ + DEC_B * CPAST]
        state_o = [gate_b[0:n, i, 0:DP] for i, n in enumerate((PAST, CPAST, NS, DEC_B * CPAST))]
        b_raw = [junk[0:2 * E, :], h_row[0][0:2 * E, :], h_row[1][0:2 * E, :]]
        logit = sb("logit", [P, TT, E])
        top_v = sb("top_v", [P, TT, 8])
        top_i = sb("top_i", [P, TT, 8], U32)
        top_f = sb("top_f", [P, TT, 8])
        neg_m = sb("neg_m", [P, TT])
        e_sum = sb("e_sum", [P, TT])
        spare = gate_c[:, :, :].rearrange("p g n -> p (g n)")
        onehot = spare[:, 0:TT * TOPK * E].rearrange("p (t k e) -> p t k e", t=TT, k=TOPK)
        ov_cmp = spare[:, TT * TOPK * E:TT * TOPK * E + MAX_OV * E].rearrange("p (j e) -> p j e", e=E)
        pick = spare[:, TT * TOPK * E + MAX_OV * E:TT * TOPK * E + (MAX_OV + TOPK) * E]\
            .rearrange("p (k e) -> p k e", e=E)
        mask = sb("mask", [P, TT, E])
        mask_bf = sb("mask_bf", [P, TT, E], BF16)
        iota_e = sb("iota_e", [P, E])
        zeros = sb("zeros", [P, ZW])
        tri = sb("tri", [P, P], BF16)
        ones_bf = sb("ones_bf", [P, P], BF16)
        small = [sb(f"small{i}", [P, E]) for i in range(7)]
        over = sb("over", [P, E])
        slot_e = sb("slot_e", [P, E])
        iota_j = sb("iota_j", [P, MAX_OV])

        zp = [acc_g[:, 0, :], acc_g[:, 1, :], acc_u[:, 0, :], acc_u[:, 1, :]]
        modp = [acc_y[:, b, 0:CW] for b in range(2)]
        zs = acc_y[:, 1, :].rearrange("p (f n) -> p f n", n=NS)
        lg = acc_y[:, 1, :]
        c_ps = tp[:, 1, 0:KT * NC].rearrange("p (k r) -> p k r", r=NC)

        c_loaded = sem("c_loaded")
        x_loaded = sem("x_loaded")
        rows_loaded = sem("rows_loaded")
        small_loaded = sem("small_loaded")
        bias_loaded = sem("bias_loaded")
        consts = sem("consts")
        pool_step = sem("pool_step")
        dve_step = sem("dve_step")
        act_step = sem("act_step")
        c_tp = sem("c_tp")
        c_ready = sem("c_ready")
        sig_ready = sem("sig_ready")
        ada_done = sem("ada_done")
        ada_added = sem("ada_added")
        scale_ready = sem("scale_ready")
        spread_done = {k: sem(f"spread_{k}") for k in ("n1", "n1_s", "g1", "g1_s", "n2", "n2_s")}
        g1_ready = sem("g1_ready")
        sq_done = sem("sq_done")
        rstd_ready = sem("rstd_ready")
        h_ready = sem("h_ready")
        h_tp = sem("h_tp")
        ht_ready = sem("ht_ready")
        par_tp = sem("par_tp")
        par_ready = sem("par_ready")
        st_tp = sem("st_tp")
        st_ready = sem("st_ready")
        z_done = sem("z_done")
        z_evac_a = sem("z_evac_a")
        v_ready = sem("v_ready")
        pooled_ready = sem("pooled_ready")
        pm_done = sem("pm_done")
        pm_ready = sem("pm_ready")
        conv_ready = sem("conv_ready")
        mix_done = sem("mix_done")
        x1_ready = sem("x1_ready")
        so_tp = sem("so_tp")
        new_packed = sem("new_packed")
        so_ready = sem("so_ready")
        state_stored = sem("state_stored")
        h2_stored = [sem(f"h2_stored{b}") for b in range(2)]
        lg_done = sem("lg_done")
        exp_done = sem("exp_done")
        top_ready = sem("top_ready")
        mask_ready = sem("mask_ready")
        rank_done = sem("rank_done")
        bias_hi = sem("bias_hi")
        bias_ready = sem("bias_ready")
        rows_zeroed = sem("rows_zeroed")

        ADA_FIRST, ADA_MID = 2 * D // CW, 3 * D // CW
        order = [("ada", k) for k in range(ADA_FIRST + ADA_MID)]
        order += [("in", k) for k in range(IN_CH)]
        order += [("out", k) for k in range(OUT_CH)]
        order += [("ada", k) for k in range(ADA_FIRST + ADA_MID, ADA_CH)]
        src = {"ada": w_ada[0], "in": w_in[0], "out": w_out[0]}
        at = {key: n for n, key in enumerate(order)}
        assert len(order) == DENSE_CH and DENSE_CH % SLOTS == 0

        def used(n):
            kind, k = order[n]
            return {"ada": (ada_done, k + 1), "in": (z_done, 2 * (k + 1)), "out": (mix_done, TT * (k + 1))}[kind]

        def chunk_view(n):
            return raw[n % SLOTS][:, :].rearrange("p (k n) -> p k n", k=KT)

        def expert_src(kind, e, c):
            w = {"g": w_gate, "u": w_up, "d": w_down}[kind]
            rows = w[0].rearrange("e (c k p) n -> e c p k n", k=KC, p=P)
            return rows[e, c] if isinstance(e, int) else rows[bass.ds(e, 1), c].rearrange("a p k n -> (a p) k n")

        FIRST_STREAM = [("g", 0, c) for c in range(MCH)] + [("u", 0, c) for c in range(MCH)]

        POOL_STEPS = 19
        CONSTS = 2 + 16 + 5

        def norm_rows(t):
            return P if t < PT else NS

        block = part.enter_context(nc.Block())

        @block.sync
        def _(sp):
            sp.dma_start(c_rows[0:1, :], c_prompt).then_inc(c_loaded, 16)
            sp.dma_start(c_rows[1:NC, :], c_sample).then_inc(c_loaded, 16)
            for n, (kind, k) in enumerate(order):
                if n >= SLOTS:
                    sp.wait_ge(*used(n - SLOTS))
                sp.dma_start(chunk_view(n), src[kind][:, k * CW:(k + 1) * CW].rearrange("(k p) n -> p k n", p=P))\
                    .then_inc(raw_loaded[n % SLOTS], 16)
            for t in range(TT):
                sp.wait_ge(h_ready, TT + t + 1)
                sp.dma_start(h2_dram[t * P:t * P + norm_rows(t), :], h_row[t % 2][0:norm_rows(t), :])\
                    .then_inc(h2_stored[t % 2], 16)
            for n, (kind, e, c) in enumerate(FIRST_STREAM[:SLOTS]):
                sp.wait_ge(*used(DENSE_CH - SLOTS + n))
                sp.dma_start(raw[n][:, :].rearrange("p (k n) -> p k n", k=KC), expert_src(kind, e, c))\
                    .then_inc(raw_loaded[n], 16)
            sp.wait_ge(h2_stored[0], 16 * ((TT + 1) // 2))
            sp.wait_ge(h2_stored[1], 16 * (TT // 2))
            sp.wait_ge(state_stored, 16 * (3 + DEC_B + DEC_B))

        @block.gpsimd
        def _(pool):
            def step(ins):
                step.n += 1
                ins.then_inc(pool_step, 1)
                pool.wait_ge(pool_step, step.n)
            step.n = 0
            step(pool.memset(ident[:, :], 0.0))
            step(pool.affine_select(out=ident[:, :], in_=ident[:, :], compare_op=ALU.not_equal, fill=1.0,
                                    base=0, pattern=[[-1, P]], channel_multiplier=1))
            step(pool.memset(zeros[:, :], 0.0))
            for b in range(MAX_OV):
                pool.dma_start(y_dram[MAIN_ROWS + b * P:MAIN_ROWS + (b + 1) * P, :]
                               .rearrange("p (a n) -> p a n", n=ZW),
                               zeros[:, :].unsqueeze(1).to_broadcast([P, D // ZW, ZW])).then_inc(rows_zeroed, 16)
            pool.memset(eps_c[:, :], EPS).then_inc(consts, 1)
            pool.memset(ss[:, :], 1.0).then_inc(consts, 1)
            step(pool.memset(sel_p[:, :], 1.0))
            step(pool.affine_select(out=sel_p[:, :], in_=sel_p[:, :], compare_op=ALU.is_equal, fill=0.0,
                                    base=0, pattern=[[0, P]], channel_multiplier=1))
            step(pool.memset(sel_s[:, :], 1.0))
            step(pool.affine_select(out=sel_s[:, :].rearrange("p (s t) -> p s t", t=DEC_T),
                                    in_=sel_s[:, :].rearrange("p (s t) -> p s t", t=DEC_T),
                                    compare_op=ALU.is_equal, fill=0.0,
                                    base=-1, pattern=[[-1, DEC_B], [0, DEC_T]], channel_multiplier=1))
            step(pool.memset(tri[:, :], 1.0))
            step(pool.affine_select(out=tri[:, :], in_=tri[:, :], compare_op=ALU.is_gt, fill=0.0,
                                    base=0, pattern=[[1, P]], channel_multiplier=-1))
            step(pool.memset(ones_bf[:, :], 1.0))
            step(pool.iota(iota_m[:, :], pattern=[[1, P]], base=0, channel_multiplier=0,
                           allow_small_or_imprecise_dtypes=True))
            step(pool.iota(iota_e[:, :], pattern=[[1, E]], base=0, channel_multiplier=0,
                           allow_small_or_imprecise_dtypes=True))
            step(pool.iota(iota_j[:, :], pattern=[[1, MAX_OV]], base=0, channel_multiplier=0,
                           allow_small_or_imprecise_dtypes=True))
            step(pool.iota(tok_bf[:, :, 0], pattern=[[P, TT]], base=0, channel_multiplier=0,
                           allow_small_or_imprecise_dtypes=True))
            step(pool.iota(tok_bf[:, :, 1], pattern=[[0, TT]], base=0, channel_multiplier=1,
                           allow_small_or_imprecise_dtypes=True))
            for half in range(2):
                step(pool.iota(expert_id2[half * E:(half + 1) * E, :], pattern=[[1, E + 1]], base=0,
                               channel_multiplier=0, allow_small_or_imprecise_dtypes=True))
                step(pool.iota(pmod[half * E:(half + 1) * E, :], pattern=[[0, 1]], base=0,
                               channel_multiplier=1, allow_small_or_imprecise_dtypes=True))
            for w in range(16):
                pool.memset(inv_n[:, w:w + 1], 1.0 / (w + 1)).then_inc(consts, 1)
            pool.memset(uext[:, :, 0:PAST], 0.0).then_inc(consts, 1)
            pool.memset(vext[:, :, 0:CPAST], 0.0).then_inc(consts, 1)
            pool.memset(mask[:, :, :], 0.0).then_inc(consts, 1)
            pool.memset(rank_m[:, :, :], -1.0).then_inc(consts, 1)
            pool.memset(slot_f[:, :, :], -1.0).then_inc(consts, 1)
            assert step.n == POOL_STEPS
            pool.wait_ge(rows_zeroed, 16 * MAX_OV)

        @block.scalar
        def _(act):
            act.dma_start(x_sb[:, 0:PT, :], x_prompt[0].rearrange("(t p) d -> p t d", p=P)).then_inc(x_loaded, 16)
            act.dma_start(x_sb[0:NS, PT, :], x_sample.rearrange("b t d -> (b t) d")).then_inc(x_loaded, 16)
            act.dma_start(mod[:, :], b_ada.partition_broadcast(NC).rearrange("a b n -> a (b n)")).then_inc(rows_loaded, 16)
            act.dma_start(n1_rows, norm1.partition_broadcast(NC).rearrange("a b n -> a (b n)")).then_inc(rows_loaded, 16)
            act.dma_start(n2_rows[:, :], norm2.partition_broadcast(NC).rearrange("a b n -> a (b n)")).then_inc(rows_loaded, 16)
            act.dma_start(par_rows[0:GR, :], pool_scale[0].rearrange("(g p) -> g p", p=P)).then_inc(small_loaded, 16)
            act.dma_start(par_rows[GR:4 * GR, :], w_conv[0].rearrange("w (g p) -> (w g) p", p=P))\
                .then_inc(small_loaded, 16)
            act.dma_start(sp_rows[:, :], state_pool[0].rearrange("b r d -> (b r) d")).then_inc(small_loaded, 16)
            act.dma_start(sc_rows[:, :], state_conv[0].rearrange("b r d -> (b r) d")).then_inc(small_loaded, 16)
            act.dma_start(wpool_sb[:, :, :], w_pool[0].rearrange("g c d -> c g d")).then_inc(small_loaded, 16)
            act.dma_start(wr_sb[:, :, :], w_router[0].rearrange("(k p) e -> p k e", p=P)).then_inc(small_loaded, 16)
            act.dma_start(br_bc[:, :], b_router.partition_broadcast(P).rearrange("a b n -> a (b n)")).then_inc(small_loaded, 16)
            for m, b in enumerate((b_gate, b_up, b_down)):
                for half in range(2):
                    act.dma_start(b_raw[m][half * E:(half + 1) * E, :], b[0]).then_inc(bias_loaded, 16)
            for s in range(DEC_B):
                act.dma_start(new_pool_sample[0, s, 0:PAST - DEC_T, :], state_pool[0, s, DEC_T:PAST, :])\
                    .then_inc(state_stored, 16)

            act.wait_ge(c_tp, 1)
            act.activation(c_sg[:, :, :], c_ps, ACT.Sigmoid).then_inc(sig_ready, 1)
            act.wait_ge(bias_loaded, 16 * 6)
            for m in range(3):
                act.activation(bias_t[m][:, :], b_raw[m], ACT.Copy).then_inc(bias_hi, 1)

            def squares(done):
                for t in range(TT):
                    r = norm_rows(t)
                    if done == 0 and t == 0:
                        act.wait_ge(x_loaded, 32)
                        act.wait_ge(consts, 2)
                    if done:
                        act.wait_ge(x1_ready, OUT_CH * TT - TT + t + 1)
                    if done or t:
                        act.wait_ge(act_step, done * TT + t)
                    act.activation(junk[0:r, :], x_sb[0:r, t, :], ACT.Square,
                                   accum_out=ss[0:r, t:t + 1]).then_inc(act_step, 1)
                act.wait_ge(act_step, (done + 1) * TT)
                if done:
                    act.wait_ge(rstd_ready, 1)
                act.activation(ss[:, :], ss[:, :], ACT.Sqrt, bias=eps_c[:, 0:1], scale=1.0 / D).then_inc(sq_done, 1)

            def spread_evac(t, base):
                act.wait_ge(h_tp, base + t + 1)
                r = norm_rows(t)
                act.activation(h_t[:, :, t * P:t * P + r],
                               tp[:, :, :].rearrange("p b (k n) -> p (b k) n", n=P)[:, :, 0:r],
                               ACT.Copy).then_inc(ht_ready, 1)

            act.wait_ge(bias_ready, 3)
            squares(0)
            act.wait_ge(par_tp, 1)
            act.activation(par[:, 0:4 * GR], tp[:, 0, 0:4 * GR], ACT.Copy).then_inc(par_ready, 1)
            act.wait_ge(st_tp, 1)
            for g in range(GR):
                act.activation(uext_s[:, g, :, 0:PAST],
                               tp[:, 0, g * DEC_B * PAST:(g + 1) * DEC_B * PAST].rearrange("p (s r) -> p s r", r=PAST),
                               ACT.Copy).then_inc(st_ready, 1)
                act.activation(vext_s[:, g, :, 0:CPAST],
                               tp[:, 1, g * DEC_B * CPAST:(g + 1) * DEC_B * CPAST].rearrange("p (s r) -> p s r", r=CPAST),
                               ACT.Copy).then_inc(st_ready, 1)
            for t in range(TT):
                spread_evac(t, 0)
            for f in range(3 * GR):
                act.wait_ge(z_done, f + 1)
                dst = [uext[:, f % GR, PAST:PAST + SEQ], gate_b[:, f % GR, 0:SEQ], gate_c[:, f % GR, 0:SEQ]][f // GR]
                act.activation(dst, zp[f % 4], ACT.Copy).then_inc(z_evac_a, 1)
            act.wait_ge(z_done, 4 * GR)
            for g in range(GR):
                act.activation(uext_s[:, g, :, PAST:PAST + DEC_T],
                               zs[:, g, :].rearrange("p (s t) -> p s t", t=DEC_T), ACT.Copy).then_inc(z_evac_a, 1)
            act.activation(gate_b[:, :, SEQ:NTOK], zs[:, GR:2 * GR, :], ACT.Copy).then_inc(z_evac_a, 1)
            act.activation(gate_c[:, :, SEQ:NTOK], zs[:, 2 * GR:3 * GR, :], ACT.Copy).then_inc(z_evac_a, 1)
            act.wait_ge(spread_done["g1"], 1)
            act.activation(g1_bc[:, :], tp[:, :, :].rearrange("p b n -> p (b n)"), ACT.Copy).then_inc(g1_ready, 1)
            act.wait_ge(spread_done["g1_s"], 1)
            act.activation(g1_bc_s[:, :], tp[0:NS, :, :].rearrange("p b n -> p (b n)"), ACT.Copy).then_inc(g1_ready, 1)
            for g in range(GR):
                act.wait_ge(pm_done, g + 1)
                act.activation(mix_t[:, g, 0:SEQ], zp[g], ACT.Identity, scale=par[:, g:g + 1]).then_inc(pm_ready, 1)
            for g in range(GR):
                act.activation(mix_t[:, g, SEQ:NTOK], tp[:, 0, g * NS:(g + 1) * NS], ACT.Identity,
                               scale=par[:, g:g + 1]).then_inc(pm_ready, 1)
            act.wait_ge(conv_ready, 2 * GR)
            act.activation(u_new.rearrange("p g (s t) -> p g s t", t=DEC_T),
                           uext_s[:, :, :, PAST:PAST + DEC_T], ACT.Copy).then_inc(new_packed, 1)
            act.activation(v_new.rearrange("p g (s t) -> p g s t", t=CPAST),
                           vext_s[:, :, :, DEC_T:DEC_T + CPAST], ACT.Copy).then_inc(new_packed, 1)
            for i in range(4):
                act.wait_ge(so_tp, i // 2 + 1)
                n = state_o[i].shape[0]
                act.activation(state_o[i], tp[0:n, i % 2, :], ACT.Copy).then_inc(so_ready, 1)
            act.wait_ge(so_ready, 4)
            act.dma_start(new_pool_prompt[0, 0], state_o[0]).then_inc(state_stored, 16)
            act.dma_start(new_conv_prompt[0, 0], state_o[1]).then_inc(state_stored, 16)
            for s in range(DEC_B):
                act.dma_start(new_pool_sample[0, s, PAST - DEC_T:PAST, :],
                              gate_b[s * DEC_T:(s + 1) * DEC_T, 2, 0:DP]).then_inc(state_stored, 16)
            act.dma_start(new_conv_sample[0].rearrange("b r d -> (b r) d"), state_o[3]).then_inc(state_stored, 16)

            squares(1)
            for t in range(TT):
                spread_evac(t, TT)
            for t in range(TT):
                r = norm_rows(t)
                act.wait_ge(top_ready, t + 1)
                act.activation(gates[0:r, t, :], top_v[0:r, t, 0:TOPK], ACT.Exp, bias=neg_m[0:r, t:t + 1],
                               accum_out=e_sum[0:r, t:t + 1]).then_inc(exp_done, 1)

        @block.vector
        def _(dve):
            def step(ins):
                step.n += 1
                ins.then_inc(dve_step, 1)
                dve.wait_ge(dve_step, step.n)
            step.n = 0

            dve.wait_ge(sig_ready, 1)
            dve.tensor_tensor(c_act[:, :, :], c_ps, c_sg[:, :, :], ALU.mult).then_inc(c_ready, 1)
            dve.wait_ge(bias_hi, 3)
            for m in range(3):
                dve.tensor_tensor(bias_t[m][E:2 * E, :], b_raw[m][E:2 * E, :],
                                  bias_t[m][E:2 * E, :].bitcast(F32), ALU.subtract).then_inc(bias_ready, 1)

            def add_ada(n):
                dve.wait_ge(ada_done, n + 1)
                dve.tensor_tensor(mod[:, n * CW:(n + 1) * CW], mod[:, n * CW:(n + 1) * CW],
                                  modp[n % 2][0:NC, :], ALU.add).then_inc(ada_added, 1)

            def scale_rows(part_, norm):
                sc = mod[:, part_ * D:(part_ + 1) * D]
                dve.scalar_tensor_tensor(out=sc, in0=sc, scalar=1.0, in1=norm, op0=ALU.add,
                                         op1=ALU.mult).then_inc(scale_ready, 1)

            def normalise(t, base):
                r = norm_rows(t)
                if t >= 2:
                    dve.wait_ge(h_tp, base + t - 1)
                    if base:
                        dve.wait_ge(h2_stored[t % 2], 16 * (t // 2))
                if t in (0, PT):
                    dve.wait_ge(spread_done[("n2" if base else "n1") + ("_s" if t == PT else "")], 1)
                h = h_row[t % 2][0:r, :]
                step(dve.scalar_tensor_tensor(out=h, in0=x_sb[0:r, t, :], scalar=rstd[0:r, t:t + 1],
                                              in1=acc_g[0:r, :, :].rearrange("p b n -> p (b n)"),
                                              op0=ALU.mult, op1=ALU.mult))
                dve.tensor_tensor(h, h, acc_u[0:r, :, :].rearrange("p b n -> p (b n)"), ALU.add).then_inc(h_ready, 1)

            dve.wait_ge(bias_ready, 3)
            dve.wait_ge(rows_loaded, 48)
            for n in range(ADA_FIRST):
                add_ada(n)
            dve.wait_ge(ada_added, ADA_FIRST)
            scale_rows(1, n1_rows)
            for n in range(ADA_FIRST, ADA_FIRST + D // CW):
                add_ada(n)
            dve.wait_ge(sq_done, 1)
            dve.reciprocal(rstd[:, :], ss[:, :]).then_inc(rstd_ready, 1)
            dve.wait_ge(rstd_ready, 1)
            for t in range(TT):
                if t < 4:
                    add_ada(ADA_FIRST + D // CW + t)
                normalise(t, 0)
            for n in range(ADA_FIRST + D // CW + 4, ADA_FIRST + ADA_MID):
                add_ada(n)
            dve.wait_ge(ada_added, ADA_FIRST + ADA_MID)
            scale_rows(4, n2_rows[:, :])

            def windows(src_, n, ext, buf):
                cur, w, i = src_, 1, 0
                while w < n:
                    o = buf[i % 2]
                    step(dve.tensor_tensor(o[..., 2 * w - 1:ext], cur[..., 2 * w - 1:ext],
                                           cur[..., w - 1:ext - w], ALU.add))
                    cur, w, i = o, 2 * w, i + 1
                return cur

            dve.wait_ge(consts, CONSTS)
            for g in range(GR):
                f = 3 * GR + g
                dve.wait_ge(z_done, f + 1)
                dve.wait_ge(z_evac_a, 2 * GR + g + 1)
                dve.tensor_tensor(vext[:, g, CPAST:CPAST + SEQ], zp[f % 4], gate_c[:, g, 0:SEQ], ALU.mult)\
                    .then_inc(v_ready, 1)
            dve.wait_ge(z_evac_a, 3 * GR + GR + 2)
            dve.wait_ge(st_ready, 2 * GR)
            for g in range(GR):
                dve.tensor_tensor(vext_s[:, g, :, CPAST:CPAST + DEC_T],
                                  zs[:, 3 * GR + g, :].rearrange("p (s t) -> p s t", t=DEC_T),
                                  gate_c[:, g, SEQ:NTOK].rearrange("p (s t) -> p s t", t=DEC_T),
                                  ALU.mult).then_inc(v_ready, 1)
            dve.wait_ge(v_ready, 2 * GR)
            for g, w in enumerate(WINDOWS):
                s = windows(uext[:, g, :], w, PAST + SEQ, [wsum[0][:, :], wsum[1][:, :]])
                dve.scalar_tensor_tensor(out=pooled[:, g, w - 1:SEQ], in0=s[:, PAST + w - 1:PAST + SEQ],
                                         scalar=1.0 / w, in1=uext[:, g, PAST + w - 1:PAST + SEQ],
                                         op0=ALU.mult, op1=ALU.subtract).then_inc(pooled_ready, 1)
                step(dve.tensor_tensor(s[:, PAST:PAST + w - 1], s[:, PAST:PAST + w - 1], inv_n[:, 0:w - 1], ALU.mult))
                dve.tensor_tensor(pooled[:, g, 0:w - 1], s[:, PAST:PAST + w - 1], uext[:, g, PAST:PAST + w - 1],
                                  ALU.subtract).then_inc(pooled_ready, 1)
                dve.wait_ge(pooled_ready, 3 * g + 2)
                bufs = [b[:, 0:DEC_B * (PAST + DEC_T)].rearrange("p (s r) -> p s r", s=DEC_B) for b in wsum]
                s = windows(uext_s[:, g, :, :], w, PAST + DEC_T, [bufs[0], bufs[1]])
                dve.scalar_tensor_tensor(out=pooled[:, g, SEQ:NTOK].rearrange("p (s t) -> p s t", t=DEC_T),
                                         in0=s[:, :, PAST:PAST + DEC_T], scalar=1.0 / w,
                                         in1=uext_s[:, g, :, PAST:PAST + DEC_T],
                                         op0=ALU.mult, op1=ALU.subtract).then_inc(pooled_ready, 1)
                dve.wait_ge(pooled_ready, 3 * g + 3)
            dve.wait_ge(par_ready, 1)
            for g in range(GR):
                for v, y, b in ((vext[:, g, :], mix_t[:, GR + g, 0:SEQ], gate_b[:, g, 0:SEQ]),
                                (vext_s[:, g, :, :],
                                 mix_t[:, GR + g, SEQ:NTOK].rearrange("p (s t) -> p s t", t=DEC_T),
                                 gate_b[:, g, SEQ:NTOK].rearrange("p (s t) -> p s t", t=DEC_T))):
                    n = y.shape[-1]
                    tap = [par[:, (1 + j) * GR + g:(1 + j) * GR + g + 1] for j in range(3)]
                    step(dve.tensor_scalar(y, v[..., 0:n], tap[0], None, ALU.mult))
                    step(dve.scalar_tensor_tensor(out=y, in0=v[..., 1:1 + n], scalar=tap[1], in1=y,
                                                  op0=ALU.mult, op1=ALU.add))
                    step(dve.scalar_tensor_tensor(out=y, in0=v[..., 2:2 + n], scalar=tap[2], in1=y,
                                                  op0=ALU.mult, op1=ALU.add))
                    dve.tensor_tensor(y, y, b, ALU.mult).then_inc(conv_ready, 1)
            dve.wait_ge(g1_ready, 2)
            for k in range(OUT_CH):
                for t in range(TT):
                    r = norm_rows(t)
                    n = k * TT + t
                    dve.wait_ge(mix_done, n + 1)
                    g1 = g1_bc if t < PT else g1_bc_s
                    w = wsum[n % 2]
                    step(dve.tensor_tensor(w[0:r, 0:CW], zp[n % 4][0:r, 0:CW], g1[0:r, k * CW:(k + 1) * CW], ALU.mult))
                    dve.tensor_tensor(x_sb[0:r, t, k * CW:(k + 1) * CW], x_sb[0:r, t, k * CW:(k + 1) * CW],
                                      w[0:r, 0:CW], ALU.add).then_inc(x1_ready, 1)
            for n in range(ADA_FIRST + ADA_MID, ADA_CH):
                add_ada(n)
            dve.wait_ge(ada_added, ADA_CH)
            step(dve.tensor_copy(g2_rows[:, :], mod[:, 5 * D:6 * D]))
            dve.wait_ge(sq_done, 2)
            dve.reciprocal(rstd[:, :], ss[:, :]).then_inc(rstd_ready, 1)
            dve.wait_ge(rstd_ready, 2)
            for t in range(TT):
                normalise(t, TT)

            dve.wait_ge(pool_step, POOL_STEPS)
            for t in range(TT):
                r = norm_rows(t)
                if t == 0:
                    dve.wait_ge(lg_done, TT)
                step(dve.tensor_tensor(logit[0:r, t, :], lg[0:r, t * E:(t + 1) * E], br_bc[0:r, :], ALU.add))
                step(dve.max(top_v[0:r, t, :], logit[0:r, t, :]))
                step(dve.max_index(top_i[0:r, t, :], top_v[0:r, t, :], logit[0:r, t, :]))
                dve.tensor_scalar(neg_m[0:r, t:t + 1], top_v[0:r, t, 0:1], -1.0, None, ALU.mult).then_inc(top_ready, 1)
                step(dve.tensor_copy(top_f[0:r, t, :], top_i[0:r, t, :]))
                for k in range(TOPK):
                    ins = dve.tensor_scalar(onehot[0:r, t, k, :], iota_e[0:r, :], top_f[0:r, t, k:k + 1], None,
                                            ALU.is_equal)
                    step(ins)
                step(dve.tensor_reduce(mask[0:r, t, :], onehot[0:r, t, :, :].rearrange("p k e -> p e k"),
                                       AX.X, ALU.add))
            dve.tensor_copy(mask_bf[:, :, :], mask[:, :, :]).then_inc(mask_ready, 1)
            for t in range(TT):
                r = norm_rows(t)
                dve.wait_ge(exp_done, t + 1)
                step(dve.reciprocal(e_sum[0:r, t:t + 1], e_sum[0:r, t:t + 1]))
                step(dve.tensor_scalar(gates[0:r, t, :], gates[0:r, t, :], e_sum[0:r, t:t + 1], None, ALU.mult))

            dve.wait_ge(rank_done, 1)
            counts = lg[:, 2 * TT * E:2 * TT * E + E]
            cnt, nb, run_a, run_b, e128, far, tmp = [s[:, :] for s in small]
            step(dve.tensor_copy(cnt, counts))
            step(dve.tensor_scalar(nb, cnt, float(P), None, ALU.is_gt))
            for k in range(2, EXTRA + 1):
                step(dve.scalar_tensor_tensor(out=nb, in0=cnt, scalar=float(k * P), in1=nb,
                                              op0=ALU.is_gt, op1=ALU.add))
            cur, w = nb, 1
            bufs = [run_a, run_b]
            while w < E:
                o = bufs[0]
                step(dve.tensor_copy(o[:, 0:w], cur[:, 0:w]))
                step(dve.tensor_tensor(o[:, w:E], cur[:, w:E], cur[:, 0:E - w], ALU.add))
                cur, w = o, 2 * w
                bufs.reverse()
            incl = cur
            step(dve.tensor_copy(n_ov_i[:, :], incl[:, E - 1:E]))
            step(dve.tensor_tensor(ov_cmp[:, :, :], incl.unsqueeze(1).to_broadcast([P, MAX_OV, E]),
                                   iota_j[:, :].unsqueeze(2).to_broadcast([P, MAX_OV, E]), ALU.is_le))
            step(dve.tensor_reduce(ov_expert[:, :], ov_cmp[:, :, :], AX.X, ALU.add))
            step(dve.tensor_scalar(ov_expert[:, :], ov_expert[:, :], float(E - 1), None, ALU.min))
            step(dve.tensor_copy(ov_expert_i[:, :], ov_expert[:, :]))
            step(dve.tensor_scalar(e128, iota_e[:, :], float(P), None, ALU.mult))
            step(dve.tensor_tensor(far, incl, nb, ALU.subtract))
            step(dve.tensor_scalar(far, far, float(P), float(MAIN_ROWS - P), ALU.mult, ALU.add))
            step(dve.tensor_tensor(far, far, e128, ALU.subtract))
            for t in range(TT):
                r = norm_rows(t)
                rank = lg[0:r, (TT + t) * E:(TT + t + 1) * E]
                step(dve.tensor_scalar(over[0:r, :], rank, float(P), None, ALU.is_ge))
                step(dve.tensor_tensor(over[0:r, :], over[0:r, :], far[0:r, :], ALU.mult))
                step(dve.tensor_tensor(over[0:r, :], over[0:r, :], e128[0:r, :], ALU.add))
                step(dve.tensor_tensor(slot_e[0:r, :], over[0:r, :], rank, ALU.add))
                step(dve.tensor_tensor(pick[0:r, :, :], onehot[0:r, t, :, :],
                                       slot_e[0:r, :].unsqueeze(1).to_broadcast([r, TOPK, E]), ALU.mult))
                step(dve.tensor_reduce(slot_f[0:r, t, :], pick[0:r, :, :], AX.X, ALU.add))
                step(dve.scalar_tensor_tensor(out=tmp[0:r, :], in0=rank, scalar=1.0, in1=mask[0:r, t, :],
                                              op0=ALU.add, op1=ALU.mult))
                step(dve.tensor_scalar(rank_m[0:r, t, 0:E], tmp[0:r, :], -1.0, None, ALU.add))
                step(dve.tensor_copy(slot_i[0:r, t, :], slot_f[0:r, t, :]))
            step(dve.tensor_scalar(slot_rel[:, :, :], slot_f[:, :, :], -float(MAIN_ROWS), None, ALU.add))

        @block.tensor
        def _(pe):
            def chunk(kind, k):
                n = at[(kind, k)]
                pe.wait_ge(raw_loaded[n % SLOTS], 16 * (n // SLOTS + 1))
                return chunk_view(n)

            def ada(n):
                w = chunk("ada", n)
                if n >= 2:
                    pe.wait_ge(ada_added, n - 1)
                for k in range(KT):
                    mm = pe.matmul(modp[n % 2][0:NC, :], c_act[:, k, :], w[:, k, :], start=(k == 0), stop=(k == KT - 1))
                mm.then_inc(ada_done, 1)

            def spread(sel, r, part_, dst):
                for h in range(2):
                    mm = pe.matmul(dst[0:r, h, :], sel[:, 0:r],
                                   mod[:, part_ * D + h * HALF:part_ * D + (h + 1) * HALF], start=True, stop=True)
                return mm

            def transposes(t, base):
                pe.wait_ge(h_ready, base + t + 1)
                if base + t:
                    pe.wait_ge(ht_ready, base + t)
                r = norm_rows(t)
                for k in range(KT):
                    mm = pe.transpose(tp[:, k // 4, (k % 4) * P:(k % 4) * P + r],
                                      h_row[t % 2][0:r, k * P:(k + 1) * P], ident[0:r, 0:r])
                mm.then_inc(h_tp, 1)

            pe.wait_ge(c_loaded, 32)
            pe.wait_ge(pool_step, 2)
            for k in range(KT):
                mm = pe.transpose(c_ps[:, k, :], c_rows[:, k * P:(k + 1) * P], ident[0:NC, 0:NC])
            mm.then_inc(c_tp, 1)
            pe.wait_ge(c_ready, 1)
            for n in range(ADA_FIRST):
                ada(n)
            pe.wait_ge(small_loaded, 16 * 7)
            pe.wait_ge(pool_step, POOL_STEPS)
            pe.transpose(tp[:, 0, 0:4 * GR], par_rows[0:4 * GR, :], ident[0:4 * GR, 0:4 * GR]).then_inc(par_tp, 1)
            pe.wait_ge(par_ready, 1)
            for g in range(GR):
                n = DEC_B * PAST
                pe.transpose(tp[:, 0, g * n:(g + 1) * n], sp_rows[:, g * P:(g + 1) * P], ident[0:n, 0:n])
            for g in range(GR):
                n = DEC_B * CPAST
                mm = pe.transpose(tp[:, 1, g * n:(g + 1) * n], sc_rows[:, g * P:(g + 1) * P], ident[0:n, 0:n])
            mm.then_inc(st_tp, 1)
            for n in range(ADA_FIRST, ADA_FIRST + D // CW):
                ada(n)
            pe.wait_ge(scale_ready, 1)
            spread(sel_p, P, 1, acc_g)
            spread(sel_p, P, 0, acc_u).then_inc(spread_done["n1"], 1)
            pe.wait_ge(st_ready, 2 * GR)
            for t in range(TT):
                if t < 4:
                    ada(ADA_FIRST + D // CW + t)
                if t == PT:
                    pe.wait_ge(h_ready, PT)
                    spread(sel_s, NS, 1, acc_g)
                    spread(sel_s, NS, 0, acc_u).then_inc(spread_done["n1_s"], 1)
                transposes(t, 0)
            for n in range(ADA_FIRST + D // CW + 4, ADA_FIRST + ADA_MID):
                ada(n)
            pe.wait_ge(ht_ready, TT)
            pe.wait_ge(ada_added, ADA_FIRST + ADA_MID)
            for f in range(4 * GR):
                w = chunk("in", f // 2)
                if f >= 4:
                    pe.wait_ge(z_evac_a, f - 3)
                for k in range(KT):
                    lhs = w[:, k, (f % 2) * P:(f % 2 + 1) * P]
                    pe.matmul(zp[f % 4], lhs, h_t[:, k, 0:SEQ], start=(k == 0), stop=(k == KT - 1))
                for k in range(KT):
                    lhs = w[:, k, (f % 2) * P:(f % 2 + 1) * P]
                    mm = pe.matmul(zs[:, f, :], lhs, h_t[:, k, SEQ:NTOK], start=(k == 0), stop=(k == KT - 1))
                mm.then_inc(z_done, 1)
            spread(sel_p, P, 2, tp).then_inc(spread_done["g1"], 1)
            pe.wait_ge(g1_ready, 1)
            spread(sel_s, NS, 2, tp).then_inc(spread_done["g1_s"], 1)
            pe.wait_ge(g1_ready, 2)
            pe.wait_ge(v_ready, GR)
            for g in range(GR):
                pe.wait_ge(pooled_ready, 3 * (g + 1))
                pe.matmul(zp[g], wpool_sb[:, g, :], pooled[:, g, 0:SEQ], start=True, stop=True)
                pe.matmul(tp[:, 0, g * NS:(g + 1) * NS], wpool_sb[:, g, :], pooled[:, g, SEQ:NTOK],
                          start=True, stop=True).then_inc(pm_done, 1)
            pe.wait_ge(pm_ready, 2 * GR)
            pe.wait_ge(conv_ready, 2 * GR)
            for k in range(OUT_CH):
                w = chunk("out", k)
                for t in range(TT):
                    n, r = k * TT + t, norm_rows(t)
                    if n >= 4:
                        pe.wait_ge(x1_ready, n - 3)
                    for j in range(2 * GR):
                        mm = pe.matmul(zp[n % 4][0:r, 0:CW], mix_t[:, j, t * P:t * P + r], w[:, j, :],
                                       start=(j == 0), stop=(j == 2 * GR - 1))
                    mm.then_inc(mix_done, 1)
            pe.wait_ge(v_ready, 2 * GR)
            for n in range(ADA_FIRST + ADA_MID, ADA_CH):
                ada(n)
            for g in range(GR):
                pe.transpose(tp[0:PAST, 0, g * P:(g + 1) * P], uext[:, g, SEQ:SEQ + PAST], ident[:, :])
            for g in range(GR):
                mm = pe.transpose(tp[0:CPAST, 1, g * P:(g + 1) * P], vext[:, g, SEQ:SEQ + CPAST], ident[:, :])
            mm.then_inc(so_tp, 1)
            pe.wait_ge(so_ready, 2)
            pe.wait_ge(new_packed, 2)
            for g in range(GR):
                pe.transpose(tp[0:NS, 0, g * P:(g + 1) * P], u_new[:, g, :], ident[:, :])
            for g in range(GR):
                mm = pe.transpose(tp[0:DEC_B * CPAST, 1, g * P:(g + 1) * P], v_new[:, g, :], ident[:, :])
            mm.then_inc(so_tp, 1)
            pe.wait_ge(scale_ready, 2)
            pe.wait_ge(x1_ready, OUT_CH * TT)
            spread(sel_p, P, 4, acc_g)
            spread(sel_p, P, 3, acc_u).then_inc(spread_done["n2"], 1)
            pe.wait_ge(so_ready, 4)

            def router(t):
                r = norm_rows(t)
                pe.wait_ge(ht_ready, TT + t + 1)
                if t == 0:
                    pe.wait_ge(ada_added, ADA_CH)
                for k in range(KT):
                    mm = pe.matmul(lg[0:r, t * E:(t + 1) * E], h_t[:, k, t * P:t * P + r], wr_sb[:, k, :],
                                   start=(k == 0), stop=(k == KT - 1))
                mm.then_inc(lg_done, 1)

            for t in range(TT):
                if t == PT:
                    pe.wait_ge(h_ready, TT + PT)
                    spread(sel_s, NS, 4, acc_g)
                    spread(sel_s, NS, 3, acc_u).then_inc(spread_done["n2_s"], 1)
                transposes(t, TT)
                if t:
                    router(t - 1)
            router(TT - 1)
            pe.wait_ge(mask_ready, 1)
            for t in range(TT):
                out_ = lg[:, (TT + t) * E:(TT + t + 1) * E]
                pe.matmul(out_, tri[:, :], mask_bf[:, t, :], start=True, stop=(t == 0))
                for b in range(t):
                    pe.matmul(out_, ones_bf[:, :], mask_bf[:, b, :], start=False, stop=(b == t - 1))
            for t in range(TT):
                mm = pe.matmul(lg[:, 2 * TT * E:2 * TT * E + E], ones_bf[:, :], mask_bf[:, t, :],
                               start=(t == 0), stop=(t == TT - 1))
            mm.then_inc(rank_done, 1)

        part.close()

        NCH = 3 * MCH
        TOTAL = E * NCH

        def pos(i, c):
            if isinstance(i, int) and i == 0:
                return c
            if isinstance(i, int) and i == E:
                return NCH * E - MCH + c - 2 * MCH
            return i * NCH + (c - MCH)

        def ring(i, c, n):
            return (pos(i, c) if isinstance(i, int) else pos(1, c)) % n

        assert NCH % SLOTS == 0 and NCH % SPLIT == 0

        def loaded_value(i, c):
            if isinstance(i, int):
                return 16 * ((DENSE_CH + pos(i, c)) // SLOTS + 1)
            base = (DENSE_CH + pos(1, c)) // SLOTS + 1
            return (i - 1) * (16 * NCH // SLOTS) + 16 * base

        with ExitStack() as experts:
            def sb(name, shape, dt=F32):
                return experts.enter_context(nc.sbuf_tensor(name, shape, dt))

            w_hi = [sb(f"w_hi{s}", [P, SLOT_F], F32R) for s in range(SPLIT)]
            w_lo = [sb(f"w_lo{s}", [P, SLOT_F], F32R) for s in range(SPLIT)]
            rows = sb("rows", [P, D])
            ht_hi = sb("ht_hi", [P, KT, P], F32R)
            ht_lo = sb("ht_lo", [P, KT, P], F32R)
            at_hi = sb("at_hi", [P, KT, P], F32R)
            at_lo = sb("at_lo", [P, KT, P], F32R)
            g_sb = sb("g_sb", [P, D])
            s_sb = sb("s_sb", [P, D])
            u_sb = sb("u_sb", [P, D])
            a_sb = sb("a_sb", [P, D])
            y_sb = sb("y_sb", [P, D])
            member = sb("member", [P, TT, P], BF16)
            row_id = sb("row_id", [P, 1], U32)
            sel_gu = sb("sel_gu", [2 * E, P], F32R)
            sel_d = sb("sel_d", [2 * E, P], F32R)

            hi_ready = sem("hi_ready")
            lo_ready = sem("lo_ready")
            mm_done = sem("mm_done")
            member_ready = sem("member_ready")
            id_done = sem("id_done")
            id_ready = sem("id_ready")
            row_gathered = sem("row_gathered")
            row_tp = sem("row_tp")
            ht_hi_ready = sem("ht_hi_ready")
            ht_lo_ready = sem("ht_lo_ready")
            g_clipped = sem("g_clipped")
            sig_done = sem("sig_done")
            u_clipped = sem("u_clipped")
            glu_done = sem("glu_done")
            act_ready = sem("act_ready")
            act_tp = sem("act_tp")
            at_hi_ready = sem("at_hi_ready")
            at_lo_ready = sem("at_lo_ready")
            sel_gu_ready = sem("sel_gu_ready")
            sel_d_ready = sem("sel_d_ready")
            y_copied = sem("y_copied")
            y_stored = sem("y_stored")

            flat = lambda t: t[:, :, :].rearrange("p b n -> p (b n)")
            tp_flat, g_ps, u_ps, y_ps = flat(tp), flat(acc_g), flat(acc_u), flat(acc_y)

            block2 = experts.enter_context(nc.Block())

            @block2.sync
            def _(sp):
                def load(i, c):
                    n = pos(i, c)
                    s = ring(i, c, SLOTS)
                    kind = "gud"[c // MCH]
                    sp.wait_ge(lo_ready, n - (SLOTS - 1))
                    sp.dma_start(raw[s][:, :].rearrange("p (k n) -> p k n", k=KC),
                                 expert_src(kind, i - (kind == "d"), c % MCH)).then_inc(raw_loaded[s], 16)

                for c in range(SLOTS, 2 * MCH):
                    load(0, c)
                with sp.Fori(1, E) as i:
                    for c in range(NCH):
                        load(i, c)
                for c in range(2 * MCH, NCH):
                    load(E, c)

            @block2.gpsimd
            def _(pool):
                def gather(e):
                    pool.wait_ge(id_ready, e + 1)
                    if not isinstance(e, int):
                        pool.wait_ge(row_tp, e)
                        pool.nop(nofuse=True)
                    pool.indirect_dma_start(rows[:, :], None, h2_dram,
                                            bass.IndirectOffsetOnAxis(ap=row_id[:, 0:1], axis=0))\
                        .then_inc(row_gathered, 16)
                gather(0)
                with pool.Fori(1, E + 1) as e:
                    gather(e)

            @block2.scalar
            def _(act):
                def hi(i, c):
                    n = pos(i, c)
                    act.wait_ge(raw_loaded[ring(i, c, SLOTS)], loaded_value(i, c))
                    if not isinstance(n, int) or n >= SPLIT:
                        act.wait_ge(mm_done, n - (SPLIT - 1))
                    act.activation(w_hi[ring(i, c, SPLIT)][:, :], raw[ring(i, c, SLOTS)][:, :], ACT.Copy)\
                        .then_inc(hi_ready, 1)

                def y_out(e):
                    act.wait_ge(mm_done, pos(e + 2, 0) if not (isinstance(e, int) and e >= E - 2) else
                                NCH * (e + 2) - MCH if e == E - 2 else TOTAL)
                    if not (isinstance(e, int) and e == 0):
                        act.wait_ge(y_stored, 16 * e)
                    act.activation(y_sb[:, :], y_ps, ACT.Copy).then_inc(y_copied, 1)
                    act.wait_ge(y_copied, e + 1)
                    dst = y_dram[e * P:(e + 1) * P, :] if isinstance(e, int) else y_dram[bass.ds(e * P, P), :]
                    act.dma_start(dst, y_sb[:, :]).then_inc(y_stored, 16)

                def turn_hi(e):
                    act.wait_ge(row_tp, e + 1)
                    act.activation(flat(ht_hi), tp_flat, ACT.Copy).then_inc(ht_hi_ready, 1)

                def act_hi(e):
                    act.wait_ge(act_tp, e + 1)
                    act.activation(flat(at_hi), tp_flat, ACT.Copy).then_inc(at_hi_ready, 1)

                def sigmoid(e):
                    act.wait_ge(g_clipped, e + 1)
                    act.activation(s_sb[:, :], g_sb[:, :], ACT.Sigmoid, scale=ALPHA).then_inc(sig_done, 1)

                def step(i):
                    first = isinstance(i, int) and i == 0
                    for c in range(6):
                        hi(i, c)
                        if c == 1 and not (isinstance(i, int) and i < 2):
                            y_out(i - 2)
                    if not first:
                        act_hi(i - 1)
                    hi(i, 6)
                    sigmoid(i)
                    hi(i, 7)
                    if not first:
                        for c in range(8, NCH):
                            hi(i, c)
                    turn_hi(i + 1)

                turn_hi(0)
                step(0)
                step(1)
                step(2)
                with act.Fori(3, E) as i:
                    step(i)
                hi(E, 8)
                hi(E, 9)
                y_out(E - 2)
                act_hi(E - 1)
                hi(E, 10)
                hi(E, 11)
                y_out(E - 1)
                act.wait_ge(y_stored, 16 * E)

            @block2.vector
            def _(dve):
                def lo(i, c):
                    dve.wait_ge(hi_ready, pos(i, c) + 1)
                    s = ring(i, c, SPLIT)
                    dve.tensor_tensor(w_lo[s][:, :], raw[ring(i, c, SLOTS)][:, :], w_hi[s][:, :].bitcast(F32),
                                      ALU.subtract).then_inc(lo_ready, 1)

                def members(e):
                    if not (isinstance(e, int) and e == 0):
                        dve.wait_ge(id_done, e)
                    col = rank_m[:, :, e:e + 1] if isinstance(e, int) else rank_m[:, :, bass.ds(e, 1)]
                    dve.tensor_tensor(member[:, :, :], iota_m[:, :].unsqueeze(1).to_broadcast([P, TT, P]),
                                      col.to_broadcast([P, TT, P]), ALU.is_equal).then_inc(member_ready, 1)

                def ids(e):
                    dve.wait_ge(id_done, e + 1)
                    if not (isinstance(e, int) and e == 0):
                        dve.wait_ge(row_gathered, 16 * e)
                    with nc.allow_low_precision("whole numbers below 1024 are exact"):
                        dve.tensor_reduce(row_id[:, :], y_ps[:, 0:2], AX.X, ALU.add).then_inc(id_ready, 1)

                def select(out_, e, done):
                    col = expert_id2[:, e:e + 1] if isinstance(e, int) else expert_id2[:, bass.ds(e, 1)]
                    dve.tensor_scalar(out_[:, :], col.to_broadcast([2 * E, P]), pmod[:, 0:1], None, ALU.is_equal)\
                        .then_inc(done, 1)

                def turn_lo(e):
                    dve.wait_ge(ht_hi_ready, e + 1)
                    dve.tensor_tensor(flat(ht_lo), tp_flat, flat(ht_hi).bitcast(F32), ALU.subtract)\
                        .then_inc(ht_lo_ready, 1)

                def act_lo(e):
                    dve.wait_ge(at_hi_ready, e + 1)
                    dve.tensor_tensor(flat(at_lo), tp_flat, flat(at_hi).bitcast(F32), ALU.subtract)\
                        .then_inc(at_lo_ready, 1)
                    select(sel_d, e, sel_d_ready)

                def step(i):
                    first = isinstance(i, int) and i == 0
                    lo(i, 0)
                    members(i + 1)
                    for c in range(1, 6):
                        lo(i, c)
                    if not first:
                        act_lo(i - 1)
                    dve.wait_ge(mm_done, pos(i, 3) + 1)
                    if not first:
                        dve.wait_ge(glu_done, i)
                    dve.tensor_scalar(g_sb[:, :], g_ps, LIMIT, None, ALU.min).then_inc(g_clipped, 1)
                    ids(i + 1)
                    lo(i, 6)
                    lo(i, 7)
                    if not first:
                        lo(i, 8)
                        lo(i, 9)
                    dve.wait_ge(mm_done, pos(i, 7) + 1)
                    if not first:
                        dve.wait_ge(act_ready, i)
                    dve.tensor_scalar(u_sb[:, :], u_ps, LIMIT, -LIMIT, ALU.min, ALU.max).then_inc(u_clipped, 1)
                    if not first:
                        lo(i, 10)
                    dve.wait_ge(sig_done, i + 1)
                    dve.tensor_tensor(g_sb[:, :], g_sb[:, :], s_sb[:, :], ALU.mult).then_inc(glu_done, 1)
                    select(sel_gu, i + 1, sel_gu_ready)
                    dve.wait_ge(glu_done, i + 1)
                    dve.wait_ge(u_clipped, i + 1)
                    dve.scalar_tensor_tensor(out=a_sb[:, :], in0=u_sb[:, :], scalar=1.0, in1=g_sb[:, :],
                                             op0=ALU.add, op1=ALU.mult).then_inc(act_ready, 1)
                    if not first:
                        lo(i, 11)
                    turn_lo(i + 1)

                members(0)
                select(sel_gu, 0, sel_gu_ready)
                ids(0)
                turn_lo(0)
                step(0)
                with dve.Fori(1, E) as i:
                    step(i)
                lo(E, 8)
                lo(E, 9)
                act_lo(E - 1)
                lo(E, 10)
                lo(E, 11)

            @block2.tensor
            def _(pe):
                def row_ids(e):
                    pe.wait_ge(member_ready, e + 1)
                    for t in range(TT):
                        mm = pe.matmul(y_ps[:, 0:2], member[:, t, :], tok_bf[:, t, :], start=(t == 0),
                                       stop=(t == TT - 1))
                    mm.then_inc(id_done, 1)

                def turn(src_, done):
                    for k in range(KT):
                        mm = pe.transpose(tp_flat[:, k * P:(k + 1) * P], src_[:, k * P:(k + 1) * P], ident[:, :])
                    mm.then_inc(done, 1)

                def turn_rows(e):
                    pe.wait_ge(row_gathered, 16 * (e + 1))
                    turn(rows, row_tp)

                def bias(out_, sel, table):
                    for h in range(2):
                        pe.matmul(out_[:, h * HALF:(h + 1) * HALF], sel[:, :], table[:, h * HALF:(h + 1) * HALF],
                                  start=True, stop=False)

                def product(i, c, x_hi, x_lo, out_):
                    pe.wait_ge(lo_ready, pos(i, c) + 1)
                    s = ring(i, c, SPLIT)
                    wh = w_hi[s][:, :].rearrange("p (k h n) -> p k h n", k=KC, h=2)
                    wl = w_lo[s][:, :].rearrange("p (k h n) -> p k h n", k=KC, h=2)
                    for kk in range(KC):
                        k = (c % MCH) * KC + kk
                        for x, w in ((x_hi, wh), (x_hi, wl), (x_lo, wh)):
                            for h in range(2):
                                mm = pe.matmul(out_[:, h * HALF:(h + 1) * HALF], x[:, k, :], w[:, kk, h, :],
                                               start=False, stop=(k == KT - 1 and x is x_lo))
                    mm.then_inc(mm_done, 1)

                def gate_up(i):
                    first = isinstance(i, int) and i == 0
                    pe.wait_ge(ht_lo_ready, i + 1)
                    pe.wait_ge(sel_gu_ready, i + 1)
                    if not first:
                        pe.wait_ge(g_clipped, i)
                    bias(g_ps, sel_gu, bias_t[0])
                    for c in range(0, MCH):
                        product(i, c, ht_hi, ht_lo, g_ps)
                    if not first:
                        pe.wait_ge(act_ready, i)
                        turn(a_sb, act_tp)
                    if not (isinstance(i, int) and i < 2):
                        pe.wait_ge(y_copied, i - 1)
                    row_ids(i + 1)
                    if not first:
                        pe.wait_ge(u_clipped, i)
                    bias(u_ps, sel_gu, bias_t[1])
                    for c in range(MCH, 2 * MCH):
                        product(i, c, ht_hi, ht_lo, u_ps)

                def down(i, last):
                    pe.wait_ge(at_lo_ready, i)
                    pe.wait_ge(sel_d_ready, i)
                    pe.wait_ge(id_ready, i + 2 if not last else E + 1)
                    bias(y_ps, sel_d, bias_t[2])
                    for c in range(2 * MCH, NCH):
                        product(i, c, at_hi, at_lo, y_ps)
                        if c == 2 * MCH + 1 and not last:
                            turn_rows(i + 1)

                row_ids(0)
                turn_rows(0)
                gate_up(0)
                pe.wait_ge(ht_lo_ready, 1)
                pe.wait_ge(id_ready, 2)
                turn_rows(1)
                gate_up(1)
                down(1, False)
                with pe.Fori(2, E) as i:
                    gate_up(i)
                    down(i, False)
                pe.wait_ge(ht_lo_ready, E + 1)
                pe.wait_ge(act_ready, E)
                turn(a_sb, act_tp)
                pe.wait_ge(y_copied, E - 1)
                down(E, True)


        LOADS = (DENSE_CH + TOTAL) // SLOTS
        with ExitStack() as extra:
            def sb(name, shape, dt=F32):
                return extra.enter_context(nc.sbuf_tensor(name, shape, dt))

            rows = sb("ov_rows", [P, D])
            ht = sb("ov_ht", [P, D])
            at_ = sb("ov_at", [P, D])
            g_sb = sb("ov_g", [P, D])
            s_sb = sb("ov_s", [P, D])
            u_sb = sb("ov_u", [P, D])
            y_sb = sb("ov_y", [P, D])
            member = sb("ov_member", [P, TT, P], BF16)
            row_id = sb("ov_row_id", [P, 1], U32)
            sel = sb("ov_sel", [2 * E, P], F32R)

            ov_chain = sem("ov_chain")
            ov_member = sem("ov_member_ready")
            ov_id_mm = sem("ov_id_mm")
            ov_id = sem("ov_id")
            ov_gathered = sem("ov_gathered")
            ov_row_tp = sem("ov_row_tp")
            ov_ht = sem("ov_ht_ready")
            ov_mm = sem("ov_mm")
            ov_g = sem("ov_g_clipped")
            ov_sig = sem("ov_sig")
            ov_act = sem("ov_act_ready")
            ov_act_tp = sem("ov_act_tp")
            ov_at = sem("ov_at_ready")
            ov_copied = sem("ov_copied")
            ov_done = sem("ov_done")

            def blocks(eng, body):
                n = eng.value_load(n_ov_i[0:1, 0:1], min_val=0, max_val=MAX_OV)
                with eng.Fori(0, MAX_OV) as j:
                    with eng.If(j < n):
                        body(j)
                        eng.wait_ge(ov_done, 16 * j + 16)
                        eng.nop(nofuse=True)

            block3 = extra.enter_context(nc.Block())

            @block3.sync
            def _(sp):
                def body(j):
                    e = sp.value_load(ov_expert_i[0:1, bass.ds(j, 1)], min_val=0, max_val=E - 1)
                    for c in range(NCH):
                        if c >= SLOTS:
                            sp.wait_ge(ov_mm, NCH * j + (c - SLOTS + 1))
                        sp.dma_start(raw[c % SLOTS][:, :].rearrange("p (k n) -> p k n", k=KC),
                                     expert_src("gud"[c // MCH], e, c % MCH)).then_inc(raw_loaded[c % SLOTS], 16)
                blocks(sp, body)

            @block3.gpsimd
            def _(pool):
                def body(j):
                    pool.wait_ge(ov_id, j + 1)
                    pool.nop(nofuse=True)
                    pool.indirect_dma_start(rows[:, :], None, h2_dram,
                                            bass.IndirectOffsetOnAxis(ap=row_id[:, 0:1], axis=0))\
                        .then_inc(ov_gathered, 16)
                blocks(pool, body)

            @block3.scalar
            def _(act):
                def body(j):
                    act.wait_ge(ov_row_tp, j + 1)
                    act.activation(ht[:, :], tp_flat, ACT.Copy).then_inc(ov_ht, 1)
                    act.wait_ge(ov_g, j + 1)
                    act.activation(s_sb[:, :], g_sb[:, :], ACT.Sigmoid, scale=ALPHA).then_inc(ov_sig, 1)
                    act.wait_ge(ov_act_tp, j + 1)
                    act.activation(at_[:, :], tp_flat, ACT.Copy).then_inc(ov_at, 1)
                    act.wait_ge(ov_mm, NCH * j + NCH)
                    act.activation(y_sb[:, :], y_ps, ACT.Copy).then_inc(ov_copied, 1)
                    act.wait_ge(ov_copied, j + 1)
                    act.dma_start(y_dram[bass.ds(j * P + MAIN_ROWS, P), :], y_sb[:, :]).then_inc(ov_done, 16)
                blocks(act, body)

            @block3.vector
            def _(dve):
                CHAIN = TT * TOPK + 3

                def body(j):
                    k = 0

                    def step(ins):
                        nonlocal k
                        k += 1
                        ins.then_inc(ov_chain, 1)
                        dve.wait_ge(ov_chain, CHAIN * j + k)

                    for t in range(TT):
                        step(dve.tensor_scalar(member[:, t, :], iota_m[:, :], slot_rel[:, t, 0:1], None, ALU.is_equal))
                        for q in range(1, TOPK):
                            step(dve.scalar_tensor_tensor(out=member[:, t, :], in0=iota_m[:, :],
                                                          scalar=slot_rel[:, t, q:q + 1], in1=member[:, t, :],
                                                          op0=ALU.is_equal, op1=ALU.add))
                    step(dve.tensor_scalar(slot_rel[:, :, :], slot_rel[:, :, :], -float(P), None, ALU.add))
                    dve.tensor_scalar(sel[:, :], ov_expert[0:2 * E, bass.ds(j, 1)].to_broadcast([2 * E, P]),
                                      pmod[:, 0:1], None, ALU.is_equal).then_inc(ov_member, 1)
                    dve.wait_ge(ov_id_mm, j + 1)
                    with nc.allow_low_precision("whole numbers below 1024 are exact"):
                        dve.tensor_reduce(row_id[:, :], y_ps[:, 0:2], AX.X, ALU.add).then_inc(ov_id, 1)
                    dve.wait_ge(ov_mm, NCH * j + MCH)
                    dve.tensor_scalar(g_sb[:, :], g_ps, LIMIT, None, ALU.min).then_inc(ov_g, 1)
                    dve.wait_ge(ov_mm, NCH * j + 2 * MCH)
                    step(dve.tensor_scalar(u_sb[:, :], u_ps, LIMIT, -LIMIT, ALU.min, ALU.max))
                    dve.wait_ge(ov_sig, j + 1)
                    step(dve.tensor_tensor(g_sb[:, :], g_sb[:, :], s_sb[:, :], ALU.mult))
                    dve.scalar_tensor_tensor(out=u_sb[:, :], in0=u_sb[:, :], scalar=1.0, in1=g_sb[:, :],
                                             op0=ALU.add, op1=ALU.mult).then_inc(ov_act, 1)
                    assert k == CHAIN
                blocks(dve, body)

            @block3.tensor
            def _(pe):
                def body(j):
                    pe.wait_ge(ov_member, j + 1)
                    for t in range(TT):
                        mm = pe.matmul(y_ps[:, 0:2], member[:, t, :], tok_bf[:, t, :], start=(t == 0),
                                       stop=(t == TT - 1))
                    mm.then_inc(ov_id_mm, 1)
                    pe.wait_ge(ov_gathered, 16 * j + 16)
                    for k in range(KT):
                        mm = pe.transpose(tp_flat[:, k * P:(k + 1) * P], rows[:, k * P:(k + 1) * P], ident[:, :])
                    mm.then_inc(ov_row_tp, 1)
                    pe.wait_ge(ov_ht, j + 1)
                    for c in range(NCH):
                        m = c // MCH
                        out_, x = (g_ps, u_ps, y_ps)[m], (ht, ht, at_)[m]
                        if c == 2 * MCH:
                            pe.wait_ge(ov_act, j + 1)
                            for k in range(KT):
                                mm = pe.transpose(tp_flat[:, k * P:(k + 1) * P], u_sb[:, k * P:(k + 1) * P],
                                                  ident[:, :])
                            mm.then_inc(ov_act_tp, 1)
                            pe.wait_ge(ov_at, j + 1)
                        if c % MCH == 0:
                            for h in range(2):
                                pe.matmul(out_[:, h * HALF:(h + 1) * HALF], sel[:, :],
                                          bias_t[m][:, h * HALF:(h + 1) * HALF], start=True, stop=False)
                        pe.wait_ge(raw_loaded[c % SLOTS],
                                   j * (16 * NCH // SLOTS) + 16 * (LOADS + c // SLOTS + 1))
                        w = raw[c % SLOTS][:, :].rearrange("p (k h n) -> p k h n", k=KC, h=2)
                        for kk in range(KC):
                            k = (c % MCH) * KC + kk
                            for h in range(2):
                                mm = pe.matmul(out_[:, h * HALF:(h + 1) * HALF], x[:, k * P:(k + 1) * P],
                                               w[:, kk, h, :], start=False, stop=(k == KT - 1))
                        mm.then_inc(ov_mm, 1)
                blocks(pe, body)

        with ExitStack() as final:
            def sb(name, shape, dt=F32):
                return final.enter_context(nc.sbuf_tensor(name, shape, dt))

            picked = [[sb(f"picked{b}_{k}", [P, D]) for k in range(TOPK)] for b in range(2)]
            ffn = [sb(f"ffn{b}", [P, D]) for b in range(2)]
            fn_bc = sb("fn_bc", [P, D])
            out_sb = [sb(f"out_sb{b}", [P, D]) for b in range(2)]
            fin_ss = sb("fin_ss", [P, TT])
            fin_rstd = sb("fin_rstd", [P, TT])

            fn_loaded = sem("fn_loaded")
            picked_in = [[sem(f"picked_in{b}_{k}") for k in range(TOPK)] for b in range(2)]
            fin_step = sem("fin_step")
            g2_spread = sem("g2_spread")
            ffn_done = sem("ffn_done")
            x2_ready = sem("x2_ready")
            fin_sq = sem("fin_sq")
            fin_sqrt = sem("fin_sqrt")
            out_ready = sem("out_ready")
            out_stored = [sem(f"out_stored{b}") for b in range(2)]

            block4 = final.enter_context(nc.Block())

            @block4.sync
            def _(sp):
                sp.dma_start(fn_bc[:, :], final_norm.partition_broadcast(P)).then_inc(fn_loaded, 16)
                for t in range(TT):
                    sp.wait_ge(out_ready, t + 1)
                    dst = y_prompt[0, t * P:(t + 1) * P, :] if t < PT else y_sample.rearrange("b t d -> (b t) d")
                    sp.dma_start(dst, out_sb[t % 2][0:norm_rows(t), :]).then_inc(out_stored[t % 2], 16)
                sp.wait_ge(out_stored[0], 16 * ((TT + 1) // 2))
                sp.wait_ge(out_stored[1], 16 * (TT // 2))

            @block4.gpsimd
            def _(pool):
                for t in range(TT):
                    r = norm_rows(t)
                    if t >= 2:
                        pool.wait_ge(ffn_done, t - 1)
                    for k in range(TOPK):
                        pool.indirect_dma_start(picked[t % 2][k][0:r, :], None, y_dram,
                                                bass.IndirectOffsetOnAxis(ap=slot_i[0:r, t, k:k + 1], axis=0))\
                            .then_inc(picked_in[t % 2][k], 16)

            @block4.tensor
            def _(pe):
                for sel_, r, out_ in ((sel_p, P, g_ps), (sel_s, NS, u_ps)):
                    for h in range(2):
                        mm = pe.matmul(out_[0:r, h * HALF:(h + 1) * HALF], sel_[:, 0:r],
                                       g2_rows[:, h * HALF:(h + 1) * HALF], start=True, stop=True)
                mm.then_inc(g2_spread, 1)

            @block4.vector
            def _(dve):
                def step(ins):
                    step.n += 1
                    ins.then_inc(fin_step, 1)
                    dve.wait_ge(fin_step, step.n)
                step.n = 0
                step(dve.memset(fin_ss[:, :], 1.0))
                dve.wait_ge(g2_spread, 1)
                dve.wait_ge(fn_loaded, 16)
                for t in range(TT):
                    r = norm_rows(t)
                    f = ffn[t % 2][0:r, :]
                    if t >= 2:
                        dve.wait_ge(fin_sq, t - 1)
                    for k in range(TOPK):
                        dve.wait_ge(picked_in[t % 2][k], 16 * (t // 2 + 1))
                        y, g = picked[t % 2][k][0:r, :], gates[0:r, t, k:k + 1]
                        ins = (dve.tensor_scalar(f, y, g, None, ALU.mult) if k == 0 else
                               dve.scalar_tensor_tensor(out=f, in0=y, scalar=g, in1=f, op0=ALU.mult, op1=ALU.add))
                        if k < TOPK - 1:
                            step(ins)
                    ins.then_inc(ffn_done, 1)
                    dve.wait_ge(ffn_done, t + 1)
                    step(dve.tensor_tensor(f, f, (g_ps if t < PT else u_ps)[0:r, :], ALU.mult))
                    dve.tensor_tensor(x_sb[0:r, t, :], x_sb[0:r, t, :], f, ALU.add).then_inc(x2_ready, 1)
                    dve.wait_ge(fin_sqrt, t + 1)
                    step(dve.reciprocal(fin_rstd[0:r, t:t + 1], fin_ss[0:r, t:t + 1]))
                    if t >= 2:
                        dve.wait_ge(out_stored[t % 2], 16 * (t // 2))
                    dve.scalar_tensor_tensor(out=out_sb[t % 2][0:r, :], in0=x_sb[0:r, t, :],
                                             scalar=fin_rstd[0:r, t:t + 1], in1=fn_bc[0:r, :],
                                             op0=ALU.mult, op1=ALU.mult).then_inc(out_ready, 1)

            @block4.scalar
            def _(act):
                for t in range(TT):
                    r = norm_rows(t)
                    act.wait_ge(x2_ready, t + 1)
                    act.activation(ffn[t % 2][0:r, :], x_sb[0:r, t, :], ACT.Square,
                                   accum_out=fin_ss[0:r, t:t + 1]).then_inc(fin_sq, 1)
                    act.wait_ge(fin_sq, t + 1)
                    act.activation(fin_ss[0:r, t:t + 1], fin_ss[0:r, t:t + 1], ACT.Sqrt, bias=eps_c[0:r, 0:1],
                                   scale=1.0 / D).then_inc(fin_sqrt, 1)


_INS = ["x_prompt", "x_sample", "state_pool", "state_conv", "c_prompt", "c_sample", "norm1", "norm2",
        "w_ada", "b_ada", "w_in", "w_pool", "pool_scale", "w_conv", "w_out", "w_router", "b_router",
        "w_gate", "b_gate", "w_up", "b_up", "w_down", "b_down", "final_norm"]
_OUTS = [(1, SEQ, D), (DEC_B, DEC_T, D), (1, 1, PAST, DP), (1, 1, CPAST, DP),
         (1, DEC_B, PAST, DP), (1, DEC_B, CPAST, DP)]


def kernel(**inputs):
    import numpy as _np
    import concourse.bacc as _bacc
    from concourse import mybir as _mybir
    from concourse.bass_utils import run_bass_kernel_spmd as _run

    nc = _bacc.Bacc("TRN2", target_bir_lowering=False, num_devices=1)
    arrays, args = {}, []
    for name in _INS:
        a = _np.ascontiguousarray(inputs[name])
        arrays[f"in_{name}"] = a
        args.append(nc.dram_tensor(f"in_{name}", a.shape, _mybir.dt.from_np(a.dtype), kind="ExternalInput").ap())
    for i, shape in enumerate(_OUTS):
        args.append(nc.dram_tensor(f"out_{i}", shape, F32, kind="ExternalOutput").ap())
    hybrid_step(nc, *args)
    r = _run(nc, [arrays], core_ids=[0])
    return tuple(r.results[0][f"out_{i}"] for i in range(len(_OUTS)))
```

```python
from contextlib import ExitStack

import concourse.bass as bass
from concourse import mybir

ALU = mybir.AluOpType
ACT = mybir.ActivationFunctionType
AX = mybir.AxisListType
F32 = mybir.dt.float32
F32R = mybir.dt.float32r
BF16 = mybir.dt.bfloat16
I32 = mybir.dt.int32
U32 = mybir.dt.uint32

P = 128
D = 1024
KT = D // P
SEQ = 512
DEC_B, DEC_T = 8, 4
NS = DEC_B * DEC_T
PT = SEQ // P
TT = PT + 1
NTOK = SEQ + NS
NC = 1 + DEC_B
DP = 512
GR = DP // P
WINDOWS = (2, 4, 8, 16)
PAST = 15
CPAST = 2
E = 32
TOPK = 4
LIMIT = 7.0
ALPHA = 1.702
EPS = 1e-5
HALF = 512
CW = 256
ADA_CH = 6 * D // CW
IN_CH = 4 * DP // CW
OUT_CH = D // CW
DENSE_CH = ADA_CH + IN_CH + OUT_CH
SLOTS = 6
KC = 2
MCH = KT // KC
SPLIT = 3
SLOT_F = KC * D
MAX_OV = TOPK * NTOK // P - 1
Q = 4
QW = D // Q
PARTS = 6
SH1, SC1, G1, SH2, SC2, G2 = range(PARTS)
CPAD = P // Q
ROWS = TOPK * NTOK
SKIP = 1 << 20
EXTRA = -(-NTOK // P) - 1


def hybrid_step(nc, x_prompt, x_sample, state_pool, state_conv, c_prompt, c_sample, norm1, norm2,
                w_ada, b_ada, w_in, w_pool, pool_scale, w_conv, w_out, w_router, b_router,
                w_gate, b_gate, w_up, b_up, w_down, b_down, final_norm,
                y_prompt, y_sample, new_pool_prompt, new_conv_prompt, new_pool_sample, new_conv_sample):
    h2_dram = nc.dram_tensor("h2_rows", (NTOK, D), F32).ap()
    y_dram = nc.dram_tensor("expert_rows", (ROWS, D), F32).ap()

    top = ExitStack()
    with top:
        def sem(name):
            return top.enter_context(nc.semaphore(name))

        def keep(name, shape, dt=F32):
            return top.enter_context(nc.sbuf_tensor(name, shape, dt))

        psum = [top.enter_context(nc.psum_tensor(f"acc{i}", [P, 2, HALF], F32)) for i in range(4)]
        acc_g, acc_u, acc_y, tp = psum

        raw = [keep(f"raw{s}", [P, SLOT_F]) for s in range(SLOTS)]
        x_sb = keep("x_sb", [P, TT, D])
        mod = keep("mod", [P, PARTS * QW])
        bias_t = [keep(f"bias_{m}", [2 * E, D], F32R) for m in ("gate", "up", "down")]
        ident = keep("ident", [P, P])
        iota_m = keep("iota_m", [P, P])
        p_col = keep("p_col", [P, 1])
        rank_m = keep("rank_m", [P, TT, E + 1])
        cnt = keep("cnt", [P, E])
        start = keep("start", [P, E])
        skip = keep("skip", [P, E + 1])
        y_row = keep("y_row", [P, E])
        slot_f = keep("slot_f", [P, TT, TOPK])
        slot_i = keep("slot_i", [P, TT, TOPK], U32)
        gates = keep("gates", [P, TT, TOPK])
        tok_bf = keep("tok_bf", [P, TT, 2], BF16)
        expert_id2 = keep("expert_id2", [2 * E, E + 1])
        pmod = keep("pmod", [2 * E, 1])
        n_ov_i = keep("n_ov_i", [P, 1], I32)
        ov_expert = keep("ov_expert", [P, MAX_OV])
        ov_expert_i = keep("ov_expert_i", [P, MAX_OV], I32)
        ov_base = keep("ov_base", [P, MAX_OV])
        sel_p = keep("sel_p", [P, Q, P])
        sel_s = keep("sel_s", [P, Q, NS])
        ss = keep("ss", [P, TT])
        rstd = keep("rstd", [P, TT])
        eps_c = keep("eps_c", [P, 1])

        raw_loaded = [sem(f"raw_loaded{s}") for s in range(SLOTS)]

        part = ExitStack()

        def sb(name, shape, dt=F32):
            return part.enter_context(nc.sbuf_tensor(name, shape, dt))

        c_sg = sb("c_sg", [P, KT, NC])
        c_act = sb("c_act", [P, KT, CPAD])
        n1_rows = sb("n1_rows", [P, QW])
        n2_rows = sb("n2_rows", [P, QW])
        junk = sb("junk", [P, D])
        h_row = [sb(f"h_row{i}", [P, D]) for i in range(2)]
        h_t = sb("h_t", [P, KT, NTOK])
        mix_t = h_t
        uext = sb("uext", [P, GR, PAST + SEQ])
        uext_s = sb("uext_s", [P, GR, DEC_B, PAST + DEC_T])
        vext = sb("vext", [P, GR, CPAST + SEQ])
        vext_s = sb("vext_s", [P, GR, DEC_B, CPAST + DEC_T])
        gate_b = sb("gate_b", [P, GR, NTOK])
        gate_c = sb("gate_c", [P, GR, NTOK])
        pooled = sb("pooled", [P, GR, NTOK])
        conv = h_t[:, GR:2 * GR, :]
        wsum = [sb(f"wsum{i}", [P, PAST + SEQ]) for i in range(2)]
        g1_bc = sb("g1_bc", [P, D])
        c_rows = g1_bc[0:NC, :]
        g1_bc_s = sb("g1_bc_s", [NS, D])
        a2_bc = sb("a2_bc", [P, 2, D])
        a2_bc_s = gate_c[0:NS, :, :].rearrange("p g n -> p (g n)")[:, 0:2 * D].rearrange("p (a n) -> p a n", a=2)
        b_raw = [a2_bc[0:2 * E, 0, :], a2_bc[0:2 * E, 1, :], junk[0:2 * E, :]]
        par = sb("par", [P, 4 * GR])
        par_rows = sb("par_rows", [4 * GR, P])
        wpool_sb = sb("wpool_sb", [P, GR, P])
        wr_sb = sb("wr_sb", [P, KT, E])
        br_bc = sb("br_bc", [P, E])
        inv_n = sb("inv_n", [P, 16])
        spare = pooled[:, :, :].rearrange("p g n -> p (g n)")
        sp_rows = spare[0:DEC_B * PAST, 0:DP]
        sc_rows = spare[0:DEC_B * CPAST, DP:2 * DP]
        onehot = spare[:, 0:TT * TOPK * E].rearrange("p (t k e) -> p t k e", t=TT, k=TOPK)
        pick = spare[:, TT * TOPK * E:2 * TT * TOPK * E].rearrange("p (t k e) -> p t k e", t=TT, k=TOPK)
        ov_cmp = spare[:, 2 * TT * TOPK * E:2 * TT * TOPK * E + MAX_OV * E].rearrange("p (j e) -> p j e", e=E)
        state_o = [gate_b[0:n, i, 0:DP] for i, n in enumerate((PAST, CPAST, NS, DEC_B * CPAST))]
        u_new = gate_b[:, :, SEQ:NTOK]
        v_new = sb("v_new", [P, GR, DEC_B * CPAST])
        logit = sb("logit", [P, TT, E])
        top_v = sb("top_v", [P, TT, 8])
        top_i = sb("top_i", [P, TT, 8], U32)
        top_f = sb("top_f", [P, TT, TOPK])
        e_sum = sb("e_sum", [P, TT])
        mask_bf = sb("mask_bf", [P, TT, E], BF16)
        slot_e = sb("slot_e", [P, TT, E])
        iota_e = sb("iota_e", [P, E])
        iota_j = sb("iota_j", [P, MAX_OV])
        tri = sb("tri", [P, P], BF16)
        ones_bf = sb("ones_bf", [P, P], BF16)
        ones_e = sb("ones_e", [P, E])
        small = [sb(f"small{i}", [P, E]) for i in range(3)]

        zp = [acc_g[:, 0, :], acc_g[:, 1, :], acc_u[:, 0, :], acc_u[:, 1, :]]
        mixp = [acc_g, acc_u]
        zs = acc_y[:, 1, :].rearrange("p (f n) -> p f n", n=NS)
        modp = acc_y[:, 0, 0:QW]
        lg_p = acc_y[:, 0, 0:PT * E].rearrange("p (t e) -> p t e", e=E)
        lg_s = acc_y[0:NS, 1, 0:E]
        rank_ps = acc_y[:, 0, PT * E:(PT + TT) * E].rearrange("p (t e) -> p t e", e=E)
        cnt_ps = acc_y[:, 0, (PT + TT) * E:(PT + TT + 1) * E]
        c_ps = tp[:, 1, 0:KT * NC].rearrange("p (k r) -> p k r", r=NC)

        c_loaded = sem("c_loaded")
        x_loaded = sem("x_loaded")
        rows_loaded = sem("rows_loaded")
        small_loaded = sem("small_loaded")
        bias_loaded = sem("bias_loaded")
        pool_step = sem("pool_step")
        rows_cleared = sem("rows_cleared")
        consts = sem("consts")
        dve_step = sem("dve_step")
        act_step = sem("act_step")
        c_ready = sem("c_ready")
        ada_done = sem("ada_done")
        ada_added = sem("ada_added")
        scale_ready = sem("scale_ready")
        n1_spread = sem("n1_spread")
        n1_spread_s = sem("n1_spread_s")
        tp_full = sem("tp_full")
        tp_free = sem("tp_free")
        sq_done = sem("sq_done")
        rstd_ready = sem("rstd_ready")
        h_ready = sem("h_ready")
        z_done = sem("z_done")
        z_evac = sem("z_evac")
        v_ready = sem("v_ready")
        pooled_ready = sem("pooled_ready")
        pooled_s_ready = sem("pooled_s_ready")
        pm_done = sem("pm_done")
        pm_ready = sem("pm_ready")
        conv_ready = sem("conv_ready")
        conv_s_ready = sem("conv_s_ready")
        mix_done = sem("mix_done")
        x1_ready = sem("x1_ready")
        new_packed = sem("new_packed")
        so_ready = sem("so_ready")
        state_stored = sem("state_stored")
        h2_stored = [sem(f"h2_stored{b}") for b in range(2)]
        lg_done = sem("lg_done")
        shifted = sem("shifted")
        exp_done = sem("exp_done")
        mask_ready = sem("mask_ready")
        rank_done = sem("rank_done")
        bias_hi = sem("bias_hi")
        bias_ready = sem("bias_ready")

        TP = ["c", "par", "st"] + [f"n{t}" for t in range(TT)]
        TP += ["g1", "g1_s", "a2", "s2", "pm_s", "h0", "a2_s", "h1", "s2_s", "h2", "h3", "h4", "so0", "so1"]
        TP = {name: n for n, name in enumerate(TP)}

        def ada_chunks(part_):
            return [("ada", Q * part_ + q) for q in range(Q)]

        def in_chunks(a, b):
            return [("in", k) for k in range(a, b)]

        order = ada_chunks(SH1) + ada_chunks(SC1) + in_chunks(0, 4) + ada_chunks(G1) + in_chunks(4, 6)
        order += ada_chunks(SH2) + ada_chunks(SC2) + in_chunks(6, 7) + ada_chunks(G2) + in_chunks(7, 8)
        order += [("out", k) for k in range(OUT_CH)]
        ADA_AT = {p: n for n, p in enumerate((SH1, SC1, G1, SH2, SC2, G2))}
        IN_COL = [0, 1, 4, 5, 6, 7, 2, 3]
        at = {key: n for n, key in enumerate(order)}
        assert len(order) == DENSE_CH and DENSE_CH % SLOTS == 0

        def dense_src(kind, k):
            if kind == "out":
                return w_out[0].rearrange("(c k p) n -> c p k n", k=KC, p=P)[k]
            w, col = (w_ada[0], k) if kind == "ada" else (w_in[0], IN_COL[k])
            return w[:, col * CW:(col + 1) * CW].rearrange("(k p) n -> p k n", p=P)

        def used(n):
            kind, k = order[n]
            return {"ada": (ada_done, ADA_AT[k // Q] + 1), "in": (z_done, 2 * (k + 1)), "out": (mix_done, TT)}[kind]

        def chunk_view(n):
            return raw[n % SLOTS][:, :].rearrange("p (k n) -> p k n", k=KC if order[n][0] == "out" else KT)

        def expert_src(kind, e, c):
            w = {"g": w_gate, "u": w_up, "d": w_down}[kind]
            rows = w[0].rearrange("e (c k p) n -> e c p k n", k=KC, p=P)
            return rows[e, c] if isinstance(e, int) else rows[bass.ds(e, 1), c].rearrange("a p k n -> (a p) k n")

        FIRST_STREAM = [("g", 0, c) for c in range(MCH)] + [("u", 0, c) for c in range(MCH)]

        POOL_STEPS = 21
        CONSTS = 21

        def norm_rows(t):
            return P if t < PT else NS

        block = part.enter_context(nc.Block())

        @block.sync
        def _(sp):
            sp.dma_start(c_rows[0:1, :], c_prompt).then_inc(c_loaded, 16)
            sp.dma_start(c_rows[1:NC, :], c_sample).then_inc(c_loaded, 16)
            for n, (kind, k) in enumerate(order):
                if n >= SLOTS:
                    sp.wait_ge(*used(n - SLOTS))
                sp.dma_start(chunk_view(n), dense_src(kind, k)).then_inc(raw_loaded[n % SLOTS], 16)
                if n == SLOTS - 1:
                    sp.dma_start(x_sb[:, 0:PT, :], x_prompt[0].rearrange("(t p) d -> p t d", p=P)).then_inc(x_loaded, 16)
                    sp.dma_start(x_sb[0:NS, PT, :], x_sample.rearrange("b t d -> (b t) d")).then_inc(x_loaded, 16)

            def first(n):
                kind, e, c = FIRST_STREAM[n]
                sp.wait_ge(*used(DENSE_CH - SLOTS + n))
                sp.dma_start(raw[n][:, :].rearrange("p (k n) -> p k n", k=KC), expert_src(kind, e, c))\
                    .then_inc(raw_loaded[n], 16)

            for n in range(SLOTS - OUT_CH):
                first(n)
            for t in range(TT):
                sp.wait_ge(h_ready, TT + t + 1)
                sp.dma_start(h2_dram[t * P:t * P + norm_rows(t), :], h_row[t % 2][0:norm_rows(t), :])\
                    .then_inc(h2_stored[t % 2], 16)
            for n in range(SLOTS - OUT_CH, SLOTS):
                first(n)
            sp.wait_ge(h2_stored[0], 16 * ((TT + 1) // 2))
            sp.wait_ge(h2_stored[1], 16 * (TT // 2))
            sp.wait_ge(state_stored, 16 * (3 + DEC_B + DEC_B))

        @block.gpsimd
        def _(pool):
            def step(ins):
                step.n += 1
                ins.then_inc(pool_step, 1)
                pool.wait_ge(pool_step, step.n)
            step.n = 0
            pool.memset(mod[:, :], 0.0).then_inc(rows_cleared, 1)
            pool.memset(n1_rows[:, :], 0.0).then_inc(rows_cleared, 1)
            pool.memset(n2_rows[:, :], 0.0).then_inc(rows_cleared, 1)
            pool.memset(c_act[:, :, :], 0.0).then_inc(rows_cleared, 1)
            step(pool.memset(ident[:, :], 0.0))
            step(pool.affine_select(out=ident[:, :], in_=ident[:, :], compare_op=ALU.not_equal, fill=1.0,
                                    base=0, pattern=[[-1, P]], channel_multiplier=1))
            step(pool.memset(sel_p[:, :, :], 1.0))
            step(pool.affine_select(out=sel_p[:, :, :], in_=sel_p[:, :, :], compare_op=ALU.is_equal, fill=0.0,
                                    base=0, pattern=[[-CPAD, Q], [0, P]], channel_multiplier=1))
            step(pool.memset(sel_s[:, :, :], 1.0))
            for q in range(Q):
                v = sel_s[:, q, :].rearrange("p (s t) -> p s t", t=DEC_T)
                step(pool.affine_select(out=v, in_=v, compare_op=ALU.is_equal, fill=0.0, base=-1 - CPAD * q,
                                        pattern=[[-1, DEC_B], [0, DEC_T]], channel_multiplier=1))
            pool.memset(eps_c[:, :], EPS).then_inc(consts, 1)
            pool.memset(ss[:, :], 1.0).then_inc(consts, 1)
            for w in range(16):
                pool.memset(inv_n[:, w:w + 1], 1.0 / (w + 1)).then_inc(consts, 1)
            pool.memset(uext[:, :, 0:PAST], 0.0).then_inc(consts, 1)
            pool.memset(vext[:, :, 0:CPAST], 0.0).then_inc(consts, 1)
            pool.memset(top_v[:, :, :], 0.0).then_inc(consts, 1)
            step(pool.memset(tri[:, :], 1.0))
            step(pool.affine_select(out=tri[:, :], in_=tri[:, :], compare_op=ALU.is_gt, fill=0.0,
                                    base=0, pattern=[[1, P]], channel_multiplier=-1))
            step(pool.memset(ones_bf[:, :], 1.0))
            step(pool.memset(ones_e[:, :], 1.0))
            for out_, pat in ((iota_m, P), (iota_e, E), (iota_j, MAX_OV)):
                step(pool.iota(out_[:, :], pattern=[[1, pat]], base=0, channel_multiplier=0,
                               allow_small_or_imprecise_dtypes=True))
            step(pool.iota(p_col[:, :], pattern=[[0, 1]], base=0, channel_multiplier=1,
                           allow_small_or_imprecise_dtypes=True))
            step(pool.iota(tok_bf[:, :, 0], pattern=[[P, TT]], base=0, channel_multiplier=0,
                           allow_small_or_imprecise_dtypes=True))
            step(pool.iota(tok_bf[:, :, 1], pattern=[[0, TT]], base=0, channel_multiplier=1,
                           allow_small_or_imprecise_dtypes=True))
            step(pool.iota(expert_id2[:, :], pattern=[[1, E + 1]], base=0,
                           channel_multiplier=0, allow_small_or_imprecise_dtypes=True))
            for half in range(2):
                ins = pool.iota(pmod[half * E:(half + 1) * E, :], pattern=[[0, 1]], base=0,
                                channel_multiplier=1, allow_small_or_imprecise_dtypes=True)
                if half:
                    step(ins)
            assert step.n == POOL_STEPS, step.n

        @block.scalar
        def _(act):
            act.wait_ge(rows_cleared, 4)
            for q in range(Q):
                lo_, hi_ = q * CPAD, q * CPAD + NC
                act.dma_start(mod[lo_:hi_, :].rearrange("p (a n) -> p a n", n=QW),
                              b_ada[0].rearrange("(a q n) -> q a n", q=Q, n=QW)[q].partition_broadcast(NC))\
                    .then_inc(rows_loaded, 16)
                for rows_, nrm in ((n1_rows, norm1), (n2_rows, norm2)):
                    act.dma_start(rows_[lo_:hi_, :], nrm[0, q * QW:(q + 1) * QW].partition_broadcast(NC))\
                        .then_inc(rows_loaded, 16)
            act.dma_start(par_rows[0:GR, :], pool_scale[0].rearrange("(g p) -> g p", p=P)).then_inc(small_loaded, 16)
            act.dma_start(par_rows[GR:4 * GR, :], w_conv[0].rearrange("w (g p) -> (w g) p", p=P))\
                .then_inc(small_loaded, 16)
            act.dma_start(sp_rows, state_pool[0].rearrange("b r d -> (b r) d")).then_inc(small_loaded, 16)
            act.dma_start(sc_rows, state_conv[0].rearrange("b r d -> (b r) d")).then_inc(small_loaded, 16)
            act.dma_start(wpool_sb[:, :, :], w_pool[0].rearrange("g c d -> c g d")).then_inc(small_loaded, 16)
            act.dma_start(wr_sb[:, :, :], w_router[0].rearrange("(k p) e -> p k e", p=P)).then_inc(small_loaded, 16)
            act.dma_start(br_bc[:, :], b_router[0].partition_broadcast(P)).then_inc(small_loaded, 16)
            for s in range(DEC_B):
                act.dma_start(new_pool_sample[0, s, 0:PAST - DEC_T, :], state_pool[0, s, DEC_T:PAST, :])\
                    .then_inc(state_stored, 16)

            def empty(name, out_, in_, scale=None):
                act.wait_ge(tp_full, TP[name] + 1)
                if scale is None:
                    act.activation(out_, in_, ACT.Copy).then_inc(tp_free, 1)
                else:
                    act.activation(out_, in_, ACT.Identity, scale=scale).then_inc(tp_free, 1)

            whole = tp[:, :, :].rearrange("p b n -> p (b n)")
            act.wait_ge(tp_full, TP["c"] + 1)
            act.activation(c_sg[:, :, :], c_ps, ACT.Sigmoid).then_inc(tp_free, 1)

            def square(t, done):
                r = norm_rows(t)
                if not (done == 0 and t == 0):
                    act.wait_ge(act_step, done * TT + t)
                act.activation(junk[0:r, :], x_sb[0:r, t, :], ACT.Square,
                               accum_out=ss[0:r, t:t + 1]).then_inc(act_step, 1)

            act.wait_ge(x_loaded, 32)
            act.wait_ge(consts, 2)
            for t in range(TT):
                square(t, 0)
            act.wait_ge(act_step, TT)
            act.activation(ss[:, :], ss[:, :], ACT.Sqrt, bias=eps_c[:, 0:1], scale=1.0 / D).then_inc(sq_done, 1)
            act.wait_ge(sq_done, 1)
            for m, b in enumerate((b_gate, b_up, b_down)):
                for half in range(2):
                    act.dma_start(b_raw[m][half * E:(half + 1) * E, :], b[0]).then_inc(bias_loaded, 16)

            empty("par", par[:, :], tp[:, 0, 0:4 * GR])
            n = DEC_B * PAST
            act.wait_ge(tp_full, TP["st"] + 1)
            act.activation(uext_s[:, :, :, 0:PAST], tp[:, 0, 0:GR * n].rearrange("p (g s r) -> p g s r", g=GR, r=PAST),
                           ACT.Copy).then_inc(new_packed, 1)
            n = DEC_B * CPAST
            act.activation(vext_s[:, :, :, 0:CPAST],
                           tp[:, 1, 0:GR * n].rearrange("p (g s r) -> p g s r", g=GR, r=CPAST),
                           ACT.Copy).then_inc(new_packed, 1)
            act.wait_ge(new_packed, 2)
            act.sem_inc(tp_free, 1)

            def turned(name, t):
                r = norm_rows(t)
                empty(name, h_t[:, :, t * P:t * P + r],
                      tp[:, :, :].rearrange("p b (k n) -> p (b k) n", n=P)[:, :, 0:r])

            for t in range(TT):
                turned(f"n{t}", t)

            def leave(f, dst):
                act.wait_ge(z_done, f + 1)
                act.activation(dst, zp[f % 4], ACT.Copy).then_inc(z_evac, 1)

            for g in range(GR):
                leave(g, uext[:, g, PAST:PAST + SEQ])
            act.wait_ge(bias_loaded, 16 * 6)
            for m in range(3):
                act.activation(bias_t[m][:, :], b_raw[m], ACT.Copy).then_inc(bias_hi, 1)
            for g in range(GR):
                leave(GR + g, gate_c[:, g, 0:SEQ])
            empty("g1", g1_bc[:, :], whole)
            leave(3 * GR, gate_b[:, 0, 0:SEQ])
            leave(3 * GR + 1, gate_b[:, 1, 0:SEQ])
            empty("g1_s", g1_bc_s[:, :], whole[0:NS, :])
            leave(3 * GR + 2, gate_b[:, 2, 0:SEQ])
            leave(3 * GR + 3, gate_b[:, 3, 0:SEQ])
            act.wait_ge(bias_ready, 3)
            empty("a2", a2_bc[:, 0, :], whole)
            act.activation(uext_s[:, :, :, PAST:PAST + DEC_T],
                           zs[:, 0:GR, :].rearrange("p g (s t) -> p g s t", t=DEC_T), ACT.Copy).then_inc(z_evac, 1)
            act.activation(gate_c[:, :, SEQ:NTOK], zs[:, GR:2 * GR, :], ACT.Copy).then_inc(z_evac, 1)
            act.activation(gate_b[:, :, SEQ:NTOK], zs[:, 3 * GR:4 * GR, :], ACT.Copy).then_inc(z_evac, 1)
            for g in range(GR):
                act.wait_ge(pm_done, g + 1)
                act.activation(mix_t[:, g, 0:SEQ], zp[g], ACT.Identity, scale=par[:, g:g + 1]).then_inc(pm_ready, 1)
            empty("s2", a2_bc[:, 1, :], whole)
            act.wait_ge(tp_full, TP["pm_s"] + 1)
            for g in range(GR):
                act.activation(mix_t[:, g, SEQ:NTOK], tp[:, 0, g * NS:(g + 1) * NS], ACT.Identity,
                               scale=par[:, g:g + 1]).then_inc(pm_ready, 1)
            act.wait_ge(pm_ready, 2 * GR)
            act.sem_inc(tp_free, 1)

            for t in range(TT):
                act.wait_ge(x1_ready, t + 1)
                square(t, 1)
                r = norm_rows(t)
                act.wait_ge(act_step, TT + t + 1)
                if t == 0:
                    act.wait_ge(rstd_ready, 1)
                act.activation(ss[0:r, t:t + 1], ss[0:r, t:t + 1], ACT.Sqrt, bias=eps_c[0:r, 0:1],
                               scale=1.0 / D).then_inc(sq_done, 1)
                turned(f"h{t}", t)
                if t == 0:
                    act.wait_ge(v_ready, 2 * GR)
                    empty("a2_s", a2_bc_s[:, 0, :], whole[0:NS, :])
                if t == 1:
                    empty("s2_s", a2_bc_s[:, 1, :], whole[0:NS, :])
            act.wait_ge(shifted, 1)
            act.activation(gates[:, :, :], gates[:, :, :], ACT.Exp).then_inc(exp_done, 1)
            act.activation(u_new.rearrange("p g (s t) -> p g s t", t=DEC_T),
                           uext_s[:, :, :, PAST:PAST + DEC_T], ACT.Copy).then_inc(new_packed, 1)
            act.activation(v_new[:, :, :].rearrange("p g (s t) -> p g s t", t=CPAST),
                           vext_s[:, :, :, DEC_T:DEC_T + CPAST], ACT.Copy).then_inc(new_packed, 1)
            for i in range(4):
                n = state_o[i].shape[0]
                act.wait_ge(tp_full, TP["so0" if i < 2 else "so1"] + 1)
                act.activation(state_o[i], tp[0:n, i % 2, :], ACT.Copy).then_inc(so_ready, 1)
                if i == 1:
                    act.wait_ge(so_ready, 2)
                    act.sem_inc(tp_free, 1)
            act.wait_ge(so_ready, 4)
            act.dma_start(new_pool_prompt[0, 0], state_o[0]).then_inc(state_stored, 16)
            act.dma_start(new_conv_prompt[0, 0], state_o[1]).then_inc(state_stored, 16)
            for s in range(DEC_B):
                act.dma_start(new_pool_sample[0, s, PAST - DEC_T:PAST, :],
                              gate_b[s * DEC_T:(s + 1) * DEC_T, 2, 0:DP]).then_inc(state_stored, 16)
            act.dma_start(new_conv_sample[0].rearrange("b r d -> (b r) d"), state_o[3]).then_inc(state_stored, 16)

        @block.vector
        def _(dve):
            def step(ins):
                step.n += 1
                ins.then_inc(dve_step, 1)
                dve.wait_ge(dve_step, step.n)
            step.n = 0

            dve.wait_ge(tp_free, TP["c"] + 1)
            dve.wait_ge(rows_cleared, 4)
            dve.tensor_tensor(c_act[:, :, 0:NC], c_ps, c_sg[:, :, :], ALU.mult).then_inc(c_ready, 1)
            dve.wait_ge(rows_loaded, 16 * 3 * Q)

            def add_ada(p):
                dve.wait_ge(ada_done, ADA_AT[p] + 1)
                v = mod[:, p * QW:(p + 1) * QW]
                dve.tensor_tensor(v, v, modp, ALU.add).then_inc(ada_added, 1)

            def scale_rows(p, norm):
                dve.wait_ge(ada_added, ADA_AT[p] + 1)
                v = mod[:, p * QW:(p + 1) * QW]
                dve.scalar_tensor_tensor(out=v, in0=v, scalar=1.0, in1=norm[:, :], op0=ALU.add,
                                         op1=ALU.mult).then_inc(scale_ready, 1)

            def normalise(t, scale_, shift_, base):
                r = norm_rows(t)
                if t >= 2:
                    dve.wait_ge(tp_full, TP[("h" if base else "n") + str(t - 2)] + 1)
                    if base:
                        dve.wait_ge(h2_stored[t % 2], 16 * (t // 2))
                h = h_row[t % 2][0:r, :]
                step(dve.scalar_tensor_tensor(out=h, in0=x_sb[0:r, t, :], scalar=rstd[0:r, t:t + 1],
                                              in1=scale_, op0=ALU.mult, op1=ALU.mult))
                dve.tensor_tensor(h, h, shift_, ALU.add).then_inc(h_ready, 1)

            add_ada(SH1)
            add_ada(SC1)
            scale_rows(SC1, n1_rows)
            dve.wait_ge(sq_done, 1)
            dve.reciprocal(rstd[:, :], ss[:, :]).then_inc(rstd_ready, 1)
            dve.wait_ge(rstd_ready, 1)
            for t in range(TT):
                r = norm_rows(t)
                dve.wait_ge(n1_spread if t < PT else n1_spread_s, 1)
                normalise(t, acc_g[0:r, :, :].rearrange("p b n -> p (b n)"),
                          acc_u[0:r, :, :].rearrange("p b n -> p (b n)"), 0)

            def windows(src_, n, ext, buf):
                cur, w, i = src_, 1, 0
                while w < n:
                    o = buf[i % 2]
                    step(dve.tensor_tensor(o[..., 2 * w - 1:ext], cur[..., 2 * w - 1:ext],
                                           cur[..., w - 1:ext - w], ALU.add))
                    cur, w, i = o, 2 * w, i + 1
                return cur

            dve.wait_ge(consts, CONSTS)
            dve.wait_ge(tp_free, TP["st"] + 1)
            for g, w in enumerate(WINDOWS):
                dve.wait_ge(z_evac, g + 1)
                s = windows(uext[:, g, :], w, PAST + SEQ, [wsum[0][:, :], wsum[1][:, :]])
                step(dve.scalar_tensor_tensor(out=pooled[:, g, w - 1:SEQ], in0=s[:, PAST + w - 1:PAST + SEQ],
                                              scalar=1.0 / w, in1=uext[:, g, PAST + w - 1:PAST + SEQ],
                                              op0=ALU.mult, op1=ALU.subtract))
                step(dve.tensor_tensor(s[:, PAST:PAST + w - 1], s[:, PAST:PAST + w - 1], inv_n[:, 0:w - 1], ALU.mult))
                dve.tensor_tensor(pooled[:, g, 0:w - 1], s[:, PAST:PAST + w - 1], uext[:, g, PAST:PAST + w - 1],
                                  ALU.subtract).then_inc(pooled_ready, 1)
                dve.wait_ge(pooled_ready, g + 1)
            dve.wait_ge(bias_hi, 3)
            for m in range(3):
                dve.tensor_tensor(bias_t[m][E:2 * E, :], b_raw[m][E:2 * E, :],
                                  bias_t[m][E:2 * E, :].bitcast(F32), ALU.subtract).then_inc(bias_ready, 1)
            add_ada(G1)
            for g in range(GR):
                f = 2 * GR + g
                dve.wait_ge(z_done, f + 1)
                dve.wait_ge(z_evac, 2 * GR)
                dve.tensor_tensor(vext[:, g, CPAST:CPAST + SEQ], zp[f % 4], gate_c[:, g, 0:SEQ], ALU.mult)\
                    .then_inc(v_ready, 1)
            add_ada(SH2)
            add_ada(SC2)
            scale_rows(SC2, n2_rows)

            def taps(v, y, b, g, ready):
                n = y.shape[-1]
                tap = [par[:, (1 + j) * GR + g:(1 + j) * GR + g + 1] for j in range(3)]
                step(dve.tensor_scalar(y, v[..., 0:n], tap[0], None, ALU.mult))
                step(dve.scalar_tensor_tensor(out=y, in0=v[..., 1:1 + n], scalar=tap[1], in1=y,
                                              op0=ALU.mult, op1=ALU.add))
                step(dve.scalar_tensor_tensor(out=y, in0=v[..., 2:2 + n], scalar=tap[2], in1=y,
                                              op0=ALU.mult, op1=ALU.add))
                if b is not None:
                    dve.tensor_tensor(y, y, b, ALU.mult).then_inc(ready, 1)

            add_ada(G2)
            dve.wait_ge(z_done, 4 * GR)
            dve.wait_ge(v_ready, GR)
            for g in range(GR):
                dve.wait_ge(z_evac, 2 * GR + g + 1)
                taps(vext[:, g, :], conv[:, g, 0:SEQ], gate_b[:, g, 0:SEQ], g, conv_ready)
            dve.wait_ge(z_evac, 3 * GR + 3)
            for g in range(GR):
                dve.tensor_tensor(vext_s[:, g, :, CPAST:CPAST + DEC_T],
                                  zs[:, 2 * GR + g, :].rearrange("p (s t) -> p s t", t=DEC_T),
                                  gate_c[:, g, SEQ:NTOK].rearrange("p (s t) -> p s t", t=DEC_T),
                                  ALU.mult).then_inc(v_ready, 1)
            bufs = [b[:, 0:DEC_B * (PAST + DEC_T)].rearrange("p (s r) -> p s r", s=DEC_B) for b in wsum]
            for g, w in enumerate(WINDOWS):
                s = windows(uext_s[:, g, :, :], w, PAST + DEC_T, bufs)
                dve.scalar_tensor_tensor(out=pooled[:, g, SEQ:NTOK].rearrange("p (s t) -> p s t", t=DEC_T),
                                         in0=s[:, :, PAST:PAST + DEC_T], scalar=1.0 / w,
                                         in1=uext_s[:, g, :, PAST:PAST + DEC_T],
                                         op0=ALU.mult, op1=ALU.subtract).then_inc(pooled_s_ready, 1)
                dve.wait_ge(pooled_s_ready, g + 1)
            dve.wait_ge(v_ready, 2 * GR)

            def by_seq(t_):
                return t_.rearrange("p (s t) -> p s t", t=DEC_T)

            for g in range(GR):
                taps(vext_s[:, g, :, :], by_seq(conv[:, g, SEQ:NTOK]), by_seq(gate_b[:, g, SEQ:NTOK]), g, conv_s_ready)

            def best(t, src_):
                r = norm_rows(t)
                step(dve.tensor_tensor(logit[0:r, t, :], src_, br_bc[0:r, :], ALU.add))
                step(dve.max(top_v[0:r, t, :], logit[0:r, t, :]))
                step(dve.max_index(top_i[0:r, t, :], top_v[0:r, t, :], logit[0:r, t, :]))
                step(dve.tensor_copy(top_f[0:r, t, :], top_i[0:r, t, 0:TOPK]))
                step(dve.tensor_tensor(onehot[0:r, t, :, :], iota_e[0:r, :].unsqueeze(1).to_broadcast([r, TOPK, E]),
                                       top_f[0:r, t, :].unsqueeze(2).to_broadcast([r, TOPK, E]), ALU.is_equal))
                with nc.allow_low_precision("zeros and ones are exact"):
                    step(dve.tensor_reduce(mask_bf[0:r, t, :], onehot[0:r, t, :, :].rearrange("p k e -> p e k"),
                                           AX.X, ALU.add))

            dve.wait_ge(tp_free, TP["s2"] + 1)
            for t in range(TT):
                r = norm_rows(t)
                dve.wait_ge(mix_done, t + 1)
                g1 = (g1_bc if t < PT else g1_bc_s)[0:r, :]
                m = mixp[t % 2][0:r, :, :].rearrange("p b n -> p (b n)")
                h = h_row[t % 2][0:r, :]
                if t >= 2:
                    dve.wait_ge(tp_full, TP[f"h{t - 2}"] + 1)
                    dve.wait_ge(h2_stored[t % 2], 16 * (t // 2))
                step(dve.tensor_tensor(h, m, g1, ALU.mult))
                dve.tensor_tensor(x_sb[0:r, t, :], x_sb[0:r, t, :], h, ALU.add).then_inc(x1_ready, 1)
                if t == PT:
                    dve.wait_ge(lg_done, PT)
                    dve.wait_ge(pool_step, POOL_STEPS)
                    dve.wait_ge(pm_ready, 2 * GR)
                    step(dve.memset(onehot[:, PT, :, :], 0.0))
                    step(dve.memset(mask_bf[:, PT, :], 0.0))
                    for b in range(PT):
                        best(b, lg_p[:, b, :])
                dve.wait_ge(sq_done, t + 2)
                step(dve.reciprocal(rstd[0:r, t:t + 1], ss[0:r, t:t + 1]))
                if t == PT:
                    dve.wait_ge(tp_free, TP["s2_s"] + 1)
                sc = a2_bc if t < PT else a2_bc_s
                normalise(t, sc[0:r, 0, :], sc[0:r, 1, :], 1)

            dve.wait_ge(lg_done, TT)
            best(PT, lg_s)
            dve.tensor_tensor(gates[:, :, :], top_v[:, :, 0:TOPK], top_v[:, :, 0:1].to_broadcast([P, TT, TOPK]),
                              ALU.subtract).then_inc(shifted, 1)
            dve.sem_inc(mask_ready, 1)

            dve.wait_ge(rank_done, 1)
            step(dve.memset(rank_m[:, :, E:E + 1], -1.0))
            step(dve.scalar_tensor_tensor(out=slot_e[:, :, :], in0=rank_ps, scalar=1.0, in1=mask_bf[:, :, :],
                                          op0=ALU.add, op1=ALU.mult))
            step(dve.tensor_scalar(rank_m[:, :, 0:E], slot_e[:, :, :], -1.0, None, ALU.add))
            step(dve.tensor_copy(cnt[:, :], cnt_ps))
            incl, nb, ov_incl = [t_[:, :] for t_ in small]
            step(dve.tensor_tensor_scan(incl, ones_e[:, :], cnt[:, :], 0.0, ALU.mult, ALU.add))
            step(dve.tensor_tensor(start[:, :], incl, cnt[:, :], ALU.subtract))
            step(dve.tensor_scalar(skip[:, 0:E], cnt[:, :], p_col[:, 0:1], float(SKIP), ALU.is_le, ALU.mult))
            step(dve.memset(skip[:, E:E + 1], float(SKIP)))
            step(dve.scalar_tensor_tensor(out=y_row[:, :], in0=start[:, :], scalar=p_col[:, 0:1], in1=skip[:, 0:E],
                                          op0=ALU.add, op1=ALU.add))
            step(dve.tensor_tensor(slot_e[:, :, :], rank_ps, start[:, :].unsqueeze(1).to_broadcast([P, TT, E]),
                                   ALU.add))
            step(dve.tensor_tensor(pick, onehot, slot_e[:, :, :].unsqueeze(2).to_broadcast([P, TT, TOPK, E]),
                                   ALU.mult))
            step(dve.tensor_reduce(slot_f[:, :, :], pick, AX.X, ALU.add))
            step(dve.tensor_copy(slot_i[:, :, :], slot_f[:, :, :]))
            step(dve.tensor_scalar(nb, cnt[:, :], float(P), None, ALU.is_gt))
            for k in range(2, EXTRA + 1):
                step(dve.scalar_tensor_tensor(out=nb, in0=cnt[:, :], scalar=float(k * P), in1=nb,
                                              op0=ALU.is_gt, op1=ALU.add))
            step(dve.tensor_tensor_scan(ov_incl, ones_e[:, :], nb, 0.0, ALU.mult, ALU.add))
            step(dve.tensor_copy(n_ov_i[:, :], ov_incl[:, E - 1:E]))
            step(dve.tensor_tensor(ov_cmp, ov_incl.unsqueeze(1).to_broadcast([P, MAX_OV, E]),
                                   iota_j[:, :].unsqueeze(2).to_broadcast([P, MAX_OV, E]), ALU.is_le))
            step(dve.tensor_reduce(ov_expert[:, :], ov_cmp, AX.X, ALU.add))
            step(dve.tensor_scalar(ov_expert[:, :], ov_expert[:, :], float(E - 1), None, ALU.min))
            step(dve.tensor_copy(ov_expert_i[:, :], ov_expert[:, :]))
            step(dve.tensor_tensor(ov_cmp, ov_cmp, nb.unsqueeze(1).to_broadcast([P, MAX_OV, E]), ALU.mult))
            step(dve.tensor_reduce(ov_base[:, :], ov_cmp, AX.X, ALU.add))
            step(dve.tensor_tensor(ov_base[:, :], iota_j[:, :], ov_base[:, :], ALU.subtract))
            step(dve.tensor_scalar(ov_base[:, :], ov_base[:, :], 1.0, float(P), ALU.add, ALU.mult))
            dve.wait_ge(exp_done, 1)
            step(dve.tensor_reduce(e_sum[:, :], gates[:, :, :], AX.X, ALU.add))
            step(dve.reciprocal(e_sum[:, :], e_sum[:, :]))
            step(dve.tensor_tensor(gates[:, :, :], gates[:, :, :],
                                   e_sum[:, :].unsqueeze(2).to_broadcast([P, TT, TOPK]), ALU.mult))

        @block.tensor
        def _(pe):
            def chunk(kind, k):
                n = at[(kind, k)]
                pe.wait_ge(raw_loaded[n % SLOTS], 16 * (n // SLOTS + 1))
                return chunk_view(n)

            def ada(p):
                w = [chunk("ada", Q * p + q) for q in range(Q)]
                if ADA_AT[p]:
                    pe.wait_ge(ada_added, ADA_AT[p])
                for k in range(KT):
                    for q in range(Q):
                        mm = pe.matmul(modp[q * CPAD:(q + 1) * CPAD, :], c_act[:, k, :], w[q][:, k, :],
                                       start=(k == 0), stop=(k == KT - 1))
                mm.then_inc(ada_done, 1)

            def spread(samples, p, dst):
                sel, r = (sel_s, NS) if samples else (sel_p, P)
                for q in range(Q):
                    mm = pe.matmul(dst[0:r, q // 2, (q % 2) * QW:(q % 2 + 1) * QW], sel[:, q, :],
                                   mod[:, p * QW:(p + 1) * QW], start=True, stop=True)
                return mm

            def take(name):
                if TP[name]:
                    pe.wait_ge(tp_free, TP[name])

            def transposes(name, t, base):
                take(name)
                pe.wait_ge(h_ready, base + t + 1)
                r = norm_rows(t)
                for k in range(KT):
                    mm = pe.transpose(tp[:, k // 4, (k % 4) * P:(k % 4) * P + r],
                                      h_row[t % 2][0:r, k * P:(k + 1) * P], ident[0:r, 0:r])
                mm.then_inc(tp_full, 1)

            pe.wait_ge(c_loaded, 32)
            pe.wait_ge(pool_step, 2)
            for k in range(KT):
                mm = pe.transpose(c_ps[:, k, :], c_rows[:, k * P:(k + 1) * P], ident[0:NC, 0:NC])
            mm.then_inc(tp_full, 1)
            pe.wait_ge(c_ready, 1)
            ada(SH1)
            pe.wait_ge(small_loaded, 16 * 7)
            take("par")
            pe.transpose(tp[:, 0, 0:4 * GR], par_rows[:, :], ident[0:4 * GR, 0:4 * GR]).then_inc(tp_full, 1)
            ada(SC1)
            take("st")
            for g in range(GR):
                n = DEC_B * PAST
                pe.transpose(tp[:, 0, g * n:(g + 1) * n], sp_rows[:, g * P:(g + 1) * P], ident[0:n, 0:n])
            for g in range(GR):
                n = DEC_B * CPAST
                mm = pe.transpose(tp[:, 1, g * n:(g + 1) * n], sc_rows[:, g * P:(g + 1) * P], ident[0:n, 0:n])
            mm.then_inc(tp_full, 1)
            pe.wait_ge(scale_ready, 1)
            pe.wait_ge(pool_step, 9)
            spread(False, SC1, acc_g)
            spread(False, SH1, acc_u).then_inc(n1_spread, 1)
            for t in range(TT):
                if t == PT:
                    pe.wait_ge(h_ready, PT)
                    spread(True, SC1, acc_g)
                    spread(True, SH1, acc_u).then_inc(n1_spread_s, 1)
                transposes(f"n{t}", t, 0)
            pe.wait_ge(tp_free, TP[f"n{PT}"] + 1)

            def project(k):
                w = chunk("in", k)
                for f in (2 * k, 2 * k + 1):
                    if 4 <= f < 3 * GR:
                        pe.wait_ge(z_evac, f - 3)
                    elif f >= 3 * GR:
                        pe.wait_ge(v_ready, f - 3 * GR + 1)
                    for out_, rhs in ((zp[f % 4], h_t[:, :, 0:SEQ]), (zs[:, f, :], h_t[:, :, SEQ:NTOK])):
                        for j in range(KT):
                            mm = pe.matmul(out_, w[:, j, (f % 2) * P:(f % 2 + 1) * P], rhs[:, j, :],
                                           start=(j == 0), stop=(j == KT - 1))
                    mm.then_inc(z_done, 1)

            for k in range(4):
                project(k)
            ada(G1)
            project(4)
            project(5)
            ada(SH2)
            ada(SC2)
            take("g1")
            spread(False, G1, tp).then_inc(tp_full, 1)
            project(6)
            take("g1_s")
            spread(True, G1, tp).then_inc(tp_full, 1)
            ada(G2)
            project(7)
            take("a2")
            pe.wait_ge(scale_ready, 2)
            spread(False, SC2, tp).then_inc(tp_full, 1)
            pe.wait_ge(pooled_ready, GR)
            for g in range(GR):
                pe.wait_ge(z_evac, 2 * GR + g + 1)
                pe.matmul(zp[g], wpool_sb[:, g, :], pooled[:, g, 0:SEQ], start=True, stop=True).then_inc(pm_done, 1)
            take("s2")
            spread(False, SH2, tp).then_inc(tp_full, 1)

            def mix(t):
                r, out_ = norm_rows(t), mixp[t % 2]
                if t >= 2:
                    pe.wait_ge(x1_ready, t - 1)
                for j in list(range(GR, 2 * GR)) + list(range(GR)):
                    w = chunk("out", j // KC)
                    for h in range(2):
                        mm = pe.matmul(out_[0:r, h, :], mix_t[:, j, t * P:t * P + r],
                                       w[:, j % KC, h * HALF:(h + 1) * HALF], start=(j == GR), stop=(j == GR - 1))
                mm.then_inc(mix_done, 1)

            def router(t):
                r = norm_rows(t)
                pe.wait_ge(tp_free, TP[f"h{t}"] + 1)
                out_ = lg_p[:, t, :] if t < PT else lg_s
                for k in range(KT):
                    mm = pe.matmul(out_, h_t[:, k, t * P:t * P + r], wr_sb[:, k, :],
                                   start=(k == 0), stop=(k == KT - 1))
                mm.then_inc(lg_done, 1)

            pe.wait_ge(pm_ready, GR)
            pe.wait_ge(conv_ready, GR)
            mix(0)
            take("pm_s")
            pe.wait_ge(pooled_s_ready, GR)
            for g in range(GR):
                mm = pe.matmul(tp[:, 0, g * NS:(g + 1) * NS], wpool_sb[:, g, :], pooled[:, g, SEQ:NTOK],
                               start=True, stop=True)
            mm.then_inc(tp_full, 1)
            mix(1)
            pe.wait_ge(ada_added, PARTS)
            transposes("h0", 0, TT)
            router(0)
            take("a2_s")
            spread(True, SC2, tp).then_inc(tp_full, 1)
            mix(2)
            transposes("h1", 1, TT)
            router(1)
            take("s2_s")
            spread(True, SH2, tp).then_inc(tp_full, 1)
            mix(3)
            transposes("h2", 2, TT)
            router(2)
            pe.wait_ge(pm_ready, 2 * GR)
            pe.wait_ge(conv_s_ready, GR)
            mix(4)
            transposes("h3", 3, TT)
            router(3)
            transposes("h4", 4, TT)
            router(4)
            pe.wait_ge(mask_ready, 1)
            for t in range(TT):
                pe.matmul(rank_ps[:, t, :], tri[:, :], mask_bf[:, t, :], start=True, stop=(t == 0))
                for b in range(t):
                    pe.matmul(rank_ps[:, t, :], ones_bf[:, :], mask_bf[:, b, :], start=False, stop=(b == t - 1))
            for t in range(TT):
                mm = pe.matmul(cnt_ps, ones_bf[:, :], mask_bf[:, t, :], start=(t == 0), stop=(t == TT - 1))
            mm.then_inc(rank_done, 1)
            take("so0")
            for g in range(GR):
                pe.transpose(tp[0:PAST, 0, g * P:(g + 1) * P], uext[:, g, SEQ:SEQ + PAST], ident[:, :])
            for g in range(GR):
                mm = pe.transpose(tp[0:CPAST, 1, g * P:(g + 1) * P], vext[:, g, SEQ:SEQ + CPAST], ident[:, :])
            mm.then_inc(tp_full, 1)
            pe.wait_ge(new_packed, 4)
            take("so1")
            for g in range(GR):
                pe.transpose(tp[0:NS, 0, g * P:(g + 1) * P], u_new[:, g, :], ident[:, :])
            for g in range(GR):
                mm = pe.transpose(tp[0:DEC_B * CPAST, 1, g * P:(g + 1) * P], v_new[:, g, :], ident[:, :])
            mm.then_inc(tp_full, 1)

        part.close()

        NCH = 3 * MCH
        TOTAL = E * NCH

        def pos(i, c):
            if isinstance(i, int) and i == 0:
                return c
            if isinstance(i, int) and i == E:
                return NCH * E - MCH + c - 2 * MCH
            return i * NCH + (c - MCH)

        def ring(i, c, n):
            return (pos(i, c) if isinstance(i, int) else pos(1, c)) % n

        assert NCH % SLOTS == 0 and NCH % SPLIT == 0

        def loaded_value(i, c):
            if isinstance(i, int):
                return 16 * ((DENSE_CH + pos(i, c)) // SLOTS + 1)
            base = (DENSE_CH + pos(1, c)) // SLOTS + 1
            return (i - 1) * (16 * NCH // SLOTS) + 16 * base

        with ExitStack() as experts:
            def sb(name, shape, dt=F32):
                return experts.enter_context(nc.sbuf_tensor(name, shape, dt))

            w_hi = [sb(f"w_hi{s}", [P, SLOT_F], F32R) for s in range(SPLIT)]
            w_lo = [sb(f"w_lo{s}", [P, SLOT_F], F32R) for s in range(SPLIT)]
            rows = sb("rows", [P, D])
            ht_hi = sb("ht_hi", [P, KT, P], F32R)
            ht_lo = sb("ht_lo", [P, KT, P], F32R)
            at_hi = sb("at_hi", [P, KT, P], F32R)
            at_lo = sb("at_lo", [P, KT, P], F32R)
            g_sb = sb("g_sb", [P, D])
            s_sb = sb("s_sb", [P, D])
            u_sb = sb("u_sb", [P, D])
            a_sb = sb("a_sb", [P, D])
            y_sb = sb("y_sb", [P, D])
            member = sb("member", [P, TT, P], BF16)
            row_id = sb("row_id", [P, 1], U32)
            y_idx = sb("y_idx", [P, 1], U32)
            sel_gu = sb("sel_gu", [2 * E, P], F32R)
            sel_d = sb("sel_d", [2 * E, P], F32R)

            hi_ready = sem("hi_ready")
            lo_ready = sem("lo_ready")
            mm_done = sem("mm_done")
            member_ready = sem("member_ready")
            id_done = sem("id_done")
            id_ready = sem("id_ready")
            row_gathered = sem("row_gathered")
            row_tp = sem("row_tp")
            ht_hi_ready = sem("ht_hi_ready")
            ht_lo_ready = sem("ht_lo_ready")
            g_clipped = sem("g_clipped")
            sig_done = sem("sig_done")
            u_clipped = sem("u_clipped")
            glu_done = sem("glu_done")
            act_ready = sem("act_ready")
            act_tp = sem("act_tp")
            at_hi_ready = sem("at_hi_ready")
            at_lo_ready = sem("at_lo_ready")
            sel_gu_ready = sem("sel_gu_ready")
            sel_d_ready = sem("sel_d_ready")
            y_idx_ready = sem("y_idx_ready")
            y_copied = sem("y_copied")
            rows_filled = sem("rows_filled")
            y_stored = sem("y_stored")

            flat = lambda t: t[:, :, :].rearrange("p b n -> p (b n)")
            tp_flat, g_ps, u_ps, y_ps = flat(tp), flat(acc_g), flat(acc_u), flat(acc_y)

            block2 = experts.enter_context(nc.Block())

            @block2.sync
            def _(sp):
                def load(i, c):
                    n = pos(i, c)
                    s = ring(i, c, SLOTS)
                    kind = "gud"[c // MCH]
                    sp.wait_ge(lo_ready, n - (SLOTS - 1))
                    sp.dma_start(raw[s][:, :].rearrange("p (k n) -> p k n", k=KC),
                                 expert_src(kind, i - (kind == "d"), c % MCH)).then_inc(raw_loaded[s], 16)

                for c in range(SLOTS, 2 * MCH):
                    load(0, c)
                with sp.Fori(1, E) as i:
                    for c in range(NCH):
                        load(i, c)
                for c in range(2 * MCH, NCH):
                    load(E, c)

            @block2.gpsimd
            def _(pool):
                pool.memset(rows[:, :], 0.0).then_inc(rows_filled, 1)
                pool.wait_ge(rows_filled, 1)

                def gather(e):
                    pool.wait_ge(id_ready, e + 1)
                    if not isinstance(e, int):
                        pool.wait_ge(row_tp, e)
                        pool.nop(nofuse=True)
                    pool.indirect_dma_start(rows[:, :], None, h2_dram,
                                            bass.IndirectOffsetOnAxis(ap=row_id[:, 0:1], axis=0),
                                            bounds_check=NTOK - 1, oob_is_err=False).then_inc(row_gathered, 16)

                def scatter(e):
                    pool.wait_ge(y_copied, e + 1)
                    pool.wait_ge(y_idx_ready, e + 1)
                    if not isinstance(e, int):
                        pool.nop(nofuse=True)
                    pool.indirect_dma_start(y_dram, bass.IndirectOffsetOnAxis(ap=y_idx[:, 0:1], axis=0),
                                            y_sb[:, :], None, bounds_check=ROWS - 1, oob_is_err=False)\
                        .then_inc(y_stored, 16)

                for e in range(3):
                    gather(e)
                with pool.Fori(3, E + 1) as e:
                    scatter(e - 3)
                    gather(e)
                scatter(E - 2)
                scatter(E - 1)

            @block2.scalar
            def _(act):
                def hi(i, c):
                    n = pos(i, c)
                    act.wait_ge(raw_loaded[ring(i, c, SLOTS)], loaded_value(i, c))
                    if not isinstance(n, int) or n >= SPLIT:
                        act.wait_ge(mm_done, n - (SPLIT - 1))
                    act.activation(w_hi[ring(i, c, SPLIT)][:, :], raw[ring(i, c, SLOTS)][:, :], ACT.Copy)\
                        .then_inc(hi_ready, 1)

                def y_out(e):
                    act.wait_ge(mm_done, pos(e + 2, 0) if not (isinstance(e, int) and e >= E - 2) else
                                NCH * (e + 2) - MCH if e == E - 2 else TOTAL)
                    if not (isinstance(e, int) and e == 0):
                        act.wait_ge(y_stored, 16 * e)
                    act.activation(y_sb[:, :], y_ps, ACT.Copy).then_inc(y_copied, 1)
                    col = y_row[:, e:e + 1] if isinstance(e, int) else y_row[:, bass.ds(e, 1)]
                    act.activation(y_idx[:, :], col, ACT.Copy).then_inc(y_idx_ready, 1)

                def turn_hi(e):
                    act.wait_ge(row_tp, e + 1)
                    act.activation(flat(ht_hi), tp_flat, ACT.Copy).then_inc(ht_hi_ready, 1)

                def act_hi(e):
                    act.wait_ge(act_tp, e + 1)
                    act.activation(flat(at_hi), tp_flat, ACT.Copy).then_inc(at_hi_ready, 1)

                def sigmoid(e):
                    act.wait_ge(g_clipped, e + 1)
                    act.activation(s_sb[:, :], g_sb[:, :], ACT.Sigmoid, scale=ALPHA).then_inc(sig_done, 1)

                def step(i):
                    first = isinstance(i, int) and i == 0
                    for c in range(6):
                        hi(i, c)
                        if c == 1 and not (isinstance(i, int) and i < 2):
                            y_out(i - 2)
                    if not first:
                        act_hi(i - 1)
                    hi(i, 6)
                    sigmoid(i)
                    hi(i, 7)
                    if not first:
                        for c in range(8, NCH):
                            hi(i, c)
                    turn_hi(i + 1)

                turn_hi(0)
                step(0)
                step(1)
                step(2)
                with act.Fori(3, E) as i:
                    step(i)
                hi(E, 8)
                hi(E, 9)
                y_out(E - 2)
                act_hi(E - 1)
                hi(E, 10)
                hi(E, 11)
                y_out(E - 1)
                act.wait_ge(y_stored, 16 * E)

            @block2.vector
            def _(dve):
                def lo(i, c):
                    dve.wait_ge(hi_ready, pos(i, c) + 1)
                    s = ring(i, c, SPLIT)
                    dve.tensor_tensor(w_lo[s][:, :], raw[ring(i, c, SLOTS)][:, :], w_hi[s][:, :].bitcast(F32),
                                      ALU.subtract).then_inc(lo_ready, 1)

                def members(e):
                    if not (isinstance(e, int) and e == 0):
                        dve.wait_ge(id_done, e)
                    col = rank_m[:, :, e:e + 1] if isinstance(e, int) else rank_m[:, :, bass.ds(e, 1)]
                    dve.tensor_tensor(member[:, :, :], iota_m[:, :].unsqueeze(1).to_broadcast([P, TT, P]),
                                      col.to_broadcast([P, TT, P]), ALU.is_equal).then_inc(member_ready, 1)

                def ids(e):
                    dve.wait_ge(id_done, e + 1)
                    if not (isinstance(e, int) and e == 0):
                        dve.wait_ge(row_gathered, 16 * e)
                    col = skip[:, e:e + 1] if isinstance(e, int) else skip[:, bass.ds(e, 1)]
                    dve.scalar_tensor_tensor(out=row_id[:, :], in0=y_ps[:, 0:1], scalar=y_ps[:, 1:2], in1=col,
                                             op0=ALU.add, op1=ALU.add).then_inc(id_ready, 1)

                def select(out_, e, done):
                    col = expert_id2[:, e:e + 1] if isinstance(e, int) else expert_id2[:, bass.ds(e, 1)]
                    dve.tensor_scalar(out_[:, :], col.to_broadcast([2 * E, P]), pmod[:, 0:1], None, ALU.is_equal)\
                        .then_inc(done, 1)

                def turn_lo(e):
                    dve.wait_ge(ht_hi_ready, e + 1)
                    dve.tensor_tensor(flat(ht_lo), tp_flat, flat(ht_hi).bitcast(F32), ALU.subtract)\
                        .then_inc(ht_lo_ready, 1)

                def act_lo(e):
                    dve.wait_ge(at_hi_ready, e + 1)
                    dve.tensor_tensor(flat(at_lo), tp_flat, flat(at_hi).bitcast(F32), ALU.subtract)\
                        .then_inc(at_lo_ready, 1)
                    select(sel_d, e, sel_d_ready)

                def step(i):
                    first = isinstance(i, int) and i == 0
                    lo(i, 0)
                    members(i + 1)
                    for c in range(1, 6):
                        lo(i, c)
                    if not first:
                        act_lo(i - 1)
                    dve.wait_ge(mm_done, pos(i, 3) + 1)
                    if not first:
                        dve.wait_ge(glu_done, i)
                    dve.tensor_scalar(g_sb[:, :], g_ps, LIMIT, None, ALU.min).then_inc(g_clipped, 1)
                    ids(i + 1)
                    lo(i, 6)
                    lo(i, 7)
                    if not first:
                        lo(i, 8)
                        lo(i, 9)
                    dve.wait_ge(mm_done, pos(i, 7) + 1)
                    if not first:
                        dve.wait_ge(act_ready, i)
                    dve.tensor_scalar(u_sb[:, :], u_ps, LIMIT, -LIMIT, ALU.min, ALU.max).then_inc(u_clipped, 1)
                    if not first:
                        lo(i, 10)
                    dve.wait_ge(sig_done, i + 1)
                    dve.tensor_tensor(g_sb[:, :], g_sb[:, :], s_sb[:, :], ALU.mult).then_inc(glu_done, 1)
                    select(sel_gu, i + 1, sel_gu_ready)
                    dve.wait_ge(glu_done, i + 1)
                    dve.wait_ge(u_clipped, i + 1)
                    dve.scalar_tensor_tensor(out=a_sb[:, :], in0=u_sb[:, :], scalar=1.0, in1=g_sb[:, :],
                                             op0=ALU.add, op1=ALU.mult).then_inc(act_ready, 1)
                    if not first:
                        lo(i, 11)
                    turn_lo(i + 1)

                members(0)
                select(sel_gu, 0, sel_gu_ready)
                ids(0)
                turn_lo(0)
                step(0)
                with dve.Fori(1, E) as i:
                    step(i)
                lo(E, 8)
                lo(E, 9)
                act_lo(E - 1)
                lo(E, 10)
                lo(E, 11)

            @block2.tensor
            def _(pe):
                def row_ids(e):
                    pe.wait_ge(member_ready, e + 1)
                    for t in range(TT):
                        mm = pe.matmul(y_ps[:, 0:2], member[:, t, :], tok_bf[:, t, :], start=(t == 0),
                                       stop=(t == TT - 1))
                    mm.then_inc(id_done, 1)

                def turn(src_, done):
                    for k in range(KT):
                        mm = pe.transpose(tp_flat[:, k * P:(k + 1) * P], src_[:, k * P:(k + 1) * P], ident[:, :])
                    mm.then_inc(done, 1)

                def turn_rows(e):
                    pe.wait_ge(row_gathered, 16 * (e + 1))
                    turn(rows, row_tp)

                def bias(out_, sel, table):
                    for h in range(2):
                        pe.matmul(out_[:, h * HALF:(h + 1) * HALF], sel[:, :], table[:, h * HALF:(h + 1) * HALF],
                                  start=True, stop=False)

                def product(i, c, x_hi, x_lo, out_):
                    pe.wait_ge(lo_ready, pos(i, c) + 1)
                    s = ring(i, c, SPLIT)
                    wh = w_hi[s][:, :].rearrange("p (k h n) -> p k h n", k=KC, h=2)
                    wl = w_lo[s][:, :].rearrange("p (k h n) -> p k h n", k=KC, h=2)
                    for kk in range(KC):
                        k = (c % MCH) * KC + kk
                        for x, w in ((x_hi, wh), (x_hi, wl), (x_lo, wh)):
                            for h in range(2):
                                mm = pe.matmul(out_[:, h * HALF:(h + 1) * HALF], x[:, k, :], w[:, kk, h, :],
                                               start=False, stop=(k == KT - 1 and x is x_lo))
                    mm.then_inc(mm_done, 1)

                def gate_up(i):
                    first = isinstance(i, int) and i == 0
                    pe.wait_ge(ht_lo_ready, i + 1)
                    pe.wait_ge(sel_gu_ready, i + 1)
                    if not first:
                        pe.wait_ge(g_clipped, i)
                    bias(g_ps, sel_gu, bias_t[0])
                    for c in range(0, MCH):
                        product(i, c, ht_hi, ht_lo, g_ps)
                    if not first:
                        pe.wait_ge(act_ready, i)
                        turn(a_sb, act_tp)
                    if not (isinstance(i, int) and i < 2):
                        pe.wait_ge(y_copied, i - 1)
                    row_ids(i + 1)
                    if not first:
                        pe.wait_ge(u_clipped, i)
                    bias(u_ps, sel_gu, bias_t[1])
                    for c in range(MCH, 2 * MCH):
                        product(i, c, ht_hi, ht_lo, u_ps)

                def down(i, last):
                    pe.wait_ge(at_lo_ready, i)
                    pe.wait_ge(sel_d_ready, i)
                    pe.wait_ge(id_ready, i + 2 if not last else E + 1)
                    bias(y_ps, sel_d, bias_t[2])
                    for c in range(2 * MCH, NCH):
                        product(i, c, at_hi, at_lo, y_ps)
                        if c == 2 * MCH + 1 and not last:
                            turn_rows(i + 1)

                row_ids(0)
                turn_rows(0)
                gate_up(0)
                pe.wait_ge(ht_lo_ready, 1)
                pe.wait_ge(id_ready, 2)
                turn_rows(1)
                gate_up(1)
                down(1, False)
                with pe.Fori(2, E) as i:
                    gate_up(i)
                    down(i, False)
                pe.wait_ge(ht_lo_ready, E + 1)
                pe.wait_ge(act_ready, E)
                turn(a_sb, act_tp)
                pe.wait_ge(y_copied, E - 1)
                down(E, True)


        LOADS = (DENSE_CH + TOTAL) // SLOTS
        with ExitStack() as extra:
            def sb(name, shape, dt=F32):
                return extra.enter_context(nc.sbuf_tensor(name, shape, dt))

            rows = sb("ov_rows", [P, D])
            ht = sb("ov_ht", [P, D])
            at_ = sb("ov_at", [P, D])
            g_sb = sb("ov_g", [P, D])
            s_sb = sb("ov_s", [P, D])
            u_sb = sb("ov_u", [P, D])
            y_sb = sb("ov_y", [P, D])
            member = sb("ov_member", [P, TT, P], BF16)
            row_id = sb("ov_row_id", [P, 1], U32)
            y_idx = sb("ov_y_idx", [P, 1], U32)
            rel = sb("ov_rel", [P, TT, 1])
            row_rank = sb("ov_row_rank", [P, 1])
            past_end = sb("ov_past_end", [P, 1])
            sel = sb("ov_sel", [2 * E, P], F32R)

            ov_chain = sem("ov_chain")
            ov_member = sem("ov_member_ready")
            ov_id_mm = sem("ov_id_mm")
            ov_id = sem("ov_id")
            ov_gathered = sem("ov_gathered")
            ov_row_tp = sem("ov_row_tp")
            ov_ht = sem("ov_ht_ready")
            ov_mm = sem("ov_mm")
            ov_g = sem("ov_g_clipped")
            ov_sig = sem("ov_sig")
            ov_act = sem("ov_act_ready")
            ov_act_tp = sem("ov_act_tp")
            ov_at = sem("ov_at_ready")
            ov_copied = sem("ov_copied")
            ov_done = sem("ov_done")

            def blocks(eng, body):
                n = eng.value_load(n_ov_i[0:1, 0:1], min_val=0, max_val=MAX_OV)
                with eng.Fori(0, MAX_OV) as j:
                    with eng.If(j < n):
                        body(j)
                        eng.wait_ge(ov_done, 16 * j + 16)
                        eng.nop(nofuse=True)

            block3 = extra.enter_context(nc.Block())
            ov_cleared = sem("ov_cleared")

            @block3.sync
            def _(sp):
                def body(j):
                    e = sp.value_load(ov_expert_i[0:1, bass.ds(j, 1)], min_val=0, max_val=E - 1)
                    for c in range(NCH):
                        if c >= SLOTS:
                            sp.wait_ge(ov_mm, NCH * j + (c - SLOTS + 1))
                        sp.dma_start(raw[c % SLOTS][:, :].rearrange("p (k n) -> p k n", k=KC),
                                     expert_src("gud"[c // MCH], e, c % MCH)).then_inc(raw_loaded[c % SLOTS], 16)
                blocks(sp, body)

            @block3.gpsimd
            def _(pool):
                pool.memset(rows[:, :], 0.0).then_inc(ov_cleared, 1)
                pool.wait_ge(ov_cleared, 1)

                def body(j):
                    pool.wait_ge(ov_id, j + 1)
                    pool.nop(nofuse=True)
                    pool.indirect_dma_start(rows[:, :], None, h2_dram,
                                            bass.IndirectOffsetOnAxis(ap=row_id[:, 0:1], axis=0),
                                            bounds_check=NTOK - 1, oob_is_err=False).then_inc(ov_gathered, 16)
                    pool.wait_ge(ov_copied, j + 1)
                    pool.nop(nofuse=True)
                    pool.indirect_dma_start(y_dram, bass.IndirectOffsetOnAxis(ap=y_idx[:, 0:1], axis=0),
                                            y_sb[:, :], None, bounds_check=ROWS - 1, oob_is_err=False)\
                        .then_inc(ov_done, 16)
                blocks(pool, body)

            @block3.scalar
            def _(act):
                def body(j):
                    act.wait_ge(ov_row_tp, j + 1)
                    act.activation(ht[:, :], tp_flat, ACT.Copy).then_inc(ov_ht, 1)
                    act.wait_ge(ov_g, j + 1)
                    act.activation(s_sb[:, :], g_sb[:, :], ACT.Sigmoid, scale=ALPHA).then_inc(ov_sig, 1)
                    act.wait_ge(ov_act_tp, j + 1)
                    act.activation(at_[:, :], tp_flat, ACT.Copy).then_inc(ov_at, 1)
                    act.wait_ge(ov_mm, NCH * j + NCH)
                    act.activation(y_sb[:, :], y_ps, ACT.Copy).then_inc(ov_copied, 1)
                blocks(act, body)

            @block3.vector
            def _(dve):
                CHAIN = 7

                def body(j):
                    k = 0

                    def step(ins):
                        nonlocal k
                        k += 1
                        ins.then_inc(ov_chain, 1)
                        dve.wait_ge(ov_chain, CHAIN * j + k)

                    e = dve.value_load(ov_expert_i[0:1, bass.ds(j, 1)], min_val=0, max_val=E - 1)
                    step(dve.tensor_scalar(rel[:, :, :], rank_m[:, :, bass.ds(e, 1)], ov_base[:, bass.ds(j, 1)], None,
                                           ALU.subtract))
                    step(dve.tensor_tensor(member[:, :, :], iota_m[:, :].unsqueeze(1).to_broadcast([P, TT, P]),
                                           rel[:, :, :].to_broadcast([P, TT, P]), ALU.is_equal))
                    step(dve.tensor_tensor(row_rank[:, :], p_col[:, :], ov_base[:, bass.ds(j, 1)], ALU.add))
                    step(dve.tensor_scalar(past_end[:, :], cnt[:, bass.ds(e, 1)], row_rank[:, 0:1], float(SKIP),
                                           ALU.is_le, ALU.mult))
                    step(dve.scalar_tensor_tensor(out=y_idx[:, :], in0=start[:, bass.ds(e, 1)],
                                                  scalar=row_rank[:, 0:1], in1=past_end[:, :],
                                                  op0=ALU.add, op1=ALU.add))
                    dve.tensor_scalar(sel[:, :], ov_expert[0:2 * E, bass.ds(j, 1)].to_broadcast([2 * E, P]),
                                      pmod[:, 0:1], None, ALU.is_equal).then_inc(ov_member, 1)
                    dve.wait_ge(ov_id_mm, j + 1)
                    dve.scalar_tensor_tensor(out=row_id[:, :], in0=y_ps[:, 0:1], scalar=y_ps[:, 1:2],
                                             in1=past_end[:, :], op0=ALU.add, op1=ALU.add).then_inc(ov_id, 1)
                    dve.wait_ge(ov_mm, NCH * j + MCH)
                    dve.tensor_scalar(g_sb[:, :], g_ps, LIMIT, None, ALU.min).then_inc(ov_g, 1)
                    dve.wait_ge(ov_mm, NCH * j + 2 * MCH)
                    step(dve.tensor_scalar(u_sb[:, :], u_ps, LIMIT, -LIMIT, ALU.min, ALU.max))
                    dve.wait_ge(ov_sig, j + 1)
                    step(dve.tensor_tensor(g_sb[:, :], g_sb[:, :], s_sb[:, :], ALU.mult))
                    dve.scalar_tensor_tensor(out=u_sb[:, :], in0=u_sb[:, :], scalar=1.0, in1=g_sb[:, :],
                                             op0=ALU.add, op1=ALU.mult).then_inc(ov_act, 1)
                    assert k == CHAIN
                blocks(dve, body)

            @block3.tensor
            def _(pe):
                def body(j):
                    pe.wait_ge(ov_member, j + 1)
                    for t in range(TT):
                        mm = pe.matmul(y_ps[:, 0:2], member[:, t, :], tok_bf[:, t, :], start=(t == 0),
                                       stop=(t == TT - 1))
                    mm.then_inc(ov_id_mm, 1)
                    pe.wait_ge(ov_gathered, 16 * j + 16)
                    for k in range(KT):
                        mm = pe.transpose(tp_flat[:, k * P:(k + 1) * P], rows[:, k * P:(k + 1) * P], ident[:, :])
                    mm.then_inc(ov_row_tp, 1)
                    pe.wait_ge(ov_ht, j + 1)
                    for c in range(NCH):
                        m = c // MCH
                        out_, x = (g_ps, u_ps, y_ps)[m], (ht, ht, at_)[m]
                        if c == 2 * MCH:
                            pe.wait_ge(ov_act, j + 1)
                            for k in range(KT):
                                mm = pe.transpose(tp_flat[:, k * P:(k + 1) * P], u_sb[:, k * P:(k + 1) * P],
                                                  ident[:, :])
                            mm.then_inc(ov_act_tp, 1)
                            pe.wait_ge(ov_at, j + 1)
                        if c % MCH == 0:
                            for h in range(2):
                                pe.matmul(out_[:, h * HALF:(h + 1) * HALF], sel[:, :],
                                          bias_t[m][:, h * HALF:(h + 1) * HALF], start=True, stop=False)
                        pe.wait_ge(raw_loaded[c % SLOTS],
                                   j * (16 * NCH // SLOTS) + 16 * (LOADS + c // SLOTS + 1))
                        w = raw[c % SLOTS][:, :].rearrange("p (k h n) -> p k h n", k=KC, h=2)
                        for kk in range(KC):
                            k = (c % MCH) * KC + kk
                            for h in range(2):
                                mm = pe.matmul(out_[:, h * HALF:(h + 1) * HALF], x[:, k * P:(k + 1) * P],
                                               w[:, kk, h, :], start=False, stop=(k == KT - 1))
                        mm.then_inc(ov_mm, 1)
                blocks(pe, body)

        with ExitStack() as final:
            def sb(name, shape, dt=F32):
                return final.enter_context(nc.sbuf_tensor(name, shape, dt))

            picked = [[sb(f"picked{b}_{k}", [P, D]) for k in range(TOPK)] for b in range(2)]
            ffn = [sb(f"ffn{b}", [P, D]) for b in range(2)]
            fn_bc = sb("fn_bc", [P, D])
            out_sb = [sb(f"out_sb{b}", [P, D]) for b in range(2)]
            fin_ss = sb("fin_ss", [P, TT])
            fin_rstd = sb("fin_rstd", [P, TT])

            fn_loaded = sem("fn_loaded")
            picked_in = [[sem(f"picked_in{b}_{k}") for k in range(TOPK)] for b in range(2)]
            fin_step = sem("fin_step")
            g2_spread = sem("g2_spread")
            ffn_done = sem("ffn_done")
            x2_ready = sem("x2_ready")
            fin_sq = sem("fin_sq")
            fin_sqrt = sem("fin_sqrt")
            out_ready = sem("out_ready")
            out_stored = [sem(f"out_stored{b}") for b in range(2)]

            block4 = final.enter_context(nc.Block())

            @block4.sync
            def _(sp):
                sp.dma_start(fn_bc[:, :], final_norm.partition_broadcast(P)).then_inc(fn_loaded, 16)
                for t in range(TT):
                    sp.wait_ge(out_ready, t + 1)
                    dst = y_prompt[0, t * P:(t + 1) * P, :] if t < PT else y_sample.rearrange("b t d -> (b t) d")
                    sp.dma_start(dst, out_sb[t % 2][0:norm_rows(t), :]).then_inc(out_stored[t % 2], 16)
                sp.wait_ge(out_stored[0], 16 * ((TT + 1) // 2))
                sp.wait_ge(out_stored[1], 16 * (TT // 2))

            @block4.gpsimd
            def _(pool):
                for t in range(TT):
                    r = norm_rows(t)
                    if t >= 2:
                        pool.wait_ge(ffn_done, t - 1)
                    for k in range(TOPK):
                        pool.indirect_dma_start(picked[t % 2][k][0:r, :], None, y_dram,
                                                bass.IndirectOffsetOnAxis(ap=slot_i[0:r, t, k:k + 1], axis=0))\
                            .then_inc(picked_in[t % 2][k], 16)

            @block4.tensor
            def _(pe):
                for sel_, r, out_ in ((sel_p, P, g_ps), (sel_s, NS, u_ps)):
                    for q in range(Q):
                        mm = pe.matmul(out_[0:r, q * QW:(q + 1) * QW], sel_[:, q, :],
                                       mod[:, G2 * QW:(G2 + 1) * QW], start=True, stop=True)
                mm.then_inc(g2_spread, 1)

            @block4.vector
            def _(dve):
                def step(ins):
                    step.n += 1
                    ins.then_inc(fin_step, 1)
                    dve.wait_ge(fin_step, step.n)
                step.n = 0
                step(dve.memset(fin_ss[:, :], 1.0))
                dve.wait_ge(g2_spread, 1)
                dve.wait_ge(fn_loaded, 16)
                for t in range(TT):
                    r = norm_rows(t)
                    f = ffn[t % 2][0:r, :]
                    if t >= 2:
                        dve.wait_ge(fin_sq, t - 1)
                    for k in range(TOPK):
                        dve.wait_ge(picked_in[t % 2][k], 16 * (t // 2 + 1))
                        y, g = picked[t % 2][k][0:r, :], gates[0:r, t, k:k + 1]
                        ins = (dve.tensor_scalar(f, y, g, None, ALU.mult) if k == 0 else
                               dve.scalar_tensor_tensor(out=f, in0=y, scalar=g, in1=f, op0=ALU.mult, op1=ALU.add))
                        if k < TOPK - 1:
                            step(ins)
                    ins.then_inc(ffn_done, 1)
                    dve.wait_ge(ffn_done, t + 1)
                    step(dve.tensor_tensor(f, f, (g_ps if t < PT else u_ps)[0:r, :], ALU.mult))
                    dve.tensor_tensor(x_sb[0:r, t, :], x_sb[0:r, t, :], f, ALU.add).then_inc(x2_ready, 1)
                    dve.wait_ge(fin_sqrt, t + 1)
                    step(dve.reciprocal(fin_rstd[0:r, t:t + 1], fin_ss[0:r, t:t + 1]))
                    if t >= 2:
                        dve.wait_ge(out_stored[t % 2], 16 * (t // 2))
                    dve.scalar_tensor_tensor(out=out_sb[t % 2][0:r, :], in0=x_sb[0:r, t, :],
                                             scalar=fin_rstd[0:r, t:t + 1], in1=fn_bc[0:r, :],
                                             op0=ALU.mult, op1=ALU.mult).then_inc(out_ready, 1)

            @block4.scalar
            def _(act):
                for t in range(TT):
                    r = norm_rows(t)
                    act.wait_ge(x2_ready, t + 1)
                    act.activation(ffn[t % 2][0:r, :], x_sb[0:r, t, :], ACT.Square,
                                   accum_out=fin_ss[0:r, t:t + 1]).then_inc(fin_sq, 1)
                    act.wait_ge(fin_sq, t + 1)
                    act.activation(fin_ss[0:r, t:t + 1], fin_ss[0:r, t:t + 1], ACT.Sqrt, bias=eps_c[0:r, 0:1],
                                   scale=1.0 / D).then_inc(fin_sqrt, 1)


_INS = ["x_prompt", "x_sample", "state_pool", "state_conv", "c_prompt", "c_sample", "norm1", "norm2",
        "w_ada", "b_ada", "w_in", "w_pool", "pool_scale", "w_conv", "w_out", "w_router", "b_router",
        "w_gate", "b_gate", "w_up", "b_up", "w_down", "b_down", "final_norm"]
_OUTS = [(1, SEQ, D), (DEC_B, DEC_T, D), (1, 1, PAST, DP), (1, 1, CPAST, DP),
         (1, DEC_B, PAST, DP), (1, DEC_B, CPAST, DP)]


def kernel(**inputs):
    import numpy as _np
    import concourse.bacc as _bacc
    from concourse import mybir as _mybir
    from concourse.bass_utils import run_bass_kernel_spmd as _run

    nc = _bacc.Bacc("TRN2", target_bir_lowering=False, num_devices=1)
    arrays, args = {}, []
    for name in _INS:
        a = _np.ascontiguousarray(inputs[name])
        arrays[f"in_{name}"] = a
        args.append(nc.dram_tensor(f"in_{name}", a.shape, _mybir.dt.from_np(a.dtype), kind="ExternalInput").ap())
    for i, shape in enumerate(_OUTS):
        args.append(nc.dram_tensor(f"out_{i}", shape, F32, kind="ExternalOutput").ap())
    hybrid_step(nc, *args)
    r = _run(nc, [arrays], core_ids=[0])
    return tuple(r.results[0][f"out_{i}"] for i in range(len(_OUTS)))
```

```python
from contextlib import ExitStack

import concourse.bass as bass
from concourse import mybir

ALU = mybir.AluOpType
ACT = mybir.ActivationFunctionType
AX = mybir.AxisListType
F32 = mybir.dt.float32
F32R = mybir.dt.float32r
BF16 = mybir.dt.bfloat16
I32 = mybir.dt.int32
U32 = mybir.dt.uint32

P = 128
D = 1024
KT = D // P
SEQ = 512
DEC_B, DEC_T = 8, 4
NS = DEC_B * DEC_T
PT = SEQ // P
TT = PT + 1
NTOK = SEQ + NS
NC = 1 + DEC_B
DP = 512
GR = DP // P
WINDOWS = (2, 4, 8, 16)
PAST = 15
CPAST = 2
E = 32
TOPK = 4
LIMIT = 7.0
ALPHA = 1.702
EPS = 1e-5
HALF = 512
CW = 256
ADA_CH = 6 * D // CW
IN_CH = 4 * DP // CW
OUT_CH = D // CW
DENSE_CH = ADA_CH + IN_CH + OUT_CH
SLOTS = 6
KC = 2
MCH = KT // KC
SPLIT = 4
SLOT_F = KC * D
MAX_OV = TOPK * NTOK // P - 1
Q = 4
QW = D // Q
PARTS = 6
SH1, SC1, G1, SH2, SC2, G2 = range(PARTS)
CPAD = P // Q
ROWS = TOPK * NTOK
SKIP = 1 << 20
EXTRA = -(-NTOK // P) - 1


def hybrid_step(nc, x_prompt, x_sample, state_pool, state_conv, c_prompt, c_sample, norm1, norm2,
                w_ada, b_ada, w_in, w_pool, pool_scale, w_conv, w_out, w_router, b_router,
                w_gate, b_gate, w_up, b_up, w_down, b_down, final_norm,
                y_prompt, y_sample, new_pool_prompt, new_conv_prompt, new_pool_sample, new_conv_sample):
    h2_dram = nc.dram_tensor("h2_rows", (NTOK, D), F32).ap()
    y_dram = nc.dram_tensor("expert_rows", (ROWS, D), F32).ap()

    top = ExitStack()
    with top:
        def sem(name):
            return top.enter_context(nc.semaphore(name))

        def keep(name, shape, dt=F32):
            return top.enter_context(nc.sbuf_tensor(name, shape, dt))

        psum = [top.enter_context(nc.psum_tensor(f"acc{i}", [P, 2, HALF], F32)) for i in range(4)]
        acc_g, acc_u, acc_y, tp = psum

        raw = [keep(f"raw{s}", [P, SLOT_F]) for s in range(SLOTS)]
        x_sb = keep("x_sb", [P, TT, D])
        mod = keep("mod", [P, PARTS * QW])
        bias_t = [keep(f"bias_{m}", [2 * E, D], F32R) for m in ("gate", "up", "down")]
        ident = keep("ident", [P, P])
        iota_m = keep("iota_m", [P, P])
        p_col = keep("p_col", [P, 1])
        rank_m = keep("rank_m", [P, TT, E + 1])
        cnt = keep("cnt", [P, E])
        start = keep("start", [P, E])
        skip = keep("skip", [P, E + 1])
        y_row = keep("y_row", [P, E])
        slot_f = keep("slot_f", [P, TT, TOPK])
        slot_i = keep("slot_i", [P, TT, TOPK], U32)
        gates = keep("gates", [P, TT, TOPK])
        tok_bf = keep("tok_bf", [P, TT, 2], BF16)
        expert_id2 = keep("expert_id2", [2 * E, E + 1])
        pmod = keep("pmod", [2 * E, 1])
        n_ov_i = keep("n_ov_i", [P, 1], I32)
        ov_expert = keep("ov_expert", [P, MAX_OV])
        ov_expert_i = keep("ov_expert_i", [P, MAX_OV], I32)
        ov_base = keep("ov_base", [P, MAX_OV])
        sel_p = keep("sel_p", [P, Q, P])
        sel_s = keep("sel_s", [P, Q, NS])
        ss = keep("ss", [P, TT])
        rstd = keep("rstd", [P, TT])
        eps_c = keep("eps_c", [P, 1])

        raw_loaded = [sem(f"raw_loaded{s}") for s in range(SLOTS)]

        part = ExitStack()

        def sb(name, shape, dt=F32):
            return part.enter_context(nc.sbuf_tensor(name, shape, dt))

        c_sg = sb("c_sg", [P, KT, NC])
        c_act = sb("c_act", [P, KT, CPAD])
        n1_rows = sb("n1_rows", [P, QW])
        n2_rows = sb("n2_rows", [P, QW])
        junk = sb("junk", [P, D])
        h_row = [sb(f"h_row{i}", [P, D]) for i in range(2)]
        h_t = sb("h_t", [P, KT, NTOK])
        mix_t = h_t
        uext = sb("uext", [P, GR, PAST + SEQ])
        uext_s = sb("uext_s", [P, GR, DEC_B, PAST + DEC_T])
        vext = sb("vext", [P, GR, CPAST + SEQ])
        vext_s = sb("vext_s", [P, GR, DEC_B, CPAST + DEC_T])
        gate_b = sb("gate_b", [P, GR, NTOK])
        gate_c = sb("gate_c", [P, GR, NTOK])
        pooled = sb("pooled", [P, GR, NTOK])
        conv = h_t[:, GR:2 * GR, :]
        wsum = [sb(f"wsum{i}", [P, PAST + SEQ]) for i in range(2)]
        g1_bc = sb("g1_bc", [P, D])
        c_rows = g1_bc[0:NC, :]
        g1_bc_s = sb("g1_bc_s", [NS, D])
        a2_bc = sb("a2_bc", [P, 2, D])
        a2_bc_s = gate_c[0:NS, :, :].rearrange("p g n -> p (g n)")[:, 0:2 * D].rearrange("p (a n) -> p a n", a=2)
        b_raw = [a2_bc[0:2 * E, 0, :], a2_bc[0:2 * E, 1, :], junk[0:2 * E, :]]
        cols = sb("cols", [P, 2, KT // Q, Q, CPAD])
        par = sb("par", [P, 4 * GR])
        par_rows = sb("par_rows", [4 * GR, P])
        wpool_sb = sb("wpool_sb", [P, GR, P])
        wr_sb = sb("wr_sb", [P, KT, E])
        br_bc = sb("br_bc", [P, E])
        inv_n = sb("inv_n", [P, 16])
        spare = pooled[:, :, :].rearrange("p g n -> p (g n)")
        sp_rows = spare[0:DEC_B * PAST, 0:DP]
        sc_rows = spare[0:DEC_B * CPAST, DP:2 * DP]
        onehot = spare[:, 0:TT * TOPK * E].rearrange("p (t k e) -> p t k e", t=TT, k=TOPK)
        pick = spare[:, TT * TOPK * E:2 * TT * TOPK * E].rearrange("p (t k e) -> p t k e", t=TT, k=TOPK)
        ov_cmp = spare[:, 2 * TT * TOPK * E:2 * TT * TOPK * E + MAX_OV * E].rearrange("p (j e) -> p j e", e=E)
        state_o = [gate_b[0:n, i, 0:DP] for i, n in enumerate((PAST, CPAST, NS, DEC_B * CPAST))]
        u_new = gate_b[:, :, SEQ:NTOK]
        v_new = sb("v_new", [P, GR, DEC_B * CPAST])
        logit = sb("logit", [P, TT, E])
        top_v = sb("top_v", [P, TT, 8])
        top_i = sb("top_i", [P, TT, 8], U32)
        top_f = sb("top_f", [P, TT, TOPK])
        e_sum = sb("e_sum", [P, TT])
        mask_bf = sb("mask_bf", [P, TT, E], BF16)
        slot_e = sb("slot_e", [P, TT, E])
        iota_e = sb("iota_e", [P, E])
        iota_j = sb("iota_j", [P, MAX_OV])
        tri = sb("tri", [P, P], BF16)
        ones_bf = sb("ones_bf", [P, P], BF16)
        ones_e = sb("ones_e", [P, E])
        small = [sb(f"small{i}", [P, E]) for i in range(3)]

        zt = [acc_g, acc_u]
        PH = SEQ // 2
        z_prompt = [z[:, :, 0:PH] for z in zt]
        z_sample = [z[:, 1, PH:PH + NS].rearrange("p (s t) -> p s t", t=DEC_T) for z in zt]
        pm_p = [acc_g[:, 0, :], acc_g[:, 1, :], acc_u[:, 0, :], acc_u[:, 1, :]]
        mixp = [acc_g, acc_u]
        modp = acc_y[:, 0, 0:QW]
        lg = [acc_y[0:NS if t == PT else P, t % 2, t // 2 * E:(t // 2 + 1) * E] for t in range(TT)]
        rank_ps = acc_y[:, 0, PT * E:(PT + TT) * E].rearrange("p (t e) -> p t e", e=E)
        cnt_ps = acc_y[:, 0, (PT + TT) * E:(PT + TT + 1) * E]
        c_ps = tp[:, 1, 0:KT * NC].rearrange("p (k r) -> p k r", r=NC)

        c_loaded = sem("c_loaded")
        x_loaded = sem("x_loaded")
        rows_loaded = sem("rows_loaded")
        small_loaded = sem("small_loaded")
        bias_loaded = sem("bias_loaded")
        pool_step = sem("pool_step")
        rows_cleared = sem("rows_cleared")
        consts = sem("consts")
        dve_step = sem("dve_step")
        act_step = sem("act_step")
        c_ready = sem("c_ready")
        ada_done = sem("ada_done")
        ada_added = sem("ada_added")
        scale_ready = sem("scale_ready")
        h_modulated = sem("h_modulated")
        tp_full = sem("tp_full")
        tp_free = sem("tp_free")
        sq_done = sem("sq_done")
        rstd_ready = sem("rstd_ready")
        h_ready = sem("h_ready")
        z_done = sem("z_done")
        z_evac = sem("z_evac")
        v_ready = sem("v_ready")
        v_s_ready = sem("v_s_ready")
        logits_in = sem("logits_in")
        pooled_ready = sem("pooled_ready")
        pooled_s_ready = sem("pooled_s_ready")
        pm_done = sem("pm_done")
        pm_ready = sem("pm_ready")
        conv_ready = sem("conv_ready")
        conv_s_ready = sem("conv_s_ready")
        mix_done = sem("mix_done")
        x1_ready = sem("x1_ready")
        new_packed = sem("new_packed")
        so_ready = sem("so_ready")
        state_stored = sem("state_stored")
        h2_stored = [sem(f"h2_stored{b}") for b in range(2)]
        lg_done = sem("lg_done")
        shifted = sem("shifted")
        exp_done = sem("exp_done")
        mask_ready = sem("mask_ready")
        rank_done = sem("rank_done")
        bias_hi = sem("bias_hi")
        bias_ready = sem("bias_ready")

        TP = ["c"] + [f"n{t}" for t in range(TT)] + ["par", "st", "cols"]
        TP += ["g1", "g1_s", "a2", "s2", "pm_s", "h0", "a2_s", "h1", "s2_s", "h2", "so0", "h3", "so1", "h4"]
        TP = {name: n for n, name in enumerate(TP)}

        def ada_chunks(part_):
            return [("ada", Q * part_ + q) for q in range(Q)]

        def in_chunks(a, b):
            return [("in", k) for k in range(a, b)]

        order = ada_chunks(SH1) + ada_chunks(SC1) + in_chunks(0, 4) + ada_chunks(G1) + in_chunks(4, 6)
        order += ada_chunks(SH2) + in_chunks(6, 7) + ada_chunks(SC2) + in_chunks(7, 8) + ada_chunks(G2)
        order += [("out", k) for k in (2, 3, 0, 1)]
        ADA_AT = {p: n for n, p in enumerate((SH1, SC1, G1, SH2, SC2, G2))}
        IN_COL = [0, 1, 4, 5, 6, 7, 2, 3]
        at = {key: n for n, key in enumerate(order)}
        assert len(order) == DENSE_CH and DENSE_CH % SLOTS == 0

        def dense_src(kind, k):
            if kind == "out":
                return w_out[0].rearrange("(c k p) n -> c p k n", k=KC, p=P)[k]
            w, col = (w_ada[0], k) if kind == "ada" else (w_in[0], IN_COL[k])
            return w[:, col * CW:(col + 1) * CW].rearrange("(k p) n -> p k n", p=P)

        def used(n):
            kind, k = order[n]
            return {"ada": (ada_done, ADA_AT[k // Q] + 1), "in": (z_done, 2 * (k + 1)), "out": (mix_done, TT)}[kind]

        def chunk_view(n):
            return raw[n % SLOTS][:, :].rearrange("p (k n) -> p k n", k=KC if order[n][0] == "out" else KT)

        def expert_src(kind, e, c):
            w = {"g": w_gate, "u": w_up, "d": w_down}[kind]
            rows = w[0].rearrange("e (c k p) n -> e c p k n", k=KC, p=P)
            return rows[e, c] if isinstance(e, int) else rows[bass.ds(e, 1), c].rearrange("a p k n -> (a p) k n")

        FIRST_STREAM = [("g", 0, c) for c in range(MCH)] + [("u", 0, c) for c in range(MCH)]

        POOL_STEPS = 21
        CONSTS = 21

        def norm_rows(t):
            return P if t < PT else NS

        block = part.enter_context(nc.Block())

        @block.sync
        def _(sp):
            sp.dma_start(c_rows[0:1, :], c_prompt).then_inc(c_loaded, 16)
            sp.dma_start(c_rows[1:NC, :], c_sample).then_inc(c_loaded, 16)
            sp.dma_start(x_sb[:, 0:PT, :], x_prompt[0].rearrange("(t p) d -> p t d", p=P)).then_inc(x_loaded, 16)
            sp.dma_start(x_sb[0:NS, PT, :], x_sample.rearrange("b t d -> (b t) d")).then_inc(x_loaded, 16)
            for n, (kind, k) in enumerate(order):
                if n >= SLOTS:
                    sp.wait_ge(*used(n - SLOTS))
                sp.dma_start(chunk_view(n), dense_src(kind, k)).then_inc(raw_loaded[n % SLOTS], 16)
                if n == SLOTS - 1:
                    sp.wait_ge(rows_cleared, 4)
                    for q in range(Q):
                        lo_, hi_ = q * CPAD, q * CPAD + NC
                        sp.dma_start(mod[lo_:hi_, :].rearrange("p (a n) -> p a n", n=QW),
                                      b_ada[0].rearrange("(a q n) -> q a n", q=Q, n=QW)[q].partition_broadcast(NC))\
                            .then_inc(rows_loaded, 16)
                        for rows_, nrm in ((n1_rows, norm1), (n2_rows, norm2)):
                            sp.dma_start(rows_[lo_:hi_, :], nrm[0, q * QW:(q + 1) * QW].partition_broadcast(NC))\
                                .then_inc(rows_loaded, 16)
                    sp.dma_start(par_rows[0:GR, :], pool_scale[0].rearrange("(g p) -> g p", p=P)).then_inc(small_loaded, 16)
                    sp.dma_start(par_rows[GR:4 * GR, :], w_conv[0].rearrange("w (g p) -> (w g) p", p=P))\
                        .then_inc(small_loaded, 16)
                    sp.dma_start(sp_rows, state_pool[0].rearrange("b r d -> (b r) d")).then_inc(small_loaded, 16)
                    sp.dma_start(sc_rows, state_conv[0].rearrange("b r d -> (b r) d")).then_inc(small_loaded, 16)
                    sp.dma_start(wpool_sb[:, :, :], w_pool[0].rearrange("g c d -> c g d")).then_inc(small_loaded, 16)
                    sp.dma_start(wr_sb[:, :, :], w_router[0].rearrange("(k p) e -> p k e", p=P)).then_inc(small_loaded, 16)
                    sp.dma_start(br_bc[:, :], b_router[0].partition_broadcast(P)).then_inc(small_loaded, 16)

            def first(n):
                kind, e, c = FIRST_STREAM[n]
                sp.wait_ge(*used(DENSE_CH - SLOTS + n))
                sp.dma_start(raw[n][:, :].rearrange("p (k n) -> p k n", k=KC), expert_src(kind, e, c))\
                    .then_inc(raw_loaded[n], 16)

            for n in range(SLOTS - OUT_CH):
                first(n)
            for t in range(TT):
                sp.wait_ge(h_ready, TT + t + 1)
                sp.dma_start(h2_dram[t * P:t * P + norm_rows(t), :], h_row[t % 2][0:norm_rows(t), :])\
                    .then_inc(h2_stored[t % 2], 16)
            for n in range(SLOTS - OUT_CH, SLOTS):
                first(n)
            sp.wait_ge(h2_stored[0], 16 * ((TT + 1) // 2))
            sp.wait_ge(h2_stored[1], 16 * (TT // 2))
            sp.wait_ge(state_stored, 16 * (3 + DEC_B + DEC_B))

        @block.gpsimd
        def _(pool):
            def step(ins):
                step.n += 1
                ins.then_inc(pool_step, 1)
                pool.wait_ge(pool_step, step.n)
            step.n = 0
            pool.memset(mod[:, :], 0.0).then_inc(rows_cleared, 1)
            pool.memset(n1_rows[:, :], 0.0).then_inc(rows_cleared, 1)
            pool.memset(n2_rows[:, :], 0.0).then_inc(rows_cleared, 1)
            pool.memset(c_act[:, :, :], 0.0).then_inc(rows_cleared, 1)
            step(pool.memset(ident[:, :], 0.0))
            step(pool.affine_select(out=ident[:, :], in_=ident[:, :], compare_op=ALU.not_equal, fill=1.0,
                                    base=0, pattern=[[-1, P]], channel_multiplier=1))
            step(pool.memset(sel_p[:, :, :], 1.0))
            step(pool.affine_select(out=sel_p[:, :, :], in_=sel_p[:, :, :], compare_op=ALU.is_equal, fill=0.0,
                                    base=0, pattern=[[-CPAD, Q], [0, P]], channel_multiplier=1))
            step(pool.memset(sel_s[:, :, :], 1.0))
            for q in range(Q):
                v = sel_s[:, q, :].rearrange("p (s t) -> p s t", t=DEC_T)
                step(pool.affine_select(out=v, in_=v, compare_op=ALU.is_equal, fill=0.0, base=-1 - CPAD * q,
                                        pattern=[[-1, DEC_B], [0, DEC_T]], channel_multiplier=1))
            pool.memset(eps_c[:, :], EPS).then_inc(consts, 1)
            pool.memset(ss[:, :], 1.0).then_inc(consts, 1)
            for w in range(16):
                pool.memset(inv_n[:, w:w + 1], 1.0 / (w + 1)).then_inc(consts, 1)
            pool.memset(uext[:, :, 0:PAST], 0.0).then_inc(consts, 1)
            pool.memset(vext[:, :, 0:CPAST], 0.0).then_inc(consts, 1)
            pool.memset(top_v[:, :, :], 0.0).then_inc(consts, 1)
            step(pool.memset(tri[:, :], 1.0))
            step(pool.affine_select(out=tri[:, :], in_=tri[:, :], compare_op=ALU.is_gt, fill=0.0,
                                    base=0, pattern=[[1, P]], channel_multiplier=-1))
            step(pool.memset(ones_bf[:, :], 1.0))
            step(pool.memset(ones_e[:, :], 1.0))
            for out_, pat in ((iota_m, P), (iota_e, E), (iota_j, MAX_OV)):
                step(pool.iota(out_[:, :], pattern=[[1, pat]], base=0, channel_multiplier=0,
                               allow_small_or_imprecise_dtypes=True))
            step(pool.iota(p_col[:, :], pattern=[[0, 1]], base=0, channel_multiplier=1,
                           allow_small_or_imprecise_dtypes=True))
            step(pool.iota(tok_bf[:, :, 0], pattern=[[P, TT]], base=0, channel_multiplier=0,
                           allow_small_or_imprecise_dtypes=True))
            step(pool.iota(tok_bf[:, :, 1], pattern=[[0, TT]], base=0, channel_multiplier=1,
                           allow_small_or_imprecise_dtypes=True))
            step(pool.iota(expert_id2[:, :], pattern=[[1, E + 1]], base=0,
                           channel_multiplier=0, allow_small_or_imprecise_dtypes=True))
            for half in range(2):
                ins = pool.iota(pmod[half * E:(half + 1) * E, :], pattern=[[0, 1]], base=0,
                                channel_multiplier=1, allow_small_or_imprecise_dtypes=True)
                if half:
                    step(ins)
            assert step.n == POOL_STEPS, step.n
            for s in range(DEC_B):
                pool.dma_start(new_pool_sample[0, s, 0:PAST - DEC_T, :], state_pool[0, s, DEC_T:PAST, :])\
                    .then_inc(state_stored, 16)

            pool.wait_ge(so_ready, 2)
            pool.dma_start(new_pool_prompt[0, 0], state_o[0]).then_inc(state_stored, 16)
            pool.dma_start(new_conv_prompt[0, 0], state_o[1]).then_inc(state_stored, 16)
            pool.wait_ge(so_ready, 4)
            for s in range(DEC_B):
                pool.dma_start(new_pool_sample[0, s, PAST - DEC_T:PAST, :],
                              gate_b[s * DEC_T:(s + 1) * DEC_T, 2, 0:DP]).then_inc(state_stored, 16)
            pool.dma_start(new_conv_sample[0].rearrange("b r d -> (b r) d"), state_o[3]).then_inc(state_stored, 16)

        @block.scalar
        def _(act):
            def empty(name, out_, in_, scale=None):
                act.wait_ge(tp_full, TP[name] + 1)
                if scale is None:
                    act.activation(out_, in_, ACT.Copy).then_inc(tp_free, 1)
                else:
                    act.activation(out_, in_, ACT.Identity, scale=scale).then_inc(tp_free, 1)

            whole = tp[:, :, :].rearrange("p b n -> p (b n)")
            act.wait_ge(tp_full, TP["c"] + 1)
            act.activation(c_sg[:, :, :], c_ps, ACT.Sigmoid).then_inc(tp_free, 1)

            def square(t, done):
                r = norm_rows(t)
                if not (done == 0 and t == 0):
                    act.wait_ge(act_step, done * TT + t)
                act.activation(junk[0:r, :], x_sb[0:r, t, :], ACT.Square,
                               accum_out=ss[0:r, t:t + 1]).then_inc(act_step, 1)

            act.wait_ge(x_loaded, 32)
            act.wait_ge(consts, 2)
            for t in range(TT):
                square(t, 0)
            act.wait_ge(act_step, TT)
            act.activation(ss[:, :], ss[:, :], ACT.Sqrt, bias=eps_c[:, 0:1], scale=1.0 / D).then_inc(sq_done, 1)
            act.wait_ge(sq_done, 1)
            for m, b in enumerate((b_gate, b_up, b_down)):
                for half in range(2):
                    act.dma_start(b_raw[m][half * E:(half + 1) * E, :], b[0]).then_inc(bias_loaded, 16)

            def turned(name, t):
                r = norm_rows(t)
                empty(name, h_t[:, :, t * P:t * P + r],
                      tp[:, :, :].rearrange("p b (k n) -> p (b k) n", n=P)[:, :, 0:r])

            for t in range(TT):
                turned(f"n{t}", t)
            empty("par", par[:, :], tp[:, 0, 0:4 * GR])
            n = DEC_B * PAST
            act.wait_ge(tp_full, TP["st"] + 1)
            act.activation(uext_s[:, :, :, 0:PAST], tp[:, 0, 0:GR * n].rearrange("p (g s r) -> p g s r", g=GR, r=PAST),
                           ACT.Copy).then_inc(new_packed, 1)
            n = DEC_B * CPAST
            act.activation(vext_s[:, :, :, 0:CPAST],
                           tp[:, 1, 0:GR * n].rearrange("p (g s r) -> p g s r", g=GR, r=CPAST),
                           ACT.Copy).then_inc(new_packed, 1)
            act.wait_ge(new_packed, 2)
            act.sem_inc(tp_free, 1)
            empty("cols", cols[:, :, :, :, :].rearrange("p a h q r -> p (a h q r)"), tp[:, 0, :])
            act.wait_ge(tp_free, TP["cols"] + 1)
            for k in range(KT // 2, KT):
                act.activation(h_t[:, k, 0:SEQ], h_t[:, k, 0:SEQ], ACT.Identity,
                               scale=cols[:, 0, k % 2, k // 2, 0:1],
                               bias=cols[:, 1, k % 2, k // 2, 0:1]).then_inc(h_modulated, 1)

            def leave(f, dst, dst_s):
                act.wait_ge(z_done, f + 1)
                act.activation(dst.rearrange("p (b n) -> p b n", b=2), z_prompt[f % 2], ACT.Copy)\
                    .then_inc(z_evac, 1)
                act.activation(dst_s, z_sample[f % 2], ACT.Copy).then_inc(z_evac, 1)

            def by_seq(t_):
                return t_.rearrange("p (s t) -> p s t", t=DEC_T)

            for g in range(GR):
                leave(g, uext[:, g, PAST:PAST + SEQ], uext_s[:, g, :, PAST:PAST + DEC_T])
            act.wait_ge(bias_loaded, 16 * 6)
            for m in range(3):
                act.activation(bias_t[m][:, :], b_raw[m], ACT.Copy).then_inc(bias_hi, 1)
            for g in range(GR):
                leave(GR + g, gate_c[:, g, 0:SEQ], by_seq(gate_c[:, g, SEQ:NTOK]))
            empty("g1", g1_bc[:, :], whole)
            leave(3 * GR, gate_b[:, 0, 0:SEQ], by_seq(gate_b[:, 0, SEQ:NTOK]))
            leave(3 * GR + 1, gate_b[:, 1, 0:SEQ], by_seq(gate_b[:, 1, SEQ:NTOK]))
            empty("g1_s", g1_bc_s[:, :], whole[0:NS, :])
            leave(3 * GR + 2, gate_b[:, 2, 0:SEQ], by_seq(gate_b[:, 2, SEQ:NTOK]))
            leave(3 * GR + 3, gate_b[:, 3, 0:SEQ], by_seq(gate_b[:, 3, SEQ:NTOK]))
            act.wait_ge(bias_ready, 3)
            empty("a2", a2_bc[:, 0, :], whole)
            for g in range(GR):
                act.wait_ge(pm_done, g + 1)
                act.activation(mix_t[:, g, 0:SEQ], pm_p[g], ACT.Identity, scale=par[:, g:g + 1]).then_inc(pm_ready, 1)
            empty("s2", a2_bc[:, 1, :], whole)
            act.wait_ge(tp_full, TP["pm_s"] + 1)
            for g in range(GR):
                act.activation(mix_t[:, g, SEQ:NTOK], tp[:, 0, g * NS:(g + 1) * NS], ACT.Identity,
                               scale=par[:, g:g + 1]).then_inc(pm_ready, 1)
            act.wait_ge(pm_ready, 2 * GR)
            act.sem_inc(tp_free, 1)

            def states(i0):
                for i in (i0, i0 + 1):
                    act.wait_ge(tp_full, TP[f"so{i0 // 2}"] + 1)
                    act.activation(state_o[i], tp[0:state_o[i].shape[0], i % 2, :], ACT.Copy).then_inc(so_ready, 1)
                act.wait_ge(so_ready, i0 + 2)
                act.sem_inc(tp_free, 1)

            for t in range(TT):
                act.wait_ge(x1_ready, t + 1)
                square(t, 1)
                r = norm_rows(t)
                act.wait_ge(act_step, TT + t + 1)
                if t == 0:
                    act.wait_ge(rstd_ready, 1)
                act.activation(ss[0:r, t:t + 1], ss[0:r, t:t + 1], ACT.Sqrt, bias=eps_c[0:r, 0:1],
                               scale=1.0 / D).then_inc(sq_done, 1)
                turned(f"h{t}", t)
                if t == 2:
                    act.wait_ge(conv_ready, GR)
                    act.wait_ge(conv_s_ready, GR)
                    act.activation(u_new.rearrange("p g (s t) -> p g s t", t=DEC_T),
                                   uext_s[:, :, :, PAST:PAST + DEC_T], ACT.Copy).then_inc(new_packed, 1)
                    act.activation(v_new[:, :, :].rearrange("p g (s t) -> p g s t", t=CPAST),
                                   vext_s[:, :, :, DEC_T:DEC_T + CPAST], ACT.Copy).then_inc(new_packed, 1)
                    states(0)
                if t == 3:
                    states(2)
                if t == 0:
                    act.wait_ge(v_ready, GR)
                    act.wait_ge(v_s_ready, GR)
                    empty("a2_s", a2_bc_s[:, 0, :], whole[0:NS, :])
                if t == 1:
                    empty("s2_s", a2_bc_s[:, 1, :], whole[0:NS, :])
            act.wait_ge(shifted, 1)
            act.activation(gates[:, :, :], gates[:, :, :], ACT.Exp).then_inc(exp_done, 1)

        @block.vector
        def _(dve):
            def step(ins):
                step.n += 1
                ins.then_inc(dve_step, 1)
                dve.wait_ge(dve_step, step.n)
            step.n = 0

            dve.wait_ge(tp_free, TP["c"] + 1)
            dve.wait_ge(rows_cleared, 4)
            dve.tensor_tensor(c_act[:, :, 0:NC], c_ps, c_sg[:, :, :], ALU.mult).then_inc(c_ready, 1)

            def add_ada(p):
                dve.wait_ge(ada_done, ADA_AT[p] + 1)
                v = mod[:, p * QW:(p + 1) * QW]
                dve.tensor_tensor(v, v, modp, ALU.add).then_inc(ada_added, 1)

            def scale_rows(p, norm):
                dve.wait_ge(ada_added, ADA_AT[p] + 1)
                v = mod[:, p * QW:(p + 1) * QW]
                dve.scalar_tensor_tensor(out=v, in0=v, scalar=1.0, in1=norm[:, :], op0=ALU.add,
                                         op1=ALU.mult).then_inc(scale_ready, 1)

            def normalise(t, scale_, shift_):
                r = norm_rows(t)
                if t >= 2:
                    dve.wait_ge(tp_full, TP[f"h{t - 2}"] + 1)
                    dve.wait_ge(h2_stored[t % 2], 16 * (t // 2))
                h = h_row[t % 2][0:r, :]
                step(dve.scalar_tensor_tensor(out=h, in0=x_sb[0:r, t, :], scalar=rstd[0:r, t:t + 1],
                                              in1=scale_, op0=ALU.mult, op1=ALU.mult))
                dve.tensor_tensor(h, h, shift_, ALU.add).then_inc(h_ready, 1)

            dve.wait_ge(sq_done, 1)
            dve.reciprocal(rstd[:, :], ss[:, :]).then_inc(rstd_ready, 1)
            dve.wait_ge(rstd_ready, 1)
            for t in range(TT):
                r = norm_rows(t)
                if t >= 2:
                    dve.wait_ge(tp_full, TP[f"n{t - 2}"] + 1)
                dve.tensor_scalar(h_row[t % 2][0:r, :], x_sb[0:r, t, :], rstd[0:r, t:t + 1], None, ALU.mult)\
                    .then_inc(h_ready, 1)
            dve.wait_ge(rows_loaded, 16 * 3 * Q)
            add_ada(SH1)
            add_ada(SC1)
            scale_rows(SC1, n1_rows)
            dve.wait_ge(tp_free, TP["cols"] + 1)
            for k in range(KT // 2):
                dve.tensor_scalar(h_t[:, k, 0:SEQ], h_t[:, k, 0:SEQ], cols[:, 0, k % 2, k // 2, 0:1],
                                  cols[:, 1, k % 2, k // 2, 0:1], ALU.mult, ALU.add).then_inc(h_modulated, 1)
            for half in range(KT // Q):
                v = h_t[:, :, SEQ:NTOK].rearrange("p (q h) (s t) -> p h q s t", q=Q, t=DEC_T)[:, half]
                a_, s_ = [cols[:, i, half, :, 1:NC].unsqueeze(3).to_broadcast([P, Q, DEC_B, DEC_T]) for i in range(2)]
                step(dve.tensor_tensor(v, v, a_, ALU.mult))
                dve.tensor_tensor(v, v, s_, ALU.add).then_inc(h_modulated, 1)

            def windows(src_, n, ext, buf):
                cur, w, i = src_, 1, 0
                while w < n:
                    o = buf[i % 2]
                    step(dve.tensor_tensor(o[..., 2 * w - 1:ext], cur[..., 2 * w - 1:ext],
                                           cur[..., w - 1:ext - w], ALU.add))
                    cur, w, i = o, 2 * w, i + 1
                return cur

            dve.wait_ge(consts, CONSTS)
            dve.wait_ge(tp_free, TP["st"] + 1)
            for g, w in enumerate(WINDOWS):
                dve.wait_ge(z_evac, 2 * (g + 1))
                s = windows(uext[:, g, :], w, PAST + SEQ, [wsum[0][:, :], wsum[1][:, :]])
                step(dve.scalar_tensor_tensor(out=pooled[:, g, w - 1:SEQ], in0=s[:, PAST + w - 1:PAST + SEQ],
                                              scalar=1.0 / w, in1=uext[:, g, PAST + w - 1:PAST + SEQ],
                                              op0=ALU.mult, op1=ALU.subtract))
                step(dve.tensor_tensor(s[:, PAST:PAST + w - 1], s[:, PAST:PAST + w - 1], inv_n[:, 0:w - 1], ALU.mult))
                dve.tensor_tensor(pooled[:, g, 0:w - 1], s[:, PAST:PAST + w - 1], uext[:, g, PAST:PAST + w - 1],
                                  ALU.subtract).then_inc(pooled_ready, 1)
                dve.wait_ge(pooled_ready, g + 1)
            dve.wait_ge(bias_hi, 3)
            for m in range(3):
                dve.tensor_tensor(bias_t[m][E:2 * E, :], b_raw[m][E:2 * E, :],
                                  bias_t[m][E:2 * E, :].bitcast(F32), ALU.subtract).then_inc(bias_ready, 1)
            add_ada(G1)
            for g in range(GR):
                f = 2 * GR + g
                dve.wait_ge(z_done, f + 1)
                dve.wait_ge(z_evac, 2 * 2 * GR)
                dve.tensor_tensor(vext[:, g, CPAST:CPAST + SEQ].rearrange("p (b n) -> p b n", b=2), z_prompt[f % 2],
                                  gate_c[:, g, 0:SEQ].rearrange("p (b n) -> p b n", b=2), ALU.mult)\
                    .then_inc(v_ready, 1)
                dve.tensor_tensor(vext_s[:, g, :, CPAST:CPAST + DEC_T], z_sample[f % 2],
                                  gate_c[:, g, SEQ:NTOK].rearrange("p (s t) -> p s t", t=DEC_T), ALU.mult)\
                    .then_inc(v_s_ready, 1)
            add_ada(SH2)
            add_ada(SC2)
            scale_rows(SC2, n2_rows)

            def taps(v, y, b, g, ready):
                n = y.shape[-1]
                tap = [par[:, (1 + j) * GR + g:(1 + j) * GR + g + 1] for j in range(3)]
                step(dve.tensor_scalar(y, v[..., 0:n], tap[0], None, ALU.mult))
                step(dve.scalar_tensor_tensor(out=y, in0=v[..., 1:1 + n], scalar=tap[1], in1=y,
                                              op0=ALU.mult, op1=ALU.add))
                step(dve.scalar_tensor_tensor(out=y, in0=v[..., 2:2 + n], scalar=tap[2], in1=y,
                                              op0=ALU.mult, op1=ALU.add))
                if b is not None:
                    dve.tensor_tensor(y, y, b, ALU.mult).then_inc(ready, 1)

            add_ada(G2)
            dve.wait_ge(z_done, 4 * GR)
            dve.wait_ge(v_ready, GR)
            for g in range(GR):
                dve.wait_ge(z_evac, 2 * (2 * GR + g + 1))
                taps(vext[:, g, :], conv[:, g, 0:SEQ], gate_b[:, g, 0:SEQ], g, conv_ready)
            bufs = [b[:, 0:DEC_B * (PAST + DEC_T)].rearrange("p (s r) -> p s r", s=DEC_B) for b in wsum]
            for g, w in enumerate(WINDOWS):
                s = windows(uext_s[:, g, :, :], w, PAST + DEC_T, bufs)
                dve.scalar_tensor_tensor(out=pooled[:, g, SEQ:NTOK].rearrange("p (s t) -> p s t", t=DEC_T),
                                         in0=s[:, :, PAST:PAST + DEC_T], scalar=1.0 / w,
                                         in1=uext_s[:, g, :, PAST:PAST + DEC_T],
                                         op0=ALU.mult, op1=ALU.subtract).then_inc(pooled_s_ready, 1)
                dve.wait_ge(pooled_s_ready, g + 1)
            dve.wait_ge(v_s_ready, GR)

            def by_seq(t_):
                return t_.rearrange("p (s t) -> p s t", t=DEC_T)

            for g in range(GR):
                taps(vext_s[:, g, :, :], by_seq(conv[:, g, SEQ:NTOK]), by_seq(gate_b[:, g, SEQ:NTOK]), g, conv_s_ready)

            def best(t):
                r = norm_rows(t)
                dve.wait_ge(lg_done, t + 1)
                dve.tensor_tensor(logit[0:r, t, :], lg[t], br_bc[0:r, :], ALU.add).then_inc(logits_in, 1)
                dve.wait_ge(logits_in, t + 1)
                step(dve.max(top_v[0:r, t, :], logit[0:r, t, :]))
                step(dve.max_index(top_i[0:r, t, :], top_v[0:r, t, :], logit[0:r, t, :]))
                step(dve.tensor_copy(top_f[0:r, t, :], top_i[0:r, t, 0:TOPK]))
                step(dve.tensor_tensor(onehot[0:r, t, :, :], iota_e[0:r, :].unsqueeze(1).to_broadcast([r, TOPK, E]),
                                       top_f[0:r, t, :].unsqueeze(2).to_broadcast([r, TOPK, E]), ALU.is_equal))
                with nc.allow_low_precision("zeros and ones are exact"):
                    step(dve.tensor_reduce(mask_bf[0:r, t, :], onehot[0:r, t, :, :].rearrange("p k e -> p e k"),
                                           AX.X, ALU.add))

            dve.wait_ge(tp_free, TP["s2"] + 1)
            for t in range(TT):
                r = norm_rows(t)
                if t == 2:
                    dve.wait_ge(pool_step, POOL_STEPS)
                    dve.wait_ge(pm_ready, 2 * GR)
                    step(dve.memset(onehot[:, PT, :, :], 0.0))
                    step(dve.memset(mask_bf[:, PT, :], 0.0))
                if t >= 2:
                    best(t - 2)
                dve.wait_ge(mix_done, t + 1)
                g1 = (g1_bc if t < PT else g1_bc_s)[0:r, :]
                m = mixp[t % 2][0:r, :, :].rearrange("p b n -> p (b n)")
                h = h_row[t % 2][0:r, :]
                if t >= 2:
                    dve.wait_ge(tp_full, TP[f"h{t - 2}"] + 1)
                    dve.wait_ge(h2_stored[t % 2], 16 * (t // 2))
                step(dve.tensor_tensor(h, m, g1, ALU.mult))
                dve.tensor_tensor(x_sb[0:r, t, :], x_sb[0:r, t, :], h, ALU.add).then_inc(x1_ready, 1)
                if t == PT:
                    best(PT - 1)
                dve.wait_ge(sq_done, t + 2)
                step(dve.reciprocal(rstd[0:r, t:t + 1], ss[0:r, t:t + 1]))
                if t == PT:
                    dve.wait_ge(tp_free, TP["s2_s"] + 1)
                sc = a2_bc if t < PT else a2_bc_s
                normalise(t, sc[0:r, 0, :], sc[0:r, 1, :])

            best(PT)
            dve.tensor_tensor(gates[:, :, :], top_v[:, :, 0:TOPK], top_v[:, :, 0:1].to_broadcast([P, TT, TOPK]),
                              ALU.subtract).then_inc(shifted, 1)
            dve.sem_inc(mask_ready, 1)

            dve.wait_ge(rank_done, 1)
            step(dve.memset(rank_m[:, :, E:E + 1], -1.0))
            step(dve.scalar_tensor_tensor(out=slot_e[:, :, :], in0=rank_ps, scalar=1.0, in1=mask_bf[:, :, :],
                                          op0=ALU.add, op1=ALU.mult))
            step(dve.tensor_scalar(rank_m[:, :, 0:E], slot_e[:, :, :], -1.0, None, ALU.add))
            step(dve.tensor_copy(cnt[:, :], cnt_ps))
            incl, nb, ov_incl = [t_[:, :] for t_ in small]
            step(dve.tensor_tensor_scan(incl, ones_e[:, :], cnt[:, :], 0.0, ALU.mult, ALU.add))
            step(dve.tensor_tensor(start[:, :], incl, cnt[:, :], ALU.subtract))
            step(dve.tensor_scalar(skip[:, 0:E], cnt[:, :], p_col[:, 0:1], float(SKIP), ALU.is_le, ALU.mult))
            step(dve.memset(skip[:, E:E + 1], float(SKIP)))
            step(dve.scalar_tensor_tensor(out=y_row[:, :], in0=start[:, :], scalar=p_col[:, 0:1], in1=skip[:, 0:E],
                                          op0=ALU.add, op1=ALU.add))
            step(dve.tensor_tensor(slot_e[:, :, :], rank_ps, start[:, :].unsqueeze(1).to_broadcast([P, TT, E]),
                                   ALU.add))
            step(dve.tensor_tensor(pick, onehot, slot_e[:, :, :].unsqueeze(2).to_broadcast([P, TT, TOPK, E]),
                                   ALU.mult))
            step(dve.tensor_reduce(slot_f[:, :, :], pick, AX.X, ALU.add))
            step(dve.tensor_copy(slot_i[:, :, :], slot_f[:, :, :]))
            step(dve.tensor_scalar(nb, cnt[:, :], float(P), None, ALU.is_gt))
            for k in range(2, EXTRA + 1):
                step(dve.scalar_tensor_tensor(out=nb, in0=cnt[:, :], scalar=float(k * P), in1=nb,
                                              op0=ALU.is_gt, op1=ALU.add))
            step(dve.tensor_tensor_scan(ov_incl, ones_e[:, :], nb, 0.0, ALU.mult, ALU.add))
            step(dve.tensor_copy(n_ov_i[:, :], ov_incl[:, E - 1:E]))
            step(dve.tensor_tensor(ov_cmp, ov_incl.unsqueeze(1).to_broadcast([P, MAX_OV, E]),
                                   iota_j[:, :].unsqueeze(2).to_broadcast([P, MAX_OV, E]), ALU.is_le))
            step(dve.tensor_reduce(ov_expert[:, :], ov_cmp, AX.X, ALU.add))
            step(dve.tensor_scalar(ov_expert[:, :], ov_expert[:, :], float(E - 1), None, ALU.min))
            step(dve.tensor_copy(ov_expert_i[:, :], ov_expert[:, :]))
            step(dve.tensor_tensor(ov_cmp, ov_cmp, nb.unsqueeze(1).to_broadcast([P, MAX_OV, E]), ALU.mult))
            step(dve.tensor_reduce(ov_base[:, :], ov_cmp, AX.X, ALU.add))
            step(dve.tensor_tensor(ov_base[:, :], iota_j[:, :], ov_base[:, :], ALU.subtract))
            step(dve.tensor_scalar(ov_base[:, :], ov_base[:, :], 1.0, float(P), ALU.add, ALU.mult))
            dve.wait_ge(exp_done, 1)
            step(dve.tensor_reduce(e_sum[:, :], gates[:, :, :], AX.X, ALU.add))
            step(dve.reciprocal(e_sum[:, :], e_sum[:, :]))
            step(dve.tensor_tensor(gates[:, :, :], gates[:, :, :],
                                   e_sum[:, :].unsqueeze(2).to_broadcast([P, TT, TOPK]), ALU.mult))

        @block.tensor
        def _(pe):
            def chunk(kind, k):
                n = at[(kind, k)]
                pe.wait_ge(raw_loaded[n % SLOTS], 16 * (n // SLOTS + 1))
                return chunk_view(n)

            def ada(p):
                w = [chunk("ada", Q * p + q) for q in range(Q)]
                if ADA_AT[p]:
                    pe.wait_ge(ada_added, ADA_AT[p])
                for k in range(KT):
                    for q in range(Q):
                        mm = pe.matmul(modp[q * CPAD:(q + 1) * CPAD, :], c_act[:, k, :], w[q][:, k, :],
                                       start=(k == 0), stop=(k == KT - 1))
                mm.then_inc(ada_done, 1)

            def spread(samples, p, dst):
                sel, r = (sel_s, NS) if samples else (sel_p, P)
                for q in range(Q):
                    mm = pe.matmul(dst[0:r, q // 2, (q % 2) * QW:(q % 2 + 1) * QW], sel[:, q, :],
                                   mod[:, p * QW:(p + 1) * QW], start=True, stop=True)
                return mm

            def take(name):
                if TP[name]:
                    pe.wait_ge(tp_free, TP[name])

            def transposes(name, t, base):
                take(name)
                pe.wait_ge(h_ready, base + t + 1)
                r = norm_rows(t)
                for k in range(KT):
                    mm = pe.transpose(tp[:, k // 4, (k % 4) * P:(k % 4) * P + r],
                                      h_row[t % 2][0:r, k * P:(k + 1) * P], ident[0:r, 0:r])
                mm.then_inc(tp_full, 1)

            pe.wait_ge(c_loaded, 32)
            pe.wait_ge(pool_step, 2)
            for k in range(KT):
                mm = pe.transpose(c_ps[:, k, :], c_rows[:, k * P:(k + 1) * P], ident[0:NC, 0:NC])
            mm.then_inc(tp_full, 1)
            pe.wait_ge(c_ready, 1)
            for t in range(2):
                transposes(f"n{t}", t, 0)
            ada(SH1)
            for t in range(2, TT):
                transposes(f"n{t}", t, 0)
            pe.wait_ge(small_loaded, 16 * 7)
            take("par")
            pe.transpose(tp[:, 0, 0:4 * GR], par_rows[:, :], ident[0:4 * GR, 0:4 * GR]).then_inc(tp_full, 1)
            take("st")
            for g in range(GR):
                n = DEC_B * PAST
                pe.transpose(tp[:, 0, g * n:(g + 1) * n], sp_rows[:, g * P:(g + 1) * P], ident[0:n, 0:n])
            for g in range(GR):
                n = DEC_B * CPAST
                mm = pe.transpose(tp[:, 1, g * n:(g + 1) * n], sc_rows[:, g * P:(g + 1) * P], ident[0:n, 0:n])
            mm.then_inc(tp_full, 1)
            ada(SC1)
            take("cols")
            pe.wait_ge(scale_ready, 1)
            for i, p in enumerate((SC1, SH1)):
                for half in range(KT // Q):
                    j, col = i * (KT // Q) + half, p * QW + half * P
                    mm = pe.transpose(tp[:, 0, j * P:(j + 1) * P], mod[:, col:col + P], ident[:, :])
            mm.then_inc(tp_full, 1)
            pe.wait_ge(h_modulated, KT + KT // Q)

            def project(k):
                w = chunk("in", k)
                for f in (2 * k, 2 * k + 1):
                    if 2 * GR + 2 <= f < 3 * GR + 2:
                        pe.wait_ge(v_ready, f - 2 * GR - 1)
                        pe.wait_ge(v_s_ready, f - 2 * GR - 1)
                    elif f >= 2:
                        pe.wait_ge(z_evac, 2 * (f - 1 if f < 2 * GR + 2 else f - 1 - GR))
                    for b, (lo_, hi_) in enumerate(((0, PH), (PH, NTOK))):
                        for j in range(KT):
                            mm = pe.matmul(zt[f % 2][:, b, 0:hi_ - lo_], w[:, j, (f % 2) * P:(f % 2 + 1) * P],
                                           h_t[:, j, lo_:hi_], start=(j == 0), stop=(j == KT - 1))
                    mm.then_inc(z_done, 1)

            for k in range(4):
                project(k)
            ada(G1)
            project(4)
            project(5)
            ada(SH2)
            take("g1")
            pe.wait_ge(pool_step, 9)
            spread(False, G1, tp).then_inc(tp_full, 1)
            project(6)
            ada(SC2)
            take("g1_s")
            spread(True, G1, tp).then_inc(tp_full, 1)
            project(7)
            ada(G2)
            take("a2")
            pe.wait_ge(scale_ready, 2)
            spread(False, SC2, tp).then_inc(tp_full, 1)
            pe.wait_ge(pooled_ready, GR)
            for g in range(GR):
                pe.wait_ge(z_evac, 2 * (3 * GR - 1 + g // 2))
                pe.matmul(pm_p[g], wpool_sb[:, g, :], pooled[:, g, 0:SEQ], start=True, stop=True).then_inc(pm_done, 1)
            take("s2")
            spread(False, SH2, tp).then_inc(tp_full, 1)

            def mix(t):
                r, out_ = norm_rows(t), mixp[t % 2]
                if t >= 2:
                    pe.wait_ge(x1_ready, t - 1)
                for j in list(range(GR, 2 * GR)) + list(range(GR)):
                    w = chunk("out", j // KC)
                    for h in range(2):
                        mm = pe.matmul(out_[0:r, h, :], mix_t[:, j, t * P:t * P + r],
                                       w[:, j % KC, h * HALF:(h + 1) * HALF], start=(j == GR), stop=(j == GR - 1))
                mm.then_inc(mix_done, 1)

            def router(t):
                r = norm_rows(t)
                pe.wait_ge(tp_free, TP[f"h{t}"] + 1)
                out_ = lg[t]
                if t >= 2:
                    pe.wait_ge(logits_in, t - 1)
                for k in range(KT):
                    mm = pe.matmul(out_, h_t[:, k, t * P:t * P + r], wr_sb[:, k, :],
                                   start=(k == 0), stop=(k == KT - 1))
                mm.then_inc(lg_done, 1)

            pe.wait_ge(pm_ready, GR)
            pe.wait_ge(conv_ready, GR)
            mix(0)
            take("pm_s")
            pe.wait_ge(pooled_s_ready, GR)
            for g in range(GR):
                mm = pe.matmul(tp[:, 0, g * NS:(g + 1) * NS], wpool_sb[:, g, :], pooled[:, g, SEQ:NTOK],
                               start=True, stop=True)
            mm.then_inc(tp_full, 1)
            mix(1)
            pe.wait_ge(ada_added, PARTS)
            transposes("h0", 0, TT)
            router(0)
            take("a2_s")
            spread(True, SC2, tp).then_inc(tp_full, 1)
            mix(2)
            transposes("h1", 1, TT)
            router(1)
            take("s2_s")
            spread(True, SH2, tp).then_inc(tp_full, 1)
            mix(3)
            transposes("h2", 2, TT)
            router(2)
            pe.wait_ge(pm_ready, 2 * GR)
            pe.wait_ge(conv_s_ready, GR)
            take("so0")
            for g in range(GR):
                pe.transpose(tp[0:PAST, 0, g * P:(g + 1) * P], uext[:, g, SEQ:SEQ + PAST], ident[:, :])
            for g in range(GR):
                mm = pe.transpose(tp[0:CPAST, 1, g * P:(g + 1) * P], vext[:, g, SEQ:SEQ + CPAST], ident[:, :])
            mm.then_inc(tp_full, 1)
            mix(4)
            transposes("h3", 3, TT)
            router(3)
            pe.wait_ge(new_packed, 4)
            take("so1")
            for g in range(GR):
                pe.transpose(tp[0:NS, 0, g * P:(g + 1) * P], u_new[:, g, :], ident[:, :])
            for g in range(GR):
                mm = pe.transpose(tp[0:DEC_B * CPAST, 1, g * P:(g + 1) * P], v_new[:, g, :], ident[:, :])
            mm.then_inc(tp_full, 1)
            transposes("h4", 4, TT)
            router(4)
            pe.wait_ge(mask_ready, 1)
            for t in range(TT):
                pe.matmul(rank_ps[:, t, :], tri[:, :], mask_bf[:, t, :], start=True, stop=(t == 0))
                for b in range(t):
                    pe.matmul(rank_ps[:, t, :], ones_bf[:, :], mask_bf[:, b, :], start=False, stop=(b == t - 1))
            for t in range(TT):
                mm = pe.matmul(cnt_ps, ones_bf[:, :], mask_bf[:, t, :], start=(t == 0), stop=(t == TT - 1))
            mm.then_inc(rank_done, 1)

        part.close()

        NCH = 3 * MCH
        TOTAL = E * NCH

        def pos(i, c):
            if isinstance(i, int) and i == 0:
                return c
            if isinstance(i, int) and i == E:
                return NCH * E - MCH + c - 2 * MCH
            return i * NCH + (c - MCH)

        def ring(i, c, n):
            return (pos(i, c) if isinstance(i, int) else pos(1, c)) % n

        assert NCH % SLOTS == 0 and NCH % SPLIT == 0

        def loaded_value(i, c):
            if isinstance(i, int):
                return 16 * ((DENSE_CH + pos(i, c)) // SLOTS + 1)
            base = (DENSE_CH + pos(1, c)) // SLOTS + 1
            return (i - 1) * (16 * NCH // SLOTS) + 16 * base

        with ExitStack() as experts:
            def sb(name, shape, dt=F32):
                return experts.enter_context(nc.sbuf_tensor(name, shape, dt))

            w_hi = [sb(f"w_hi{s}", [P, SLOT_F], F32R) for s in range(SPLIT)]
            w_lo = [sb(f"w_lo{s}", [P, SLOT_F], F32R) for s in range(SPLIT)]
            rows = sb("rows", [P, D])
            ht_hi = sb("ht_hi", [P, KT, P], F32R)
            ht_lo = sb("ht_lo", [P, KT, P], F32R)
            at_hi = sb("at_hi", [P, KT, P], F32R)
            at_lo = sb("at_lo", [P, KT, P], F32R)
            g_sb = sb("g_sb", [P, D])
            s_sb = sb("s_sb", [P, D])
            u_sb = sb("u_sb", [P, D])
            a_sb = sb("a_sb", [P, D])
            y_sb = sb("y_sb", [P, D])
            member = sb("member", [P, TT, P], BF16)
            row_id = sb("row_id", [P, 1], U32)
            y_idx = sb("y_idx", [P, 1], U32)
            sel_gu = sb("sel_gu", [2 * E, P], F32R)
            sel_d = sb("sel_d", [2 * E, P], F32R)

            hi_ready = sem("hi_ready")
            lo_ready = sem("lo_ready")
            mm_done = sem("mm_done")
            member_ready = sem("member_ready")
            id_done = sem("id_done")
            id_ready = sem("id_ready")
            row_gathered = sem("row_gathered")
            row_tp = sem("row_tp")
            ht_hi_ready = sem("ht_hi_ready")
            ht_lo_ready = sem("ht_lo_ready")
            g_clipped = sem("g_clipped")
            sig_done = sem("sig_done")
            u_clipped = sem("u_clipped")
            u_plus = sem("u_plus_one")
            glu_done = sem("glu_done")
            act_ready = sem("act_ready")
            act_tp = sem("act_tp")
            at_hi_ready = sem("at_hi_ready")
            at_lo_ready = sem("at_lo_ready")
            sel_gu_ready = sem("sel_gu_ready")
            sel_d_ready = sem("sel_d_ready")
            y_idx_ready = sem("y_idx_ready")
            y_copied = sem("y_copied")
            rows_filled = sem("rows_filled")
            y_stored = sem("y_stored")

            flat = lambda t: t[:, :, :].rearrange("p b n -> p (b n)")
            tp_flat, g_ps, u_ps, y_ps = flat(tp), flat(acc_g), flat(acc_u), flat(acc_y)

            block2 = experts.enter_context(nc.Block())

            @block2.sync
            def _(sp):
                def load(i, c):
                    n = pos(i, c)
                    s = ring(i, c, SLOTS)
                    kind = "gud"[c // MCH]
                    sp.wait_ge(lo_ready, n - (SLOTS - 1))
                    sp.dma_start(raw[s][:, :].rearrange("p (k n) -> p k n", k=KC),
                                 expert_src(kind, i - (kind == "d"), c % MCH)).then_inc(raw_loaded[s], 16)

                for c in range(SLOTS, 2 * MCH):
                    load(0, c)
                with sp.Fori(1, E) as i:
                    for c in range(NCH):
                        load(i, c)
                for c in range(2 * MCH, NCH):
                    load(E, c)

            @block2.gpsimd
            def _(pool):
                pool.memset(rows[:, :], 0.0).then_inc(rows_filled, 1)
                pool.wait_ge(rows_filled, 1)

                def gather(e):
                    pool.wait_ge(id_ready, e + 1)
                    if not (isinstance(e, int) and e == 0):
                        pool.wait_ge(row_tp, e)
                    if not isinstance(e, int):
                        pool.nop(nofuse=True)
                    pool.indirect_dma_start(rows[:, :], None, h2_dram,
                                            bass.IndirectOffsetOnAxis(ap=row_id[:, 0:1], axis=0),
                                            bounds_check=NTOK - 1, oob_is_err=False).then_inc(row_gathered, 16)

                def scatter(e):
                    pool.wait_ge(y_copied, e + 1)
                    pool.wait_ge(y_idx_ready, e + 1)
                    if not isinstance(e, int):
                        pool.nop(nofuse=True)
                    pool.indirect_dma_start(y_dram, bass.IndirectOffsetOnAxis(ap=y_idx[:, 0:1], axis=0),
                                            y_sb[:, :], None, bounds_check=ROWS - 1, oob_is_err=False)\
                        .then_inc(y_stored, 16)

                def gate(e):
                    pool.wait_ge(sig_done, e + 1)
                    pool.tensor_tensor(g_sb[:, :], g_sb[:, :], s_sb[:, :], ALU.mult).then_inc(glu_done, 1)
                    pool.wait_ge(u_clipped, e + 1)
                    if not isinstance(e, int):
                        pool.nop(nofuse=True)
                    pool.tensor_scalar(u_sb[:, :], u_sb[:, :], 1.0, None, ALU.add).then_inc(u_plus, 1)
                    pool.wait_ge(glu_done, e + 1)
                    pool.wait_ge(u_plus, e + 1)
                    if not (isinstance(e, int) and e == 0):
                        pool.wait_ge(act_tp, e)
                    pool.tensor_tensor(a_sb[:, :], u_sb[:, :], g_sb[:, :], ALU.mult).then_inc(act_ready, 1)

                def step(i):
                    if not (isinstance(i, int) and i == E - 1):
                        gather(i + 1)
                    if not (isinstance(i, int) and i < 2):
                        scatter(i - 2)
                    gate(i)

                gather(0)
                step(0)
                step(1)
                with pool.Fori(2, E - 1) as i:
                    step(i)
                step(E - 1)
                scatter(E - 2)
                scatter(E - 1)
                pool.wait_ge(y_stored, 16 * E)

            @block2.scalar
            def _(act):
                def hi(i, c):
                    n = pos(i, c)
                    act.wait_ge(raw_loaded[ring(i, c, SLOTS)], loaded_value(i, c))
                    if not isinstance(n, int) or n >= SPLIT:
                        act.wait_ge(mm_done, n - (SPLIT - 1))
                    act.activation(w_hi[ring(i, c, SPLIT)][:, :], raw[ring(i, c, SLOTS)][:, :], ACT.Copy)\
                        .then_inc(hi_ready, 1)

                def y_out(e):
                    act.wait_ge(mm_done, pos(e + 2, 0) if not (isinstance(e, int) and e >= E - 2) else
                                NCH * (e + 2) - MCH if e == E - 2 else TOTAL)
                    if not (isinstance(e, int) and e == 0):
                        act.wait_ge(y_stored, 16 * e)
                    act.activation(y_sb[:, :], y_ps, ACT.Copy).then_inc(y_copied, 1)
                    col = y_row[:, e:e + 1] if isinstance(e, int) else y_row[:, bass.ds(e, 1)]
                    act.activation(y_idx[:, :], col, ACT.Copy).then_inc(y_idx_ready, 1)

                def turn_hi(e):
                    act.wait_ge(row_tp, e + 1)
                    act.activation(flat(ht_hi), tp_flat, ACT.Copy).then_inc(ht_hi_ready, 1)

                def act_hi(e):
                    act.wait_ge(act_tp, e + 1)
                    act.activation(flat(at_hi), tp_flat, ACT.Copy).then_inc(at_hi_ready, 1)

                def sigmoid(e):
                    act.wait_ge(g_clipped, e + 1)
                    act.activation(s_sb[:, :], g_sb[:, :], ACT.Sigmoid, scale=ALPHA).then_inc(sig_done, 1)

                def step(i, last=False):
                    first = isinstance(i, int) and i == 0
                    hi(i, 3)
                    if not (isinstance(i, int) and i < 2):
                        y_out(i - 2)
                    for c in range(4, 8):
                        hi(i, c)
                    if not first:
                        act_hi(i - 1)
                    sigmoid(i)
                    if not first:
                        for c in range(8, NCH):
                            hi(i, c)
                    lead = 2 * MCH if last else 0
                    hi(i + 1, lead)
                    hi(i + 1, lead + 1)
                    if not last:
                        turn_hi(i + 1)
                    hi(i + 1, lead + 2)

                for c in range(3):
                    hi(0, c)
                turn_hi(0)
                step(0)
                step(1)
                step(2)
                with act.Fori(3, E - 1) as i:
                    step(i)
                step(E - 1, last=True)
                hi(E, NCH - 1)
                y_out(E - 2)
                act_hi(E - 1)
                y_out(E - 1)

            @block2.vector
            def _(dve):
                def lo(i, c):
                    dve.wait_ge(hi_ready, pos(i, c) + 1)
                    s = ring(i, c, SPLIT)
                    dve.tensor_tensor(w_lo[s][:, :], raw[ring(i, c, SLOTS)][:, :], w_hi[s][:, :].bitcast(F32),
                                      ALU.subtract).then_inc(lo_ready, 1)

                def members(e):
                    if not (isinstance(e, int) and e == 0):
                        dve.wait_ge(id_done, e)
                    col = rank_m[:, :, e:e + 1] if isinstance(e, int) else rank_m[:, :, bass.ds(e, 1)]
                    dve.tensor_tensor(member[:, :, :], iota_m[:, :].unsqueeze(1).to_broadcast([P, TT, P]),
                                      col.to_broadcast([P, TT, P]), ALU.is_equal).then_inc(member_ready, 1)

                def ids(e):
                    dve.wait_ge(id_done, e + 1)
                    if not (isinstance(e, int) and e == 0):
                        dve.wait_ge(row_gathered, 16 * e)
                    col = skip[:, e:e + 1] if isinstance(e, int) else skip[:, bass.ds(e, 1)]
                    dve.scalar_tensor_tensor(out=row_id[:, :], in0=y_ps[:, 0:1], scalar=y_ps[:, 1:2], in1=col,
                                             op0=ALU.add, op1=ALU.add).then_inc(id_ready, 1)

                def select(out_, e, done):
                    col = expert_id2[:, e:e + 1] if isinstance(e, int) else expert_id2[:, bass.ds(e, 1)]
                    dve.tensor_scalar(out_[:, :], col.to_broadcast([2 * E, P]), pmod[:, 0:1], None, ALU.is_equal)\
                        .then_inc(done, 1)

                def turn_lo(e):
                    dve.wait_ge(ht_hi_ready, e + 1)
                    dve.tensor_tensor(flat(ht_lo), tp_flat, flat(ht_hi).bitcast(F32), ALU.subtract)\
                        .then_inc(ht_lo_ready, 1)

                def act_lo(e):
                    dve.wait_ge(at_hi_ready, e + 1)
                    dve.tensor_tensor(flat(at_lo), tp_flat, flat(at_hi).bitcast(F32), ALU.subtract)\
                        .then_inc(at_lo_ready, 1)
                    select(sel_d, e, sel_d_ready)

                def step(i, last=False):
                    first = isinstance(i, int) and i == 0
                    lo(i, 3)
                    if not last:
                        members(i + 2)
                    for c in range(4, 7):
                        lo(i, c)
                    dve.wait_ge(mm_done, pos(i, 3) + 1)
                    if not first:
                        dve.wait_ge(act_ready, i)
                    dve.tensor_scalar(g_sb[:, :], g_ps, LIMIT, None, ALU.min).then_inc(g_clipped, 1)
                    lo(i, 7)
                    if not first:
                        act_lo(i - 1)
                    if not last:
                        ids(i + 2)
                    if not first:
                        lo(i, 8)
                        lo(i, 9)
                        lo(i, 10)
                    dve.wait_ge(mm_done, pos(i, 7) + 1)
                    dve.tensor_scalar(u_sb[:, :], u_ps, LIMIT, -LIMIT, ALU.min, ALU.max).then_inc(u_clipped, 1)
                    if not first:
                        lo(i, 11)
                    if not last:
                        select(sel_gu, i + 1, sel_gu_ready)
                    lead = 2 * MCH if last else 0
                    lo(i + 1, lead)
                    lo(i + 1, lead + 1)
                    if not last:
                        turn_lo(i + 1)
                    lo(i + 1, lead + 2)

                members(0)
                ids(0)
                members(1)
                for c in range(3):
                    lo(0, c)
                select(sel_gu, 0, sel_gu_ready)
                ids(1)
                turn_lo(0)
                step(0)
                with dve.Fori(1, E - 1) as i:
                    step(i)
                step(E - 1, last=True)
                act_lo(E - 1)
                lo(E, NCH - 1)

            @block2.tensor
            def _(pe):
                def row_ids(e):
                    pe.wait_ge(member_ready, e + 1)
                    for t in range(TT):
                        mm = pe.matmul(y_ps[:, 0:2], member[:, t, :], tok_bf[:, t, :], start=(t == 0),
                                       stop=(t == TT - 1))
                    mm.then_inc(id_done, 1)

                def turn(src_, done):
                    for k in range(KT):
                        mm = pe.transpose(tp_flat[:, k * P:(k + 1) * P], src_[:, k * P:(k + 1) * P], ident[:, :])
                    mm.then_inc(done, 1)

                def turn_rows(e):
                    pe.wait_ge(row_gathered, 16 * (e + 1))
                    turn(rows, row_tp)

                def bias(out_, sel, table):
                    for h in range(2):
                        pe.matmul(out_[:, h * HALF:(h + 1) * HALF], sel[:, :], table[:, h * HALF:(h + 1) * HALF],
                                  start=True, stop=False)

                def product(i, c, x_hi, x_lo, out_):
                    pe.wait_ge(lo_ready, pos(i, c) + 1)
                    s = ring(i, c, SPLIT)
                    wh = w_hi[s][:, :].rearrange("p (k h n) -> p k h n", k=KC, h=2)
                    wl = w_lo[s][:, :].rearrange("p (k h n) -> p k h n", k=KC, h=2)
                    for kk in range(KC):
                        k = (c % MCH) * KC + kk
                        for x, w in ((x_hi, wh), (x_hi, wl), (x_lo, wh)):
                            for h in range(2):
                                mm = pe.matmul(out_[:, h * HALF:(h + 1) * HALF], x[:, k, :], w[:, kk, h, :],
                                               start=False, stop=(k == KT - 1 and x is x_lo))
                    mm.then_inc(mm_done, 1)

                def gate_up(i, last=False):
                    first = isinstance(i, int) and i == 0
                    pe.wait_ge(ht_lo_ready, i + 1)
                    pe.wait_ge(sel_gu_ready, i + 1)
                    if not first:
                        pe.wait_ge(g_clipped, i)
                    bias(g_ps, sel_gu, bias_t[0])
                    for c in range(0, MCH):
                        product(i, c, ht_hi, ht_lo, g_ps)
                    if not first:
                        pe.wait_ge(act_ready, i)
                        turn(a_sb, act_tp)
                    if not last:
                        if isinstance(i, int) and i < 2:
                            pe.wait_ge(id_ready, i + 2)
                        else:
                            pe.wait_ge(y_copied, i - 1)
                        row_ids(i + 2)
                    if not first:
                        pe.wait_ge(u_clipped, i)
                    bias(u_ps, sel_gu, bias_t[1])
                    for c in range(MCH, 2 * MCH):
                        product(i, c, ht_hi, ht_lo, u_ps)

                def down(i, rows_follow=True):
                    pe.wait_ge(at_lo_ready, i)
                    pe.wait_ge(sel_d_ready, i)
                    if rows_follow:
                        pe.wait_ge(id_ready, i + 3)
                    else:
                        pe.wait_ge(y_copied, i - 1)
                    bias(y_ps, sel_d, bias_t[2])
                    for c in range(2 * MCH, NCH):
                        product(i, c, at_hi, at_lo, y_ps)
                        if c == 2 * MCH + 1 and rows_follow:
                            turn_rows(i + 1)

                row_ids(0)
                pe.wait_ge(id_ready, 1)
                row_ids(1)
                turn_rows(0)
                gate_up(0)
                turn_rows(1)
                gate_up(1)
                down(1)
                with pe.Fori(2, E - 1) as i:
                    gate_up(i)
                    down(i)
                gate_up(E - 1, last=True)
                down(E - 1, rows_follow=False)
                pe.wait_ge(act_ready, E)
                turn(a_sb, act_tp)
                down(E, rows_follow=False)

        LOADS = (DENSE_CH + TOTAL) // SLOTS
        with ExitStack() as extra:
            def sb(name, shape, dt=F32):
                return extra.enter_context(nc.sbuf_tensor(name, shape, dt))

            rows = sb("ov_rows", [P, D])
            ht = sb("ov_ht", [P, D])
            at_ = sb("ov_at", [P, D])
            g_sb = sb("ov_g", [P, D])
            s_sb = sb("ov_s", [P, D])
            u_sb = sb("ov_u", [P, D])
            y_sb = sb("ov_y", [P, D])
            member = sb("ov_member", [P, TT, P], BF16)
            row_id = sb("ov_row_id", [P, 1], U32)
            y_idx = sb("ov_y_idx", [P, 1], U32)
            rel = sb("ov_rel", [P, TT, 1])
            row_rank = sb("ov_row_rank", [P, 1])
            past_end = sb("ov_past_end", [P, 1])
            sel = sb("ov_sel", [2 * E, P], F32R)

            ov_chain = sem("ov_chain")
            ov_member = sem("ov_member_ready")
            ov_id_mm = sem("ov_id_mm")
            ov_id = sem("ov_id")
            ov_gathered = sem("ov_gathered")
            ov_row_tp = sem("ov_row_tp")
            ov_ht = sem("ov_ht_ready")
            ov_mm = sem("ov_mm")
            ov_g = sem("ov_g_clipped")
            ov_sig = sem("ov_sig")
            ov_act = sem("ov_act_ready")
            ov_act_tp = sem("ov_act_tp")
            ov_at = sem("ov_at_ready")
            ov_copied = sem("ov_copied")
            ov_done = sem("ov_done")

            def blocks(eng, body):
                n = eng.value_load(n_ov_i[0:1, 0:1], min_val=0, max_val=MAX_OV)
                with eng.If(n > 0):
                    with eng.Fori(0, MAX_OV) as j:
                        with eng.If(j < n):
                            body(j)
                            eng.wait_ge(ov_done, 16 * j + 16)
                            eng.nop(nofuse=True)

            block3 = extra.enter_context(nc.Block())
            ov_cleared = sem("ov_cleared")

            @block3.sync
            def _(sp):
                def body(j):
                    e = sp.value_load(ov_expert_i[0:1, bass.ds(j, 1)], min_val=0, max_val=E - 1)
                    for c in range(NCH):
                        if c >= SLOTS:
                            sp.wait_ge(ov_mm, NCH * j + (c - SLOTS + 1))
                        sp.dma_start(raw[c % SLOTS][:, :].rearrange("p (k n) -> p k n", k=KC),
                                     expert_src("gud"[c // MCH], e, c % MCH)).then_inc(raw_loaded[c % SLOTS], 16)
                blocks(sp, body)

            @block3.gpsimd
            def _(pool):
                pool.memset(rows[:, :], 0.0).then_inc(ov_cleared, 1)
                pool.wait_ge(ov_cleared, 1)

                def body(j):
                    pool.wait_ge(ov_id, j + 1)
                    pool.nop(nofuse=True)
                    pool.indirect_dma_start(rows[:, :], None, h2_dram,
                                            bass.IndirectOffsetOnAxis(ap=row_id[:, 0:1], axis=0),
                                            bounds_check=NTOK - 1, oob_is_err=False).then_inc(ov_gathered, 16)
                    pool.wait_ge(ov_copied, j + 1)
                    pool.nop(nofuse=True)
                    pool.indirect_dma_start(y_dram, bass.IndirectOffsetOnAxis(ap=y_idx[:, 0:1], axis=0),
                                            y_sb[:, :], None, bounds_check=ROWS - 1, oob_is_err=False)\
                        .then_inc(ov_done, 16)
                blocks(pool, body)

            @block3.scalar
            def _(act):
                def body(j):
                    act.wait_ge(ov_row_tp, j + 1)
                    act.activation(ht[:, :], tp_flat, ACT.Copy).then_inc(ov_ht, 1)
                    act.wait_ge(ov_g, j + 1)
                    act.activation(s_sb[:, :], g_sb[:, :], ACT.Sigmoid, scale=ALPHA).then_inc(ov_sig, 1)
                    act.wait_ge(ov_act_tp, j + 1)
                    act.activation(at_[:, :], tp_flat, ACT.Copy).then_inc(ov_at, 1)
                    act.wait_ge(ov_mm, NCH * j + NCH)
                    act.activation(y_sb[:, :], y_ps, ACT.Copy).then_inc(ov_copied, 1)
                blocks(act, body)

            @block3.vector
            def _(dve):
                CHAIN = 7

                def body(j):
                    k = 0

                    def step(ins):
                        nonlocal k
                        k += 1
                        ins.then_inc(ov_chain, 1)
                        dve.wait_ge(ov_chain, CHAIN * j + k)

                    e = dve.value_load(ov_expert_i[0:1, bass.ds(j, 1)], min_val=0, max_val=E - 1)
                    step(dve.tensor_scalar(rel[:, :, :], rank_m[:, :, bass.ds(e, 1)], ov_base[:, bass.ds(j, 1)], None,
                                           ALU.subtract))
                    step(dve.tensor_tensor(member[:, :, :], iota_m[:, :].unsqueeze(1).to_broadcast([P, TT, P]),
                                           rel[:, :, :].to_broadcast([P, TT, P]), ALU.is_equal))
                    step(dve.tensor_tensor(row_rank[:, :], p_col[:, :], ov_base[:, bass.ds(j, 1)], ALU.add))
                    step(dve.tensor_scalar(past_end[:, :], cnt[:, bass.ds(e, 1)], row_rank[:, 0:1], float(SKIP),
                                           ALU.is_le, ALU.mult))
                    step(dve.scalar_tensor_tensor(out=y_idx[:, :], in0=start[:, bass.ds(e, 1)],
                                                  scalar=row_rank[:, 0:1], in1=past_end[:, :],
                                                  op0=ALU.add, op1=ALU.add))
                    dve.tensor_scalar(sel[:, :], ov_expert[0:2 * E, bass.ds(j, 1)].to_broadcast([2 * E, P]),
                                      pmod[:, 0:1], None, ALU.is_equal).then_inc(ov_member, 1)
                    dve.wait_ge(ov_id_mm, j + 1)
                    dve.scalar_tensor_tensor(out=row_id[:, :], in0=y_ps[:, 0:1], scalar=y_ps[:, 1:2],
                                             in1=past_end[:, :], op0=ALU.add, op1=ALU.add).then_inc(ov_id, 1)
                    dve.wait_ge(ov_mm, NCH * j + MCH)
                    dve.tensor_scalar(g_sb[:, :], g_ps, LIMIT, None, ALU.min).then_inc(ov_g, 1)
                    dve.wait_ge(ov_mm, NCH * j + 2 * MCH)
                    step(dve.tensor_scalar(u_sb[:, :], u_ps, LIMIT, -LIMIT, ALU.min, ALU.max))
                    dve.wait_ge(ov_sig, j + 1)
                    step(dve.tensor_tensor(g_sb[:, :], g_sb[:, :], s_sb[:, :], ALU.mult))
                    dve.scalar_tensor_tensor(out=u_sb[:, :], in0=u_sb[:, :], scalar=1.0, in1=g_sb[:, :],
                                             op0=ALU.add, op1=ALU.mult).then_inc(ov_act, 1)
                    assert k == CHAIN
                blocks(dve, body)

            @block3.tensor
            def _(pe):
                def body(j):
                    pe.wait_ge(ov_member, j + 1)
                    for t in range(TT):
                        mm = pe.matmul(y_ps[:, 0:2], member[:, t, :], tok_bf[:, t, :], start=(t == 0),
                                       stop=(t == TT - 1))
                    mm.then_inc(ov_id_mm, 1)
                    pe.wait_ge(ov_gathered, 16 * j + 16)
                    for k in range(KT):
                        mm = pe.transpose(tp_flat[:, k * P:(k + 1) * P], rows[:, k * P:(k + 1) * P], ident[:, :])
                    mm.then_inc(ov_row_tp, 1)
                    pe.wait_ge(ov_ht, j + 1)
                    for c in range(NCH):
                        m = c // MCH
                        out_, x = (g_ps, u_ps, y_ps)[m], (ht, ht, at_)[m]
                        if c == 2 * MCH:
                            pe.wait_ge(ov_act, j + 1)
                            for k in range(KT):
                                mm = pe.transpose(tp_flat[:, k * P:(k + 1) * P], u_sb[:, k * P:(k + 1) * P],
                                                  ident[:, :])
                            mm.then_inc(ov_act_tp, 1)
                            pe.wait_ge(ov_at, j + 1)
                        if c % MCH == 0:
                            for h in range(2):
                                pe.matmul(out_[:, h * HALF:(h + 1) * HALF], sel[:, :],
                                          bias_t[m][:, h * HALF:(h + 1) * HALF], start=True, stop=False)
                        pe.wait_ge(raw_loaded[c % SLOTS],
                                   j * (16 * NCH // SLOTS) + 16 * (LOADS + c // SLOTS + 1))
                        w = raw[c % SLOTS][:, :].rearrange("p (k h n) -> p k h n", k=KC, h=2)
                        for kk in range(KC):
                            k = (c % MCH) * KC + kk
                            for h in range(2):
                                mm = pe.matmul(out_[:, h * HALF:(h + 1) * HALF], x[:, k * P:(k + 1) * P],
                                               w[:, kk, h, :], start=False, stop=(k == KT - 1))
                        mm.then_inc(ov_mm, 1)
                blocks(pe, body)

        with ExitStack() as final:
            def sb(name, shape, dt=F32):
                return final.enter_context(nc.sbuf_tensor(name, shape, dt))

            picked = [[sb(f"picked{b}_{k}", [P, D]) for k in range(TOPK)] for b in range(2)]
            ffn = [sb(f"ffn{b}", [P, D]) for b in range(2)]
            fn_bc = sb("fn_bc", [P, D])
            out_sb = [sb(f"out_sb{b}", [P, D]) for b in range(2)]
            fin_ss = sb("fin_ss", [P, TT])
            fin_rstd = sb("fin_rstd", [P, TT])

            fn_loaded = sem("fn_loaded")
            picked_in = [[sem(f"picked_in{b}_{k}") for k in range(TOPK)] for b in range(2)]
            fin_step = sem("fin_step")
            g2_spread = sem("g2_spread")
            first_scaled = sem("first_scaled")
            ffn_done = sem("ffn_done")
            x2_ready = sem("x2_ready")
            fin_sq = sem("fin_sq")
            fin_sqrt = sem("fin_sqrt")
            out_ready = sem("out_ready")
            out_stored = [sem(f"out_stored{b}") for b in range(2)]

            block4 = final.enter_context(nc.Block())

            @block4.sync
            def _(sp):
                sp.dma_start(fn_bc[:, :], final_norm.partition_broadcast(P)).then_inc(fn_loaded, 16)
                for t in range(TT):
                    sp.wait_ge(out_ready, t + 1)
                    dst = y_prompt[0, t * P:(t + 1) * P, :] if t < PT else y_sample.rearrange("b t d -> (b t) d")
                    sp.dma_start(dst, out_sb[t % 2][0:norm_rows(t), :]).then_inc(out_stored[t % 2], 16)
                sp.wait_ge(out_stored[0], 16 * ((TT + 1) // 2))
                sp.wait_ge(out_stored[1], 16 * (TT // 2))

            @block4.gpsimd
            def _(pool):
                for t in range(TT):
                    r = norm_rows(t)
                    if t >= 2:
                        pool.wait_ge(ffn_done, t - 1)
                    for k in range(TOPK):
                        pool.indirect_dma_start(picked[t % 2][k][0:r, :], None, y_dram,
                                                bass.IndirectOffsetOnAxis(ap=slot_i[0:r, t, k:k + 1], axis=0))\
                            .then_inc(picked_in[t % 2][k], 16)

            @block4.tensor
            def _(pe):
                for sel_, r, out_ in ((sel_p, P, g_ps), (sel_s, NS, u_ps)):
                    for q in range(Q):
                        mm = pe.matmul(out_[0:r, q * QW:(q + 1) * QW], sel_[:, q, :],
                                       mod[:, G2 * QW:(G2 + 1) * QW], start=True, stop=True)
                mm.then_inc(g2_spread, 1)

            @block4.vector
            def _(dve):
                def step(ins):
                    step.n += 1
                    ins.then_inc(fin_step, 1)
                    dve.wait_ge(fin_step, step.n)
                step.n = 0
                step(dve.memset(fin_ss[:, :], 1.0))
                def weighted(t):
                    r = norm_rows(t)
                    f = ffn[t % 2][0:r, :]
                    dve.wait_ge(first_scaled, t + 1)
                    for k in range(1, TOPK):
                        dve.wait_ge(picked_in[t % 2][k], 16 * (t // 2 + 1))
                        ins = dve.scalar_tensor_tensor(out=f, in0=picked[t % 2][k][0:r, :], scalar=gates[0:r, t, k:k + 1],
                                                       in1=f, op0=ALU.mult, op1=ALU.add)
                        if k < TOPK - 1:
                            step(ins)
                    ins.then_inc(ffn_done, 1)
                    dve.wait_ge(ffn_done, t + 1)
                    if t == 0:
                        dve.wait_ge(g2_spread, 1)
                    step(dve.tensor_tensor(f, f, (g_ps if t < PT else u_ps)[0:r, :], ALU.mult))
                    dve.tensor_tensor(x_sb[0:r, t, :], x_sb[0:r, t, :], f, ALU.add).then_inc(x2_ready, 1)

                def finish(t):
                    r = norm_rows(t)
                    dve.wait_ge(fin_sqrt, t + 1)
                    step(dve.reciprocal(fin_rstd[0:r, t:t + 1], fin_ss[0:r, t:t + 1]))
                    if t == 0:
                        dve.wait_ge(fn_loaded, 16)
                    if t >= 2:
                        dve.wait_ge(out_stored[t % 2], 16 * (t // 2))
                    dve.scalar_tensor_tensor(out=out_sb[t % 2][0:r, :], in0=x_sb[0:r, t, :],
                                             scalar=fin_rstd[0:r, t:t + 1], in1=fn_bc[0:r, :],
                                             op0=ALU.mult, op1=ALU.mult).then_inc(out_ready, 1)

                for t in range(TT):
                    weighted(t)
                    if t:
                        finish(t - 1)
                finish(TT - 1)

            @block4.scalar
            def _(act):
                def first_row(t):
                    r = norm_rows(t)
                    if t >= 2:
                        act.wait_ge(fin_sq, t - 1)
                    act.wait_ge(picked_in[t % 2][0], 16 * (t // 2 + 1))
                    act.activation(ffn[t % 2][0:r, :], picked[t % 2][0][0:r, :], ACT.Copy,
                                   scale=gates[0:r, t, 0:1]).then_inc(first_scaled, 1)

                first_row(0)
                for t in range(TT):
                    r = norm_rows(t)
                    if t + 1 < TT:
                        first_row(t + 1)
                    act.wait_ge(x2_ready, t + 1)
                    act.activation(ffn[t % 2][0:r, :], x_sb[0:r, t, :], ACT.Square,
                                   accum_out=fin_ss[0:r, t:t + 1]).then_inc(fin_sq, 1)
                    act.wait_ge(fin_sq, t + 1)
                    act.activation(fin_ss[0:r, t:t + 1], fin_ss[0:r, t:t + 1], ACT.Sqrt, bias=eps_c[0:r, 0:1],
                                   scale=1.0 / D).then_inc(fin_sqrt, 1)


_INS = ["x_prompt", "x_sample", "state_pool", "state_conv", "c_prompt", "c_sample", "norm1", "norm2",
        "w_ada", "b_ada", "w_in", "w_pool", "pool_scale", "w_conv", "w_out", "w_router", "b_router",
        "w_gate", "b_gate", "w_up", "b_up", "w_down", "b_down", "final_norm"]
_OUTS = [(1, SEQ, D), (DEC_B, DEC_T, D), (1, 1, PAST, DP), (1, 1, CPAST, DP),
         (1, DEC_B, PAST, DP), (1, DEC_B, CPAST, DP)]


def kernel(**inputs):
    import numpy as _np
    import concourse.bacc as _bacc
    from concourse import mybir as _mybir
    from concourse.bass_utils import run_bass_kernel_spmd as _run

    nc = _bacc.Bacc("TRN2", target_bir_lowering=False, num_devices=1)
    arrays, args = {}, []
    for name in _INS:
        a = _np.ascontiguousarray(inputs[name])
        arrays[f"in_{name}"] = a
        args.append(nc.dram_tensor(f"in_{name}", a.shape, _mybir.dt.from_np(a.dtype), kind="ExternalInput").ap())
    for i, shape in enumerate(_OUTS):
        args.append(nc.dram_tensor(f"out_{i}", shape, F32, kind="ExternalOutput").ap())
    hybrid_step(nc, *args)
    r = _run(nc, [arrays], core_ids=[0])
    return tuple(r.results[0][f"out_{i}"] for i in range(len(_OUTS)))
```
